# Optimizing a Trainium2 kernel written in Bass

```python
import math
import jax
import jax.numpy as jnp
from jax import lax
import numpy as np

D_MODEL = 1024
BATCH = 1
SEQ = 512
DEPTH = 2

N_META = 16
RMS_EPS = 1e-6
GN_EPS = 64e-5

RWKV_HEADS = 12
RWKV_HEAD_DIM = 64
RWKV_DIM = RWKV_HEADS * RWKV_HEAD_DIM
DECAY_LORA = 64
AAA_LORA = 64
GATE_LORA = 128
RWKV_COLS = 3 * RWKV_DIM + DECAY_LORA + AAA_LORA + GATE_LORA

S5_DIM = D_MODEL - RWKV_DIM
S5_GROUP = 16
S5_GROUPS = S5_DIM // S5_GROUP
S5_STATE = 64
EVEN_IN = RWKV_COLS + S5_DIM

FOX_HEADS = 16
FOX_HEAD_DIM = D_MODEL // FOX_HEADS
ODD_IN = 3 * D_MODEL + FOX_HEADS
Q_BLOCK = 128

D_FF = 2816
CONV_WIDTH = 3

N_EVEN = (DEPTH + 1) // 2
N_ODD = DEPTH // 2

kernel_name = 'hybrid_rwkv7_s5_fox_convffn'

def rms_norm(x, gain):
    xf = x.astype(jnp.float32)
    y = xf * lax.rsqrt(jnp.mean(xf * xf, axis=-1, keepdims=True) + RMS_EPS)
    return (y * gain.astype(jnp.float32)).astype(x.dtype)

def token_shift(p, mu):
    prev = jnp.pad(p, ((0, 0), (1, 0), (0, 0)))[:, :-1]
    return p + (prev - p) * mu

def rwkv7_step(state, inp):
    r_t, w_t, k_t, v_t, kk_t, ka_t = inp
    sa = jnp.einsum('bhvk,bhk->bhv', state, -kk_t)
    state = (state * w_t[:, :, None, :] + sa[..., None] * ka_t[:, :, None, :]
             + v_t[..., None] * k_t[:, :, None, :])
    return state, jnp.einsum('bhvk,bhk->bhv', state, r_t)

def rwkv7_mix(p, mu, w0, w2, a0, a2, g2, k_k, k_a, r_k, ln_w, ln_b):
    bsz, length, _ = p.shape
    hd = (bsz, length, RWKV_HEADS, RWKV_HEAD_DIM)
    p = token_shift(p.astype(jnp.float32), mu)
    splits = [RWKV_DIM, 2 * RWKV_DIM, 3 * RWKV_DIM, 3 * RWKV_DIM + DECAY_LORA,
              3 * RWKV_DIM + DECAY_LORA + AAA_LORA]
    r, k, v, wd, ad, gd = jnp.split(p, splits, axis=-1)
    w = -jax.nn.softplus(-(w0 + jnp.tanh(wd) @ w2)) - 0.5
    decay = jnp.exp(-jnp.exp(w))
    a = jax.nn.sigmoid(a0 + ad @ a2)
    g = jax.nn.sigmoid(gd) @ g2
    kk = (k * k_k).reshape(hd)
    kk = kk / jnp.maximum(jnp.sqrt(jnp.sum(kk * kk, axis=-1, keepdims=True)), 1e-12)
    k = k * (1.0 + (a - 1.0) * k_a)
    r, k, v, decay, a = [t.reshape(hd) for t in (r, k, v, decay, a)]
    xs = tuple(jnp.moveaxis(t, 1, 0) for t in (r, decay, k, v, kk, kk * a))
    state0 = jnp.zeros((bsz, RWKV_HEADS, RWKV_HEAD_DIM, RWKV_HEAD_DIM), jnp.float32)
    _, y = lax.scan(rwkv7_step, state0, xs)
    y = jnp.moveaxis(y, 0, 1)
    mean = jnp.mean(y, axis=-1, keepdims=True)
    var = jnp.mean((y - mean) ** 2, axis=-1, keepdims=True)
    y = ((y - mean) * lax.rsqrt(var + GN_EPS) * ln_w.reshape(RWKV_HEADS, RWKV_HEAD_DIM)
         + ln_b.reshape(RWKV_HEADS, RWKV_HEAD_DIM))
    bonus = jnp.sum(r * k * r_k, axis=-1, keepdims=True) * v
    return (y + bonus).reshape(bsz, length, RWKV_DIM) * g

def complex_linear_combine(e1, e2):
    ar1, ai1, br1, bi1 = e1
    ar2, ai2, br2, bi2 = e2
    return (ar2 * ar1 - ai2 * ai1,
            ar2 * ai1 + ai2 * ar1,
            ar2 * br1 - ai2 * bi1 + br2,
            ar2 * bi1 + ai2 * br1 + bi2)

def s5_mix(u, a_re, a_im, log_dt, b_re, b_im, c_re, c_im, d_skip, glu_w, glu_b):
    bsz, length, _ = u.shape
    f32 = jnp.float32
    uf = u.astype(f32)
    ug = uf.reshape(bsz, length, S5_GROUPS, S5_GROUP)
    a_re = a_re.astype(f32)
    a_im = a_im.astype(f32)
    dt = jnp.exp(log_dt.astype(f32))[:, None]
    mag = jnp.exp(a_re * dt)
    lam_re = mag * jnp.cos(a_im * dt)
    lam_im = mag * jnp.sin(a_im * dt)
    den = a_re * a_re + a_im * a_im
    z_re = ((lam_re - 1.0) * a_re + lam_im * a_im) / den
    z_im = (lam_im * a_re - (lam_re - 1.0) * a_im) / den
    bb_re = z_re[..., None] * b_re - z_im[..., None] * b_im
    bb_im = z_re[..., None] * b_im + z_im[..., None] * b_re
    bu_re = jnp.einsum('gnc,blgc->blgn', bb_re, ug)
    bu_im = jnp.einsum('gnc,blgc->blgn', bb_im, ug)
    shape_a = (1, length, S5_GROUPS, S5_STATE)
    elems = (jnp.broadcast_to(lam_re, shape_a), jnp.broadcast_to(lam_im, shape_a), bu_re, bu_im)
    _, _, h_re, h_im = lax.associative_scan(complex_linear_combine, elems, axis=1)
    y = (jnp.einsum('gcn,blgn->blgc', c_re, h_re)
         - jnp.einsum('gcn,blgn->blgc', c_im, h_im)).reshape(bsz, length, S5_DIM)
    y = jax.nn.gelu(y + d_skip * uf)
    return y * jax.nn.sigmoid(y @ glu_w + glu_b)

def fox_mix(p, b_f, q_gain, k_gain):
    bsz, length, _ = p.shape
    hd = (bsz, length, FOX_HEADS, FOX_HEAD_DIM)
    q, k, v, f_pre = jnp.split(p.astype(jnp.float32), [D_MODEL, 2 * D_MODEL, 3 * D_MODEL], axis=-1)
    q = rms_norm(q.reshape(hd), q_gain)
    k = rms_norm(k.reshape(hd), k_gain)
    v = v.reshape(hd)
    log_f = jax.nn.log_sigmoid(f_pre + b_f)
    cum = jnp.transpose(jnp.cumsum(log_f, axis=1), (0, 2, 1))
    q, k, v = [jnp.transpose(t, (0, 2, 1, 3)) for t in (q, k, v)]
    scale = FOX_HEAD_DIM ** -0.5
    n_blocks = (length - N_META) // Q_BLOCK
    bounds = [(0, N_META)] + [(N_META + i * Q_BLOCK, N_META + (i + 1) * Q_BLOCK)
                              for i in range(n_blocks)]
    outs = []
    for s0, s1 in bounds:
        logits = (jnp.einsum('bhqd,bhkd->bhqk', q[:, :, s0:s1], k[:, :, :s1]) * scale
                  + cum[:, :, s0:s1, None] - cum[:, :, None, :s1])
        causal = jnp.arange(s1)[None, :] <= jnp.arange(s0, s1)[:, None]
        probs = jax.nn.softmax(jnp.where(causal, logits, -jnp.inf), axis=-1)
        outs.append(jnp.einsum('bhqk,bhkd->bhqd', probs, v[:, :, :s1]))
    o = jnp.concatenate(outs, axis=2)
    return jnp.transpose(o, (0, 2, 1, 3)).reshape(bsz, length, D_MODEL)

def conv_gated_mlp(x, w_up, conv_w, conv_b, w_down):
    h = x @ w_up
    h = lax.conv_general_dilated(h, conv_w[:, None, :].astype(h.dtype), (1,),
                                 [(CONV_WIDTH - 1, 0)],
                                 dimension_numbers=('NWC', 'WIO', 'NWC'),
                                 feature_group_count=2 * D_FF) + conv_b
    gate, val = jnp.split(h, 2, axis=-1)
    return (jax.nn.silu(gate) * val) @ w_down

def setup_inputs(seed: int = 0) -> dict:
    key = jax.random.key(seed)
    ks = iter(jax.random.split(key, 40))
    f32 = jnp.float32

    def nrm(shape, scale):
        return scale * jax.random.normal(next(ks), shape, f32)

    n_lin = jnp.arange(RWKV_DIM, dtype=f32) / (RWKV_DIM - 1)
    w0_base = -6.5 + 5.0 * n_lin ** 0.85
    a_im_base = jnp.pi * jnp.arange(S5_STATE, dtype=f32)
    return {
        'x': nrm((BATCH, SEQ, D_MODEL), 1.0),
        'meta_tokens': nrm((N_META, D_MODEL), 1.0),
        'mix_norm': 1.0 + nrm((DEPTH, D_MODEL), 0.02),
        'ffn_norm': 1.0 + nrm((DEPTH, D_MODEL), 0.02),
        'even_w_in': nrm((N_EVEN, D_MODEL, EVEN_IN), D_MODEL ** -0.5),
        'even_w_out': nrm((N_EVEN, D_MODEL, D_MODEL), D_MODEL ** -0.5),
        'rwkv_mu': jax.random.uniform(next(ks), (N_EVEN, RWKV_COLS), f32),
        'rwkv_w0': w0_base[None] + nrm((N_EVEN, RWKV_DIM), 0.1),
        'rwkv_w2': nrm((N_EVEN, DECAY_LORA, RWKV_DIM), 0.1 * DECAY_LORA ** -0.5),
        'rwkv_a0': nrm((N_EVEN, RWKV_DIM), 0.1),
        'rwkv_a2': nrm((N_EVEN, AAA_LORA, RWKV_DIM), AAA_LORA ** -0.5),
        'rwkv_g2': nrm((N_EVEN, GATE_LORA, RWKV_DIM), GATE_LORA ** -0.5),
        'rwkv_k_k': 0.85 + nrm((N_EVEN, RWKV_DIM), 0.02),
        'rwkv_k_a': 1.0 + nrm((N_EVEN, RWKV_DIM), 0.02),
        'rwkv_r_k': nrm((N_EVEN, RWKV_HEADS, RWKV_HEAD_DIM), 0.1),
        'rwkv_ln_w': 1.0 + nrm((N_EVEN, RWKV_DIM), 0.02),
        'rwkv_ln_b': nrm((N_EVEN, RWKV_DIM), 0.02),
        's5_a_re': -0.5 + nrm((N_EVEN, S5_GROUPS, S5_STATE), 0.01),
        's5_a_im': a_im_base[None, None] + nrm((N_EVEN, S5_GROUPS, S5_STATE), 0.01),
        's5_log_dt': jax.random.uniform(next(ks), (N_EVEN, S5_GROUPS), f32,
                                        minval=math.log(1e-3), maxval=math.log(1e-1)),
        's5_b_re': nrm((N_EVEN, S5_GROUPS, S5_STATE, S5_GROUP), (2 * S5_GROUP) ** -0.5),
        's5_b_im': nrm((N_EVEN, S5_GROUPS, S5_STATE, S5_GROUP), (2 * S5_GROUP) ** -0.5),
        's5_c_re': nrm((N_EVEN, S5_GROUPS, S5_GROUP, S5_STATE), S5_STATE ** -0.5),
        's5_c_im': nrm((N_EVEN, S5_GROUPS, S5_GROUP, S5_STATE), S5_STATE ** -0.5),
        's5_d': nrm((N_EVEN, S5_DIM), 1.0),
        's5_glu_w': nrm((N_EVEN, S5_DIM, S5_DIM), S5_DIM ** -0.5),
        's5_glu_b': nrm((N_EVEN, S5_DIM), 0.02),
        'odd_w_in': nrm((N_ODD, D_MODEL, ODD_IN), D_MODEL ** -0.5),
        'odd_w_out': nrm((N_ODD, D_MODEL, D_MODEL), D_MODEL ** -0.5),
        'fox_b_f': jnp.linspace(1.0, 6.0, FOX_HEADS, dtype=f32)[None] + nrm((N_ODD, FOX_HEADS), 0.1),
        'fox_q_gain': 1.0 + nrm((N_ODD, FOX_HEAD_DIM), 0.02),
        'fox_k_gain': 1.0 + nrm((N_ODD, FOX_HEAD_DIM), 0.02),
        'ffn_w_up': nrm((DEPTH, D_MODEL, 2 * D_FF), D_MODEL ** -0.5),
        'ffn_conv_w': nrm((DEPTH, CONV_WIDTH, 2 * D_FF), CONV_WIDTH ** -0.5),
        'ffn_conv_b': nrm((DEPTH, 2 * D_FF), 0.02),
        'ffn_w_down': nrm((DEPTH, D_FF, D_MODEL), D_FF ** -0.5),
    }

def reference(x, meta_tokens, mix_norm, ffn_norm, even_w_in, even_w_out, rwkv_mu, rwkv_w0,
              rwkv_w2, rwkv_a0, rwkv_a2, rwkv_g2, rwkv_k_k, rwkv_k_a, rwkv_r_k, rwkv_ln_w,
              rwkv_ln_b, s5_a_re, s5_a_im, s5_log_dt, s5_b_re, s5_b_im, s5_c_re, s5_c_im, s5_d,
              s5_glu_w, s5_glu_b, odd_w_in, odd_w_out, fox_b_f, fox_q_gain, fox_k_gain,
              ffn_w_up, ffn_conv_w, ffn_conv_b, ffn_w_down):
    bsz = x.shape[0]
    meta = jnp.broadcast_to(meta_tokens[None].astype(x.dtype), (bsz, N_META, D_MODEL))
    h = jnp.concatenate([meta, x], axis=1)
    for layer in range(DEPTH):
        i = layer // 2
        hn = rms_norm(h, mix_norm[layer])
        if layer % 2 == 0:
            p = hn @ even_w_in[i]
            a_out = rwkv7_mix(p[..., :RWKV_COLS], rwkv_mu[i], rwkv_w0[i], rwkv_w2[i],
                              rwkv_a0[i], rwkv_a2[i], rwkv_g2[i], rwkv_k_k[i], rwkv_k_a[i],
                              rwkv_r_k[i], rwkv_ln_w[i], rwkv_ln_b[i])
            b_out = s5_mix(p[..., RWKV_COLS:], s5_a_re[i], s5_a_im[i], s5_log_dt[i],
                           s5_b_re[i], s5_b_im[i], s5_c_re[i], s5_c_im[i], s5_d[i],
                           s5_glu_w[i], s5_glu_b[i])
            mix = jnp.concatenate([a_out, b_out], axis=-1) @ even_w_out[i]
        else:
            p = hn @ odd_w_in[i]
            mix = fox_mix(p, fox_b_f[i], fox_q_gain[i], fox_k_gain[i]) @ odd_w_out[i]
        h = h + mix.astype(h.dtype)
        ffn = conv_gated_mlp(rms_norm(h, ffn_norm[layer]), ffn_w_up[layer], ffn_conv_w[layer],
                             ffn_conv_b[layer], ffn_w_down[layer])
        h = h + ffn.astype(h.dtype)
    return h[:, N_META:]


_drawn_inputs = setup_inputs


def setup_inputs(seed=0):
    import zlib

    import numpy as np

    out = dict(_drawn_inputs(seed))
    spreads = {}
    factors = {'ffn_norm': 2.989,
     'rwkv_w2': 8.0,
     'rwkv_a0': 2.915,
     'rwkv_k_k': 6.699,
     'rwkv_k_a': 4.829,
     'rwkv_ln_w': 5.679,
     'rwkv_ln_b': 5.338,
     's5_a_re': 64.0,
     's5_a_im': 25.928,
     's5_log_dt': 26.88,
     's5_b_re': 36.472,
     's5_b_im': 36.264,
     's5_c_re': 37.632,
     's5_c_im': 35.472,
     's5_glu_b': 34.697,
     'fox_q_gain': 8.0,
     'fox_k_gain': 23.94,
     'ffn_conv_b': 2.911}
    for name, (base, spread) in spreads.items():
        noise = np.random.default_rng([zlib.crc32(name.encode()), seed]).standard_normal(out[name].shape)
        drawn = base * np.exp(spread * noise) if base else spread * noise
        out[name] = jnp.asarray(drawn.astype(out[name].dtype))
    for name, factor in factors.items():
        out[name] = (out[name] * factor).astype(out[name].dtype)
    return out
```

```python
from contextlib import ExitStack
import math

import concourse.bass as bass
from concourse import mybir

F32 = mybir.dt.float32
F32R = mybir.dt.float32r
ALU = mybir.AluOpType
ACT = mybir.ActivationFunctionType
AXX = mybir.AxisListType.X
ds = bass.ds

P = 128
D_MODEL = 1024
KD = D_MODEL // P
SEQ = 512
N_META = 16
T = SEQ + N_META
HT = T // 2
D_FF = 2816
KF = D_FF // P
RWKV_DIM = 768
PAIRS = RWKV_DIM // P
LORA = 64
S5_TILES = 2
N_STATE_TILES = 8
C = 64
CHUNKS = -(-T // C)
TP = CHUNKS * C
G3 = 3
FOX_PAIRS = 8
QT = 88
NQ = T // QT
RMS_EPS = 1e-6
GN_EPS = 64e-5
DECAY = math.exp(-0.5)
LN_SHIFT = 2.0 ** 30
MASKED = -(2.0 ** 100)

PC_MIX, PC_FFN, PC_MU, PC_W0, PC_A0, PC_KK, PC_KA, PC_RK, PC_LNW, PC_LNB, PC_SD, PC_GLB, PC_ARE, PC_AIM = (
    0, 16, 32, 52, 58, 64, 70, 76, 82, 88, 94, 96, 98, 106)
PC_CONV = 114
CONV_COLS = 4 * 2 * KF
N_PRM = PC_CONV + 2 * CONV_COLS
N_PRM_LOADS = 24
MIXED = (6, 7, 0, 1, 2, 3, 4, 5)

GEMMS = [("in0", 22, KD, 22), ("out0", 8, KD, 8), ("up0", 2 * KF, KD, 2 * KF), ("down0", 16, KF // 2, 8),
         ("in1", 24, KD, 24), ("out1", 8, KD, 8), ("up1", 2 * KF, KD, 2 * KF), ("down1", 16, KF // 2, 8)]


def plan(stages):
    need = {"mix0": ("in0", "out0"), "ffn0": ("up0", "down0"), "fox": ("in1", "out1"), "ffn1": ("up1", "down1")}
    used = {g for s in stages if s in need for g in need[s]}
    u = q = 0
    at = {}
    for name, units, k, groups in GEMMS:
        if name in used:
            at[name] = (u, q, units, k)
            u += units
            q += groups
    return at


def decoder_trunk(nc, a, out, stages=("mix0", "ffn0", "fox", "ffn1")):
    at = plan(stages)
    ctx = ExitStack()
    with ctx:
        base = [16512]
        END = 229368
        used_to = [0]

        def put(name, shape, dt, offset):
            n = 4
            for d in shape[1:]:
                n *= d
            assert offset + n <= END, (name, offset, n)
            used_to[0] = max(used_to[0], offset + n)
            return nc.alloc_sbuf_tensor_at(name, shape, dt, offset=offset)

        def row(start):
            pos = [start]

            def place(name, *shape, dt=F32):
                n = 4
                for d in shape:
                    n *= d
                t = put(name, [P, *shape], dt, pos[0])
                pos[0] += -(-n // 32) * 32
                return t
            place.pos = pos
            return place

        keep = row(base[0])
        H = keep("H", KD, T)
        PRM = keep("PRM", N_PRM)
        IDENT = keep("IDENT", P)
        BONES = keep("BONES", P)
        BONES64 = keep("BONES64", P)
        ONES = keep("ONES", P)
        EPS = keep("EPS", 4)
        GAINS = keep("GAINS", 2)
        MAG = keep("MAG", N_STATE_TILES)
        POW = keep("POW", N_STATE_TILES, 10, 2)
        PCH = keep("PCH", PAIRS, CHUNKS)
        RAW = keep("RAW", 2, KF // 2, P)
        wpos = keep.pos[0]
        WHI = keep("WHI", 2, KF // 2, P, dt=F32R)
        WLO = keep("WLO", 2, KF // 2, P, dt=F32R)
        wend = keep.pos[0]
        hpos = keep.pos[0]
        XNH = keep("XNH", KD, T, dt=F32R)
        XNL = keep("XNL", KD, T, dt=F32R)
        zpos = keep.pos[0]
        z = row(zpos)
        XIN = z("XIN", 5, D_MODEL)
        PRAW = z("PRAW", 6, P)
        SQ = z("SQ", 2, T)
        RST = z("RST", 2, HT)
        NT = z("NT", 2, T)
        z = row(zpos)
        GH = z("GH", KF, T, dt=F32R)
        GL = z("GL", KF, T, dt=F32R)
        CP = z("CP", 2, T + 2)
        CA = z("CA", 2, T)
        SG = z("SG", T)
        GT = z("GT", T)
        z = row(zpos)
        RKV = z("RKV", 20, TP)
        KK = z("KK", PAIRS, TP)
        AA = z("AA", PAIRS, TP)
        SIG = z("SIG", PAIRS, TP)
        r6 = z.pos[0]
        CS = z("CS", PAIRS, TP)
        PP = z("PP", PAIRS, CHUNKS, C + 1)
        UIN = z("UIN", S5_TILES, T)
        tail = z.pos[0]
        PB = put("PB", [P, 2, T + 1], F32, r6)
        DT = put("DT", [P, 2, T], F32, r6 + 2 * (T + 1) * 4 + 24)
        z = row(r6 + 9216)
        WB = z("WB", 2, N_STATE_TILES, P)
        BR = z("BR", 2, N_STATE_TILES, 16)
        BB = z("BB", 2, N_STATE_TILES, 16)
        S5V = z("S5V", 16, N_STATE_TILES)
        assert z.pos[0] <= tail - 4 * S5_TILES * T
        BBM = put("BBM", [P, 2, N_STATE_TILES, P], F32, zpos + 36864)
        U = put("U", [P, 2, N_STATE_TILES, T], F32, hpos)
        W2A2 = put("W2A2", [P, RWKV_DIM], F32, wpos)
        RESET = put("RESET", [P, TP], F32, wpos + 4 * RWKV_DIM)
        G2 = put("G2", [P, RWKV_DIM], F32, wpos)
        GLW = put("GLW", [P, 2, 2 * P], F32, wpos + 4 * RWKV_DIM)
        z = row(wpos)
        KR = z("KR", PAIRS, 3, C)
        BH = z("BH", PAIRS, C)
        KH = z("KH", PAIRS, C)
        VH = z("VH", PAIRS, C)
        MQA = z("MQA", PAIRS, 2, 2, C)
        SS0 = z("SS0", PAIRS, C)
        LVL = z("LVL", 5, P)
        M1 = z("M1", P)
        M1T = z("M1T", P)
        MU2 = z("MU2", P)
        MQ = z("MQ", 2, C)
        assert z.pos[0] <= wend
        z = row(r6)
        AT = z("AT", PAIRS, 2, C)
        XX = z("XX", PAIRS, 2, C)
        XT = z("XT", PAIRS, 2, C)
        TM = z("TM", PAIRS, 2, C)
        BKT = z("BKT", PAIRS, 2, C)
        VT = z("VT", PAIRS, C)
        NG = z("NG", PAIRS, C)
        SA = z("SA", PAIRS, C)
        assert z.pos[0] <= tail - 4 * S5_TILES * T - 8 * T
        FC = put("FC", [P, 2, T], F32, tail - 4 * S5_TILES * T - 8 * T)
        z = row(tail)
        FT2 = z("FT2", T)
        FT1 = put("FT1", [P, T], F32, zpos + 18 * 4 * TP)
        MK = put("MK", [P, 4, P], F32, zpos + 20 * 4 * TP)
        BOTH = put("BOTH", [P, P], F32, wpos + 4 * RWKV_DIM + 4 * TP)
        z = row(r6)
        RS6 = z("RS6", PAIRS, T)
        WC = z("WC", 2, N_STATE_TILES, P)
        CRAW = z("CRAW", 2, 2, 2, C)
        MK2 = z("MK2", 4, P)
        assert z.pos[0] <= tail - 4 * S5_TILES * T
        PT2 = put("PT2", [P, 2, T], F32, zpos)
        z = row(zpos)
        QKV = z("QKV", 24, T)
        FRS = z("FRS", 16, T)
        PTT = z("PTT", 2, NQ, T)
        SS = z("SS", 2, T)
        PR = z("PR", 2, T)
        MX = z("MX", 2)
        SM = z("SM", 2)
        RC = z("RC", 2)
        CM = z("CM", QT)
        CUM = put("CUM", [P, 3, T], F32, zpos + 24 * T * 4 + 16 * T * 4)
        WF = put("WF", [P, KD, 16], F32, zpos + 24 * T * 4 + 16 * T * 4 + 3 * T * 4)
        BF = put("BF", [P, 1], F32, zpos + 24 * T * 4 + 16 * T * 4 + 3 * T * 4 + 512)
        FSQ = put("FSQ", [P, 2, T], F32, zpos + 24 * T * 4 + 16 * T * 4 + 3 * T * 4 + 1024)
        z = row(wpos)
        QS = z("QS", T)
        KS = z("KS", T)
        VF = z("VF", T)
        VS = z("VS", NQ, P)
        CB = z("CB", 2, T)
        RQ = z("RQ", 2, T)
        assert z.pos[0] <= wend
        OT = put("OT", [P, T], F32, zpos + 24 * T * 4)
        OUTB = put("OUTB", [P, 4, D_MODEL], F32, zpos)
        BK = ctx.enter_context(nc.psum_tensor("BK", [P, 8, 512], F32))
        cum_dram = nc.dram_tensor("cum_dram", [16, T], F32, kind="Internal").ap()

        sems = {}

        def S(name):
            if name not in sems:
                sems[name] = ctx.enter_context(nc.semaphore(name))
            return sems[name]

        def some(count):
            return not isinstance(count, int) or count > 0

        class Order:

            def __init__(self, eng, name):
                self.eng, self.name, self.at = eng, name, 0

            def done(self, ins):
                ins.then_inc(S(self.name), 1)
                self.at = self.at + 1

            def settle(self):
                if some(self.at):
                    self.eng.wait_ge(S(self.name), self.at)

        def rounds(eng, n, body, first=False, last=True):
            lo, hi = (1 if first else 0), (n - 1 if last else n)
            if first:
                body(0)
            if hi > lo:
                with eng.Fori(lo, hi) as i:
                    body(i)
            if last:
                body(n - 1)

        def bk(lo, n):
            return BK[:, lo:lo + n, 0:HT]

        def halves(ap):
            return ap.rearrange("p (a b) -> p a b", a=2)

        w_src = {
            "in0": a["even_w_in"][0], "out0": a["even_w_out"][0], "in1": a["odd_w_in"][0], "out1": a["odd_w_out"][0],
            "up0": a["ffn_w_up"][0], "up1": a["ffn_w_up"][1], "down0": a["ffn_w_down"][0], "down1": a["ffn_w_down"][1],
        }
        x_in = {g: (XNH, XNL) for g in ("in0", "out0", "in1", "out1", "up0", "up1")}
        x_in["down0"] = x_in["down1"] = (GH, GL)
        x_ready, n_x = {}, 0
        for g, _, _, _ in GEMMS:
            if g in at:
                n_x += KF if g.startswith("down") else KD
                x_ready[g] = n_x
        h_ready = {g: at[g][1] + KD for g in ("out0", "down0", "out1", "down1") if g in at}
        n_groups = max([0] + list(h_ready.values()))

        block = ctx.enter_context(nc.Block())

        @block.sync
        def _(sp):
            def rows(src, n, tile, r0):
                sp.dma_start(PRAW[r0:r0 + n, tile, :], src.rearrange("(m p) -> m p", p=P)).then_inc(S("prm_in"), 16)
                return 1
            n = 0
            for l in range(2):
                n += rows(a["mix_norm"][l], KD, 0, PC_MIX + KD * l)
                n += rows(a["ffn_norm"][l], KD, 0, PC_FFN + KD * l)
            for key, col, m in (("rwkv_mu", PC_MU, 20), ("rwkv_w0", PC_W0, 6), ("rwkv_a0", PC_A0, 6),
                                ("rwkv_k_k", PC_KK, 6), ("rwkv_k_a", PC_KA, 6), ("rwkv_ln_w", PC_LNW, 6),
                                ("rwkv_ln_b", PC_LNB, 6), ("s5_d", PC_SD, 2), ("s5_glu_b", PC_GLB, 2)):
                n += rows(a[key][0], m, 0, col)
            n += rows(a["rwkv_r_k"][0].rearrange("h d -> (h d)"), 6, 0, PC_RK)
            n += rows(a["s5_a_re"][0].rearrange("g n -> (g n)"), 8, 0, PC_ARE)
            n += rows(a["s5_a_im"][0].rearrange("g n -> (g n)"), 8, 0, PC_AIM)
            for l in range(2):
                for t in range(2):
                    n += rows(a["ffn_conv_w"][l, t], 2 * KF, 1 + 2 * l, 2 * KF * t)
                n += rows(a["ffn_conv_w"][l, 2], 2 * KF, 2 + 2 * l, 0)
                n += rows(a["ffn_conv_b"][l], 2 * KF, 2 + 2 * l, 2 * KF)
            sp.dma_start(S5V[0:8, 15, 0:2], a["s5_log_dt"][0].rearrange("(j g) -> j g", g=2)).then_inc(S("prm_in"), 16)
            assert n == N_PRM_LOADS
            for i, key in enumerate(("s5_b_re", "s5_b_im")):
                sp.dma_start(BR[:, i, :, :], a[key][0].rearrange("(j g) n c -> (g n) j c", g=2)).then_inc(S("b_in"), 16)
            for e in range(2):
                for i, key in enumerate(("fox_q_gain", "fox_k_gain")):
                    sp.dma_start(GAINS[64 * e:64 * e + 64, i:i + 1],
                                 a[key][0].rearrange("(d o) -> d o", o=1)).then_inc(S("gain_in"), 16)
            sp.dma_start(XIN[0:N_META, 0, :], a["meta_tokens"]).then_inc(S("x_in"), 16)
            for j in range(4):
                sp.dma_start(XIN[:, 1 + j, :], a["x"][0, P * j:P * j + P, :]).then_inc(S("x_in"), 16)

            def load(g, i, s):
                u0, _, _, k = at[g]
                if some(u0 + 2 * i + s - 1):
                    sp.wait_ge(S("w_lo"), u0 + 2 * i + s - 1)
                w = w_src[g]
                if g.startswith("down"):
                    src = w.rearrange("(s k p) n -> s p k n", s=2, p=P)[s, :, :, ds(i * P, P)]
                elif g.startswith("up"):
                    src = w.rearrange("(k p) n -> p k n", p=P)[:, :, ds(i * P + s * D_FF, P)]
                else:
                    src = w.rearrange("(k p) n -> p k n", p=P)[:, :, ds((2 * i + s) * P, P)]
                sp.dma_start(RAW[:, s, 0:k, :], src).then_inc(S(f"w_in{s}"), 16)

            def loads(g, lo=0):
                first = at[g][0] == 0
                n = at[g][2] // 2
                if first or lo:
                    for s in range(2):
                        load(g, lo, s)
                    lo += 1
                with sp.Fori(lo, n) as i:
                    for s in range(2):
                        load(g, i, s)

            if "mix0" in stages:
                loads("in0")
                sp.wait_ge(S("w_used"), 22)
                sp.dma_start(W2A2[0:LORA, :], a["rwkv_w2"][0]).then_inc(S("lora_in"), 16)
                sp.dma_start(W2A2[LORA:2 * LORA, :], a["rwkv_a2"][0]).then_inc(S("lora_in"), 16)
                for s in range(2):
                    load("out0", 0, s)
                for g in range(2):
                    sp.wait_ge(S(f"y_out{g}"), CHUNKS)
                    sp.wait_ge(S(f"state{g}"), CHUNKS)
                sp.dma_start(G2[:, :], a["rwkv_g2"][0]).then_inc(S("post_in"), 16)
                sp.dma_start(GLW[:, :, :], a["s5_glu_w"][0].rearrange("(k p) n -> p k n", p=P)).then_inc(S("post_in"), 16)
                for i, key in enumerate(("s5_c_re", "s5_c_im")):
                    src = a[key][0].rearrange("g c n -> (g c) n").rearrange("(t r) n -> r t n", r=P)
                    for e in range(2):
                        sp.dma_start(CRAW[:, i, :, e, :], src).then_inc(S("post_in"), 16)
                u0 = at["out0"][0]
                with sp.Fori(1, 4) as i:
                    for s in range(2):
                        load("out0", i, s)
            if "ffn0" in stages:
                loads("up0")
                loads("down0")
            if "fox" in stages:
                loads("in1")
                sp.wait_ge(S("ps_free"), at["in1"][1] + 24)
                sp.dma_start(WF[:, :, :], a["odd_w_in"][0].rearrange("(k p) n -> p k n", p=P)[:, :, 3 * D_MODEL:]).then_inc(S("wf_in"), 16)
                sp.dma_start(BF[0:16, :], a["fox_b_f"][0].rearrange("(h o) -> h o", o=1)).then_inc(S("wf_in"), 16)
                for s in range(2):
                    load("out1", 0, s)
                sp.wait_ge(S("cum"), 1)
                sp.dma_start(cum_dram, CUM[0:16, 0, :]).then_inc(S("cum_out"), 16)
                sp.wait_ge(S("cum_out"), 16)

                def bias_rows(i):
                    if some(12 * i):
                        sp.wait_ge(S("fx_ss"), 12 * i)
                    for e in range(2):
                        sp.dma_start(CB[:, e, :], cum_dram[ds(2 * i + e, 1), :].to_broadcast([P, T])).then_inc(S("cb_in"), 16)
                rounds(sp, FOX_PAIRS, bias_rows, first=True, last=False)
                with sp.Fori(1, 4) as i:
                    for s in range(2):
                        load("out1", i, s)
            if "ffn1" in stages:
                loads("up1")
                loads("down1")
            for j in range(4):
                sp.wait_ge(S("o_cp"), 2 * j + 2)
                sp.dma_start(out[0, P * j:P * j + P, :], OUTB[:, j, :]).then_inc(S("stored"), 16)
            sp.wait_ge(S("stored"), 64)

        @block.gpsimd
        def _(po):
            od = Order(po, "po_order")

            def step(ins):
                od.done(ins)
                od.settle()

            step(po.memset(IDENT[:, :], 0.0))
            po.affine_select(out=IDENT[:, :], in_=IDENT[:, :], compare_op=ALU.not_equal, fill=1.0, base=0,
                             pattern=[[-1, P]], channel_multiplier=1).then_inc(S("ident"), 1)
            po.wait_ge(S("ident"), 1)
            for t, v in ((BONES, 1.0), (BONES64, 1.0 / 64)):
                step(po.memset(t[:, :], 0.0))
                step(po.memset(t[0:64, 0:64], v))
                step(po.memset(t[64:128, 64:128], v))
            for i, v in enumerate((RMS_EPS, GN_EPS, 0.5 * math.log(LN_SHIFT))):
                step(po.memset(EPS[:, i:i + 1], v))

            def channel_masks(mk, name):
                step(po.memset(mk[:, :, :], 0.0))
                for e in range(2):
                    for jj in range(4):
                        po.memset(mk[64 * e:64 * e + 64, jj, 16 * (2 * jj + e):16 * (2 * jj + e) + 16], 1.0)\
                            .then_inc(S(name), 1)
                        po.wait_ge(S(name), 4 * e + jj + 1)
            channel_masks(MK, "mk")
            po.memset(ONES[:, :], 1.0).then_inc(S("consts"), 1)
            po.wait_ge(S("consts"), 1)
            if "mix0" in stages:
                po.wait_ge(S("w_used"), 22)
                step(po.memset(MU2[:, :], 1.0))
                step(po.affine_select(out=MU2[:, :], in_=MU2[:, :], compare_op=ALU.is_gt, fill=0.0, base=0,
                                      pattern=[[1, P]], channel_multiplier=-1))
                step(po.memset(MU2[0:64, 64:128], 0.0))
                incl = BOTH[:, :]
                step(po.memset(incl, 1.0))
                step(po.affine_select(out=incl, in_=incl, compare_op=ALU.is_ge, fill=0.0, base=0,
                                      pattern=[[1, P]], channel_multiplier=-1))
                for e in range(2):
                    h = slice(64 * e, 64 * e + 64)
                    step(po.tensor_copy(MQ[h, 0, :], MU2[h, 64 * e:64 * e + 64]))
                    step(po.tensor_copy(MQ[h, 1, :], BOTH[h, 64 * e:64 * e + 64]))
                step(po.memset(M1[:, :], 0.0))
                step(po.memset(M1T[:, :], 0.0))
                m1 = M1[:, :].rearrange("p (q r) -> p q r", r=2)
                m1t = M1T[:, :].rearrange("p (q r) -> p q r", r=2)
                step(po.affine_select(out=m1[:, :, 0], in_=m1[:, :, 0], compare_op=ALU.not_equal, fill=-1.0, base=-1,
                                      pattern=[[-2, 64]], channel_multiplier=1))
                step(po.affine_select(out=m1t[:, :, 1], in_=m1t[:, :, 1], compare_op=ALU.not_equal, fill=-1.0, base=0,
                                      pattern=[[-2, 64]], channel_multiplier=1))
                for n in range(5):
                    b = 2 << n
                    m = LVL[:, n, :].rearrange("p (q r c) -> p q r c", r=2, c=b)
                    step(po.memset(LVL[:, n, :], 0.0))
                    step(po.memset(m[:, :, 0, :], 1.0))
                    step(po.affine_select(out=m[:, :, 0, :], in_=m[:, :, 0, :], compare_op=ALU.is_ge, fill=0.0, base=-b,
                                          pattern=[[-2 * b, 64 // b], [0, b]], channel_multiplier=1))
                    po.affine_select(out=m[:, :, 0, :], in_=m[:, :, 0, :], compare_op=ALU.is_ge, fill=0.0,
                                     base=2 * b - 1, pattern=[[2 * b, 64 // b], [0, b]], channel_multiplier=-1)\
                        .then_inc(S("masks"), 1)
                    po.wait_ge(S("masks"), n + 1)
                step(po.memset(RESET[:, :], 1.0))
                po.memset(RESET[:, :].rearrange("p (c t) -> p c t", t=C)[:, :, 0:1], 0.0).then_inc(S("reset"), 1)
                po.wait_ge(S("reset"), 1)
                for n, t in enumerate((RKV[:, 0:3 * PAIRS, T:TP], KK[:, :, T:TP], AA[:, :, T:TP], SIG[:, :, T:TP])):
                    po.memset(t, 0.0).then_inc(S("pads"), 1)
                    po.wait_ge(S("pads"), n + 1)
                po.wait_ge(S("tilde"), 1)
                step(po.memset(SS0[:, :, :], 0.0))
                for e in range(2):
                    h = slice(64 * e, 64 * e + 64)
                    for p in range(PAIRS):
                        po.tensor_copy(KR[h, p, 2, :], IDENT[h, 64 * e:64 * e + 64]).then_inc(S("chunk_init"), 1)
                        po.wait_ge(S("chunk_init"), PAIRS * e + p + 1)
                po.wait_ge(S("s5_pow"), 1)
                po.wait_ge(S("s5_ucp"), 2 * N_STATE_TILES)
                od_loop = od.at

                def own_wait():
                    po.sem_inc(S("po_turn"), 1)

                def s5_tile(j):
                    od.at = od_loop + PER * j
                    cos, sin = FC[:, 0, :], FC[:, 1, :]
                    t1, t2 = FT1[:, :], FT2[:, :]
                    if some(2 * j):
                        po.wait_ge(S("s5_out"), 2 * j)
                    own_wait()
                    step(po.memset(FC[:, 0, 0:1], 1.0))
                    own_wait()
                    step(po.memset(FC[:, 1, 0:1], 0.0))
                    n = 1
                    for lev in range(10):
                        m = min(n, T - n)
                        pc = POW[:, ds(j, 1), lev, 0:1].rearrange("p a b -> p (a b)").to_broadcast([P, m])
                        ps = POW[:, ds(j, 1), lev, 1:2].rearrange("p a b -> p (a b)").to_broadcast([P, m])
                        own_wait()
                        step(po.tensor_tensor(t1[:, 0:m], cos[:, 0:m], pc, ALU.mult))
                        own_wait()
                        step(po.tensor_tensor(t2[:, 0:m], sin[:, 0:m], ps, ALU.mult))
                        step(po.tensor_tensor(cos[:, n:n + m], t1[:, 0:m], t2[:, 0:m], ALU.subtract))
                        own_wait()
                        step(po.tensor_tensor(t1[:, 0:m], sin[:, 0:m], pc, ALU.mult))
                        own_wait()
                        step(po.tensor_tensor(t2[:, 0:m], cos[:, 0:m], ps, ALU.mult))
                        step(po.tensor_tensor(sin[:, n:n + m], t1[:, 0:m], t2[:, 0:m], ALU.add))
                        n += m
                    ur = U[:, 0, ds(j, 1), :].rearrange("p a t -> p (a t)")
                    ui = U[:, 1, ds(j, 1), :].rearrange("p a t -> p (a t)")
                    own_wait()
                    step(po.tensor_tensor(t1, ur, sin, ALU.mult))
                    own_wait()
                    step(po.tensor_tensor(t2, ui, sin, ALU.mult))
                    own_wait()
                    step(po.tensor_tensor(ur, ur, cos, ALU.mult))
                    own_wait()
                    step(po.tensor_tensor(ui, ui, cos, ALU.mult))
                    own_wait()
                    po.tensor_tensor(ur, ur, t2, ALU.add).then_inc(S("s5_in"), 1)
                    po.wait_ge(S("s5_in"), 2 * j + 1)
                    own_wait()
                    po.tensor_tensor(ui, ui, t1, ALU.subtract).then_inc(S("s5_in"), 1)
                    po.wait_ge(S("s5_scan"), 2 * j + 2)
                    own_wait()
                    step(po.tensor_tensor(t1, ur, sin, ALU.mult))
                    own_wait()
                    step(po.tensor_tensor(t2, ui, sin, ALU.mult))
                    own_wait()
                    step(po.tensor_tensor(ur, ur, cos, ALU.mult))
                    own_wait()
                    step(po.tensor_tensor(ui, ui, cos, ALU.mult))
                    own_wait()
                    po.tensor_tensor(ur, ur, t2, ALU.subtract).then_inc(S("s5_out"), 1)
                    po.wait_ge(S("s5_out"), 2 * j + 1)
                    own_wait()
                    po.tensor_tensor(ui, ui, t1, ALU.add).then_inc(S("s5_out"), 1)

                PER = 2 + 10 * 6 + 4 + 4
                rounds(po, N_STATE_TILES, s5_tile, first=True, last=False)
                od.at = od_loop + PER * N_STATE_TILES
                for g in range(2):
                    po.wait_ge(S(f"y_out{g}"), CHUNKS)
                    po.wait_ge(S(f"state{g}"), CHUNKS)
                channel_masks(MK2, "mk2")
            if "fox" in stages:
                po.wait_ge(S("x_lo"), x_ready["in1"])
                step(po.memset(CM[:, :], 0.0))
                po.affine_select(out=CM[0:QT, :], in_=CM[0:QT, :], compare_op=ALU.is_ge, fill=MASKED, base=0,
                                 pattern=[[-1, QT]], channel_multiplier=1).then_inc(S("causal"), 1)
                po.wait_ge(S("w_used"), at["in1"][0] + 24)
                po.wait_ge(S("ps_free"), at["in1"][1] + 24)

                def values(i):
                    if some(i):
                        po.wait_ge(S("fx_vt"), i)
                    po.tensor_copy(VF[:, :], QKV[:, ds(16 + i, 1), :].rearrange("p a t -> p (a t)")).then_inc(S("fx_vf"), 1)
                rounds(po, FOX_PAIRS, values, first=True, last=False)

        @block.tensor
        def _(pe):
            def mm(o, l, r, start=True, stop=True, check=False):
                return pe.matmul(o, l, r, start=start, stop=stop, skip_group_check=check)

            def norm_sums(n):
                for k in range(KD):
                    pe.wait_ge(S("sq"), KD * n + k + 1)
                    for h in range(2):
                        x = mm(BK[:, 4 + h, 0:HT], ONES[:, :], SQ[:, k % 2, h * HT:h * HT + HT], k == 0, k == KD - 1)
                    x.then_inc(S("sq_used"), 1)

            def unit(g, i, s, group, slot, start, stop):
                u0, _, _, kn = at[g]
                xh, xl = x_in[g]
                k0 = s * kn if g.startswith("down") else 0
                pe.wait_ge(S("w_lo"), u0 + 2 * i + s + 1)
                if start:
                    if some(group - 1):
                        pe.wait_ge(S("ps_free"), group - 1)
                for k in range(kn):
                    for n, (w, x) in enumerate(((WHI, xh), (WHI, xl), (WLO, xh))):
                        for h in range(2):
                            last = mm(BK[:, 2 * slot + h, 0:HT], w[:, s, k, :], x[:, k0 + k, h * HT:h * HT + HT],
                                      start and k == 0 and n == 0, stop and k == kn - 1 and n == 2)
                last.then_inc(S("w_used"), 1)

            def gemm(g):
                u0, q0, units, _ = at[g]
                pe.wait_ge(S("x_lo"), x_ready[g])
                if g.startswith("down"):
                    def body(ii):
                        for r in range(2):
                            for s in range(2):
                                unit(g, 2 * ii + r, s, q0 + 2 * ii + r, r, s == 0, s == 1)
                    rounds(pe, KD // 2, body, last=False, first=q0 == 0)
                else:
                    def body(i):
                        for s in range(2):
                            unit(g, i, s, q0 + 2 * i + s, s, True, True)
                    rounds(pe, units // 2, body, last=False, first=q0 == 0)

            pe.wait_ge(S("ident"), 1)
            pe.wait_ge(S("consts"), 1)
            pe.wait_ge(S("prm_in"), 16 * (N_PRM_LOADS + 1))
            pe.wait_ge(S("ldt"), 1)
            sizes = (114, 88, 88, 88, 88)
            for t, n in enumerate(sizes):
                pe.transpose(BK[:, t // 4, P * (t % 4):P * (t % 4) + n], PRAW[0:n, t, :], IDENT[0:n, 0:n])
            pe.transpose(BK[:, 1, P:P + 8], PRAW[0:8, 5, :], IDENT[0:8, 0:8]).then_inc(S("prm_t"), 1)
            pe.wait_ge(S("x_in"), 80)
            for j in range(5):
                n = N_META if j == 0 else P
                for b in range(2):
                    i = 2 * j + b
                    if some(i - 1):
                        pe.wait_ge(S("x_cp"), i - 1)
                    for k in range(4):
                        x = pe.transpose(BK[:, 2 + i % 2, P * k:P * k + n], XIN[0:n, j, P * (4 * b + k):P * (4 * b + k) + P],
                                         IDENT[0:n, 0:n])
                    x.then_inc(S("x_t"), 1)

            nn = 0
            if "mix0" in stages:
                pe.wait_ge(S("bbm"), 1)
                for i in range(2):
                    for j in range(0, N_STATE_TILES, 4):
                        b = 6 + (2 * i + j // 4) % 2
                        if some(2 * i + j // 4 - 1):
                            pe.wait_ge(S("wb_cp"), 2 * i + j // 4 - 1)
                        for jj in range(4):
                            x = pe.transpose(BK[:, b, P * jj:P * jj + P], BBM[:, i, j + jj, :], IDENT[:, :])
                        x.then_inc(S("wb_t"), 1)
                norm_sums(nn); nn += 1
                gemm("in0")
                pe.wait_ge(S("wb_cp"), 4)
                pe.wait_ge(S("ps_free"), 22)
                for j in range(N_STATE_TILES):
                    for i in range(2):
                        n = 2 * j + i
                        if some(n - 1):
                            pe.wait_ge(S("s5_ucp"), n - 1)
                        for h in range(2):
                            x = mm(BK[:, 4 + 2 * (n % 2) + h, 0:HT], WB[:, i, j, :], UIN[:, j // 4, h * HT:h * HT + HT])
                        x.then_inc(S("s5_bum"), 1)
                pe.wait_ge(S("lora_in"), 32)
                pe.wait_ge(S("lora_act"), 1)
                for m in range(PAIRS):
                    for i in range(2):
                        n = 2 * m + i
                        if some(n - 1):
                            pe.wait_ge(S("lora_cp"), n - 1)
                        r = slice(LORA * i, LORA * i + LORA)
                        for h in range(2):
                            x = mm(BK[:, 2 * (n % 2) + h, 0:HT], W2A2[r, P * m:P * m + P], RKV[r, 18, h * HT:h * HT + HT])
                        x.then_inc(S("lora_mm"), 1)
                for m in range(PAIRS):
                    pe.wait_ge(S("kk_sq"), m + 1)
                    if some(m - 1):
                        pe.wait_ge(S("kk_max"), m - 1)
                    for h in range(2):
                        x = mm(BK[:, 4 + 2 * (m % 2) + h, 0:HT], BONES[:, :], CS[:, m, h * HT:h * HT + HT])
                    x.then_inc(S("kk_sum"), 1)
                for m in range(PAIRS):
                    pe.wait_ge(S("rk"), m + 1)
                    if some(m - 1):
                        pe.wait_ge(S("bonus"), m - 1)
                    for h in range(2):
                        x = mm(BK[:, 2 * (m % 2) + h, 0:HT], BONES[:, :], SIG[:, m, h * HT:h * HT + HT])
                    x.then_inc(S("bonus_mm"), 1)

                def own_wait():
                    pe.sem_inc(S("pe_turn"), 1)
                pe.wait_ge(S("chunk_init"), 2 * PAIRS)

                def chunk(c):
                    for p in range(PAIRS):
                        g = p // G3
                        if p % G3 == 0:
                            pe.wait_ge(S(f"stage{g}"), c + 1)
                        if p == 0:
                            pe.wait_ge(S("v_stage"), c + 1)
                        if isinstance(c, int) and c == 0:
                            if some(p - 1):
                                pe.wait_ge(S("ph_out"), p - 1)
                        else:
                            pe.wait_ge(S("ph_out"), PAIRS * c + p - 1)
                        own_wait()
                        b = p % 2
                        for e in range(2):
                            h = slice(64 * e, 64 * e + 64)
                            mm(BK[h, b, 0:192], BH[h, p, :], KR[h, p, :, :])
                            mm(BK[h, b, 192:384], KH[h, p, :], KR[h, p, :, :])
                            mm(BK[h, b, 384:448], KR[h, p, 0, :], BH[h, p, :])
                            x = mm(BK[h, b, 448:512], VH[h, p, :], KR[h, p, 2, :])
                        x.then_inc(S("ph"), 1)
                    for n in range(5):
                        for g in range(2):
                            pe.wait_ge(S(f"x_up{g}"), 6 * c + n + 1)
                            for q in range(G3):
                                p = G3 * g + q
                                x = mm(BK[:, 2 + 3 * g, P * q:P * q + P], AT[:, p, :, :], XX[:, p, :, :])
                            x.then_inc(S(f"t_mm{g}"), 1)
                        for g in range(2):
                            pe.wait_ge(S(f"t_mask{g}"), 5 * c + n + 1)
                            for q in range(G3):
                                p = G3 * g + q
                                if n < 4:
                                    mm(BK[:, 3 + 3 * g, P * q:P * q + P], XT[:, p, :, :], TM[:, p, :, :])
                                x = mm(BK[:, 4 + 3 * g, P * q:P * q + P], TM[:, p, :, :], XT[:, p, :, :])
                            x.then_inc(S(f"x_mm{g}"), 1)
                    for g in range(2):
                        pe.wait_ge(S(f"x_up{g}"), 6 * c + 6)
                        if some(c):
                            pe.wait_ge(S(f"state{g}"), c)
                        pe.wait_ge(S("ph_out"), PAIRS * c + G3 * (g + 1))
                        own_wait()
                        for q in range(G3):
                            p = G3 * g + q
                            for e in range(2):
                                h = slice(64 * e, 64 * e + 64)
                                o = BK[h, 2 + 3 * g, C * q:C * q + C]
                                mm(o, KR[h, p, 0, :], SS0[h, p, :], True, False)
                                x = mm(o, MQA[h, p, 1, 0, :], VT[h, p, :], False, True)
                        x.then_inc(S(f"g_mm{g}"), 1)
                    for g in range(2):
                        pe.wait_ge(S(f"g_cp{g}"), c + 1)
                        own_wait()
                        for q in range(G3):
                            p = G3 * g + q
                            for e in range(2):
                                h = slice(64 * e, 64 * e + 64)
                                x = mm(BK[h, 3 + 3 * g, C * q:C * q + C], XT[h, p, e, :], NG[h, p, :])
                        x.then_inc(S(f"sa_mm{g}"), 1)
                    for g in range(2):
                        pe.wait_ge(S(f"sa_cp{g}"), c + 1)
                        own_wait()
                        for q in range(G3):
                            p = G3 * g + q
                            for e in range(2):
                                h = slice(64 * e, 64 * e + 64)
                                o = BK[h, 4 + 3 * g, C * q:C * q + C]
                                mm(o, SS0[h, p, :], KR[h, p, 1, :], True, False)
                                mm(o, SA[h, p, :], MQA[h, p, 0, 1, :], False, False)
                                mm(o, VT[h, p, :], MQA[h, p, 1, 1, :], False, True)
                                o = BK[h, 2 + 3 * g, C * q:C * q + C]
                                mm(o, BKT[h, p, 0, :], SA[h, p, :], True, False)
                                x = mm(o, BKT[h, p, 1, :], VT[h, p, :], False, True)
                        x.then_inc(S(f"y_mm{g}"), 1)
                rounds(pe, CHUNKS, chunk, first=True, last=False)

                pe.wait_ge(S("post_in"), 16 * 6)
                for i in range(2):
                    for t in range(2):
                        x = pe.transpose(BK[:, 0, P * (2 * i + t):P * (2 * i + t) + P],
                                         CRAW[:, i, t, :, :], IDENT[:, :])
                x.then_inc(S("c_t"), 1)
                pe.wait_ge(S("wc"), 2)
                pe.wait_ge(S("s5_out"), 2 * N_STATE_TILES)
                for t in range(2):
                    for h in range(2):
                        n = 0
                        for jj in range(4):
                            for i in range(2):
                                x = mm(BK[:, 1 + 2 * t + h, 0:HT], WC[:, i, 4 * t + jj, :],
                                       U[:, i, 4 * t + jj, h * HT:h * HT + HT], n == 0, n == 7)
                                n += 1
                    x.then_inc(S("s5_ymm"), 1)
                pe.wait_ge(S("s5_gelu"), 2)
                for t in range(2):
                    for h in range(2):
                        for k in range(2):
                            x = mm(BK[:, 1 + 2 * t + h, 0:HT], GLW[:, k, P * t:P * t + P], UIN[:, k, h * HT:h * HT + HT],
                                   k == 0, k == 1)
                    x.then_inc(S("glu_mm"), 1)
                pe.wait_ge(S("y_out0"), CHUNKS)
                pe.wait_ge(S("y_out1"), CHUNKS)
                for m in range(PAIRS):
                    if some(m - 1):
                        pe.wait_ge(S("gn_d"), m - 1)
                    if m == 1:
                        pe.wait_ge(S("glu_sg"), 2)
                    for h in range(2):
                        x = mm(BK[:, (6 if m % 2 == 0 else 4) + h, 0:HT], BONES64[:, :], KK[:, m, h * HT:h * HT + HT])
                    x.then_inc(S("gn_mean"), 1)
                for m in range(PAIRS):
                    pe.wait_ge(S("gn_sq"), m + 1)
                    if some(m - 1):
                        pe.wait_ge(S("gn_ln"), m - 1)
                    for h in range(2):
                        x = mm(BK[:, 2 * (m % 2) + h, 0:HT], BONES64[:, :], AA[:, m, h * HT:h * HT + HT])
                    x.then_inc(S("gn_var"), 1)
                for m in range(PAIRS):
                    pe.wait_ge(S("mx"), m + 1)
                    for h in range(2):
                        x = mm(BK[:, 4 + 2 * (m % 2) + h, 0:HT], G2[:, P * m:P * m + P], RKV[:, 19, h * HT:h * HT + HT])
                    x.then_inc(S("gate_mm"), 1)
                gemm("out0")
            if "ffn0" in stages:
                norm_sums(nn); nn += 1
                gemm("up0")
                gemm("down0")
            if "fox" in stages:
                norm_sums(nn); nn += 1
                gemm("in1")
                pe.wait_ge(S("wf_in"), 32)
                for h in range(2):
                    n = 0
                    for k in range(KD):
                        for x_part in (XNH, XNL):
                            x = mm(BK[0:16, 4 + h, 0:HT], WF[:, k, :], x_part[:, k, h * HT:h * HT + HT].bitcast(F32),
                                   n == 0, n == 2 * KD - 1)
                            n += 1
                x.then_inc(S("f_mm"), 1)

                def qk_sums(i):
                    pe.wait_ge(S("fx_sq"), 2 * i + 2)
                    if some(i):
                        pe.wait_ge(S("fx_ln"), i)
                    for e in range(2):
                        for h in range(2):
                            x = mm(BK[:, 2 * e + h, 0:HT], BONES64[:, :], FSQ[:, e, h * HT:h * HT + HT])
                    x.then_inc(S("fx_sum"), 1)
                pe.wait_ge(S("ps_free"), at["in1"][1] + 24)
                rounds(pe, FOX_PAIRS, qk_sums, first=True, last=False)
                pe.wait_ge(S("causal"), 1)
                pe.wait_ge(S("f_act"), 1)

                def pair(i):
                    pe.wait_ge(S("fx_vf"), i + 1)
                    if some(12 * i):
                        pe.wait_ge(S("fx_pt"), 12 * i)
                    for j in range(NQ):
                        x = pe.transpose(BK[0:QT, 4 + j // 3, P * (j % 3):P * (j % 3) + P], VF[:, QT * j:QT * j + QT],
                                         IDENT[:, :])
                    x.then_inc(S("fx_vt"), 1)
                    pe.wait_ge(S("fx_k"), i + 1)

                    def scores(t):
                        e, j = divmod(t, NQ)
                        h = slice(64 * e, 64 * e + 64)
                        if some(12 * i + t - 1):
                            pe.wait_ge(S("fx_ss"), 12 * i + t - 1)
                        n = QT * (j + 1)
                        b = 2 * (t % 2)
                        top = j >= 3
                        mm(BK[0:QT, b, 0:min(n, HT)], QS[h, QT * j:QT * j + QT], KS[h, 0:min(n, HT)], True, top)
                        if top:
                            mm(BK[0:QT, b + 1, 0:n - HT], QS[h, QT * j:QT * j + QT], KS[h, HT:n], True, False)
                        lo = n - QT - (HT if top else 0)
                        mm(BK[0:QT, b + top, lo:lo + QT], IDENT[0:QT, 0:QT], CM[0:QT, :], False, True)\
                            .then_inc(S("fx_s"), 1)

                    def turn(t):
                        e, j = divmod(t, NQ)
                        pe.wait_ge(S("fx_p"), 12 * i + t + 1)
                        if some(12 * i + t):
                            pe.wait_ge(S("fx_pt"), 12 * i + t)
                        if t == 0:
                            pe.wait_ge(S("fx_vs"), i + 1)
                        for k in range(j + 1):
                            x = pe.transpose(BK[0:QT, 4 + k // 3, QT * (k % 3):QT * (k % 3) + QT],
                                             PR[0:QT, t % 2, QT * k:QT * k + QT], IDENT[0:QT, 0:QT])
                        x.then_inc(S("fx_t"), 1)

                    def mix(e):
                        pe.wait_ge(S("fx_pt"), 12 * i + NQ * e + NQ)
                        if some(i):
                            pe.wait_ge(S("fx_oc"), i)
                        h = slice(64 * e, 64 * e + 64)
                        for b in range(2):
                            last = 3 * b + 2
                            for k in range(last + 1):
                                lo = max(QT * k, HT * b)
                                x = mm(BK[h, 6 + b, lo - HT * b:HT], VS[0:QT, k, h], PTT[0:QT, e, k, lo:HT * (b + 1)],
                                       k == 0, k == last)
                        x.then_inc(S("fx_o"), 1)
                    scores(0)
                    for t in range(12):
                        if t < 11:
                            scores(t + 1)
                        turn(t)
                        if t == 6:
                            mix(0)
                    mix(1)

                rounds(pe, FOX_PAIRS, pair, first=True, last=False)
                gemm("out1")
            if "ffn1" in stages:
                norm_sums(nn); nn += 1
                gemm("up1")
                gemm("down1")
            if some(n_groups):
                pe.wait_ge(S("ps_free"), n_groups)
            for j in range(4):
                for b in range(2):
                    i = 2 * j + b
                    if some(i - 1):
                        pe.wait_ge(S("o_cp"), i - 1)
                    for k in range(4):
                        t0 = N_META + P * j
                        x = pe.transpose(BK[:, 4 + i % 2, P * k:P * k + P], H[:, 4 * b + k, t0:t0 + P], IDENT[:, :])
                    x.then_inc(S("o_t"), 1)

        @block.scalar
        def _(act):
            def fn(o, i, f, **kw):
                return nc.scalar.activation(o, i, f, **kw)

            def split(g, i, s):
                u0, _, _, k = at[g]
                u = u0 + 2 * i + s
                act.wait_ge(S(f"w_in{s}"), 16 * (u0 // 2 + i + 1))
                if some(u - 1):
                    act.wait_ge(S("w_used"), u - 1)
                fn(WHI[:, s, 0:k, :], RAW[:, s, 0:k, :], ACT.Copy).then_inc(S("w_hi"), 1)

            def norm(n, h_done):
                if some(h_done):
                    act.wait_ge(S("ps_free"), h_done)
                for k in range(KD):
                    if some(KD * n + k - 1):
                        act.wait_ge(S("sq_used"), KD * n + k - 1)
                    fn(SQ[:, k % 2, :], H[:, k, :], ACT.Square).then_inc(S("sq"), 1)
                act.wait_ge(S("sq_used"), KD * n + KD)
                fn(RST[:, :, :], bk(4, 2), ACT.Ln, scale=1.0 / D_MODEL, bias=EPS[:, 0:1]).then_inc(S("rms_ln"), 1)
                act.wait_ge(S("rms_ln"), n + 1)
                fn(RST[:, :, :], RST[:, :, :], ACT.Exp, scale=-0.5).then_inc(S("rms"), 1)
                for k in range(KD):
                    act.wait_ge(S("nt"), KD * n + k + 1)
                    fn(XNH[:, k, :], NT[:, k % 2, :], ACT.Copy).then_inc(S("nt_hi"), 1)

            def gemm(g, evac, peel=False):
                n = at[g][2] // 2

                def body(i):
                    last = isinstance(i, int) and i == n - 1
                    split(g, i, 1)
                    evac(i, 0)
                    if not last:
                        split(g, i + 1, 0)
                    evac(i, 1)
                rounds(act, n, body, first=peel or at[g][0] == 0)

            def nothing(i, s):
                pass

            def up(l):
                g = f"up{l}"
                u0 = at[g][0]
                uc = 2 * KF * l if "ffn0" in stages else 0
                mc = uc // 2

                def evac(i, s):
                    act.wait_ge(S("w_used"), u0 + 2 * i + s + 1)
                    if some(uc + 2 * i + s - 1):
                        act.wait_ge(S("conv"), uc + 2 * i + s - 1)
                    if s == 0:
                        if some(mc + i):
                            act.wait_ge(S("mlp_mul"), mc + i)
                    src = bk(2 * s, 2)
                    fn(halves(CP[:, s, 2:T + 2]), src, ACT.Copy).then_inc(S("cp"), 1)
                    col = PC_CONV + CONV_COLS * l + KF * s + i
                    fn(halves(CA[:, s, :]), src, ACT.Identity, scale=PRM[:, ds(col + 4 * KF, 1)],
                       bias=PRM[:, ds(col + 6 * KF, 1)]).then_inc(S("ps_free"), 1)
                    if s == 1:
                        act.wait_ge(S("conv"), uc + 2 * i + 1)
                        fn(SG[:, :], CA[:, 0, :], ACT.Silu).then_inc(S("silu"), 1)
                        act.wait_ge(S("mlp_mul"), mc + i + 1)
                        fn(GH[:, ds(i, 1), :], GT[:, :].unsqueeze(1), ACT.Copy).then_inc(S("mlp_hi"), 1)
                gemm(g, evac, peel=uc == 0)

            act.wait_ge(S("prm_t"), 1)
            act.wait_ge(S("x_t"), 1)
            for i in range(1, 10, 2):
                j, b = divmod(i, 2)
                n, t0 = (N_META, 0) if j == 0 else (P, N_META + P * (j - 1))
                act.wait_ge(S("x_t"), i + 1)
                act.wait_ge(S("x_cp"), i)
                fn(H[:, 4 * b:4 * b + 4, t0:t0 + n], BK[:, 3, :].rearrange("p (k t) -> p k t", k=4)[:, :, 0:n],
                   ACT.Copy).then_inc(S("x_cp"), 1)
            act.wait_ge(S("x_cp"), 10)
            act.wait_ge(S("consts"), 1)
            nn = 0
            if "mix0" in stages:
                v = lambda i: S5V[:, i, :]
                act.wait_ge(S("s5_ldt"), 1)
                fn(v(0), v(0), ACT.Exp).then_inc(S("s5_dt"), 1)
                act.wait_ge(S("s5_ph"), 1)
                fn(MAG[:, :], v(1), ACT.Exp).then_inc(S("s5_mag"), 1)
                fn(v(4), v(4), ACT.Sin).then_inc(S("s5_mag"), 1)
                fn(v(5), v(5), ACT.Sin).then_inc(S("s5_mag"), 1)
                split("in0", 0, 0)
                norm(nn, 0); nn += 1

                def evac(i, s):
                    u = 2 * i + s
                    act.wait_ge(S("w_used"), u + 1)
                    if some(u - 1):
                        act.wait_ge(S("shift"), u - 1)
                    fn(halves(PB[:, s, 1:T + 1]), bk(2 * s, 2), ACT.Copy).then_inc(S("ps_free"), 1)

                def body(i):
                    split("in0", i, 1)
                    evac(i, 0)
                    split("in0", i + 1, 0)
                    evac(i, 1)
                act.wait_ge(S("pb0"), 1)
                body(0)
                with act.Fori(1, 10) as i:
                    body(i)
                split("in0", 10, 1)
                for s in range(2):
                    act.wait_ge(S("w_used"), 21 + s)
                    if s == 0:
                        act.wait_ge(S("shift"), 20)
                    fn(halves(UIN[:, s, :]), bk(2 * s, 2), ACT.Copy).then_inc(S("ps_free"), 1)
                for n in range(16):
                    j, i = divmod(n, 2)
                    act.wait_ge(S("s5_bum"), n + 1)
                    fn(halves(U[:, i, j, :]), bk(4 + 2 * (n % 2), 2), ACT.Copy).then_inc(S("s5_ucp"), 1)
                    if n == 0:
                        act.wait_ge(S("shift"), 20)
                        fn(RKV[0:LORA, 18, 0:T], RKV[0:LORA, 18, 0:T], ACT.Tanh).then_inc(S("lora_act"), 1)
                        fn(RKV[:, 19, 0:T], RKV[:, 19, 0:T], ACT.Sigmoid).then_inc(S("g_act"), 1)
                act.wait_ge(S("s5_ucp"), 16)
                for n in range(2 * PAIRS):
                    m, i = divmod(n, 2)
                    act.wait_ge(S("lora_mm"), n + 1)
                    fn(halves((AA if i else SIG)[:, m, 0:T]), bk(2 * (n % 2), 2), ACT.Sigmoid,
                       bias=PRM[:, (PC_A0 if i else PC_W0) + m:(PC_A0 if i else PC_W0) + m + 1]).then_inc(S("lora_cp"), 1)
                for m in range(PAIRS):
                    act.wait_ge(S("kk_raw"), m + 1)
                    fn(CS[:, m, 0:T], KK[:, m, 0:T], ACT.Square).then_inc(S("kk_sq"), 1)
                act.wait_ge(S("kk_max"), PAIRS)
                pp = PP[:, :, :, :].rearrange("p a b c -> p (a b c)")[:, 0:PAIRS * T].rearrange("p (m t) -> p m t", t=T)
                fn(pp, pp, ACT.Ln, scale=LN_SHIFT).then_inc(S("kk_ln"), 1)
                act.wait_ge(S("kk_ln"), 1)
                fn(pp, pp, ACT.Exp, scale=-0.5, bias=EPS[:, 2:3]).then_inc(S("kk_rn"), 1)
                act.wait_ge(S("cs"), PAIRS)
                act.wait_ge(S("kkn"), 1)
                act.wait_ge(S("pads"), 4)
                csv = CS[:, :, :].rearrange("p m (c t) -> p m c t", t=C)
                for m in range(PAIRS):
                    fn(PP[:, m, :, 1:C + 1], csv[:, m], ACT.Exp, scale=-DECAY).then_inc(S("dec"), 1)
                act.wait_ge(S("dec"), PAIRS)
                fn(CS[:, :, :], CS[:, :, :], ACT.Exp, scale=DECAY).then_inc(S("pinv"), 1)

                def chunk(c):
                    if some(PAIRS * c):
                        act.wait_ge(S("ph"), PAIRS * c)
                    fn(VH[:, :, :], RKV[:, 2 * PAIRS:3 * PAIRS, ds(c * C, C)], ACT.Copy).then_inc(S("v_stage"), 1)
                    for p in range(PAIRS):
                        act.wait_ge(S("ph_dve"), PAIRS * c + p + 1)
                        ph = BK[:, p % 2, :]
                        fn(BKT[:, p, :, :], ph[:, 0:384].rearrange("p (a b t) -> p a b t", a=2, b=3)[:, :, 2, :],
                           ACT.Copy).then_inc(S("bk_cp"), 1)
                        fn(VT[:, p, :], ph[:, 448:512], ACT.Copy).then_inc(S("ph_out"), 1)
                    for g in range(2):
                        q = slice(G3 * g, G3 * g + G3)
                        act.wait_ge(S(f"g_mm{g}"), c + 1)
                        fn(NG[:, q, :], BK[:, 2 + 3 * g, 0:G3 * C].rearrange("p (q t) -> p q t", t=C), ACT.Copy,
                           scale=-1.0).then_inc(S(f"g_cp{g}"), 1)
                    for g in range(2):
                        q = slice(G3 * g, G3 * g + G3)
                        act.wait_ge(S(f"sa_mm{g}"), c + 1)
                        fn(SA[:, q, :], BK[:, 3 + 3 * g, 0:G3 * C].rearrange("p (q t) -> p q t", t=C),
                           ACT.Copy).then_inc(S(f"sa_cp{g}"), 1)
                    for g in range(2):
                        q = slice(G3 * g, G3 * g + G3)
                        act.wait_ge(S(f"y_mm{g}"), c + 1)
                        fn(KK[:, q, ds(c * C, C)], BK[:, 4 + 3 * g, 0:G3 * C].rearrange("p (q t) -> p q t", t=C),
                           ACT.Copy).then_inc(S(f"y_out{g}"), 1)
                act.wait_ge(S("tilde"), 1)
                rounds(act, CHUNKS, chunk, first=True, last=False)

                for t in range(2):
                    act.wait_ge(S("s5_y"), t + 1)
                    fn(UIN[:, t, :], UIN[:, t, :], ACT.Gelu_apprx_tanh).then_inc(S("s5_gelu"), 1)
                for t in range(2):
                    act.wait_ge(S("glu_mm"), t + 1)
                    fn(halves(PT2[:, t, :]), bk(1 + 2 * t, 2), ACT.Sigmoid, bias=PRM[:, PC_GLB + t:PC_GLB + t + 1])\
                        .then_inc(S("glu_sg"), 1)
                def mixed(k):
                    act.wait_ge(S("mx"), k + 1)
                    fn(XNH[:, MIXED[k], :], PT2[:, k % 2, :], ACT.Copy).then_inc(S("mx_hi"), 1)
                for k in range(2):
                    mixed(k)
                for m in range(PAIRS):
                    act.wait_ge(S("gn_d"), m + 1)
                    fn(AA[:, m, 0:T], KK[:, m, 0:T], ACT.Square).then_inc(S("gn_sq"), 1)
                for m in range(PAIRS):
                    act.wait_ge(S("gn_var"), m + 1)
                    fn(halves(RS6[:, m, :]), bk(2 * (m % 2), 2), ACT.Ln, bias=EPS[:, 1:2]).then_inc(S("gn_ln"), 1)
                act.wait_ge(S("gn_ln"), PAIRS)
                fn(RS6[:, :, :], RS6[:, :, :], ACT.Exp, scale=-0.5).then_inc(S("gn_rs"), 1)
                for k in range(2, KD):
                    mixed(k)
                split("out0", 0, 0)
                gemm("out0", nothing)
            if "ffn0" in stages:
                split("up0", 0, 0)
                norm(nn, h_ready.get("out0", 0)); nn += 1
                up(0)
                split("down0", 0, 0)
                gemm("down0", nothing)
            if "fox" in stages:
                split("in1", 0, 0)
                norm(nn, h_ready.get("down0", 0)); nn += 1
                u0 = at["in1"][0]

                def evac(i, s):
                    act.wait_ge(S("w_used"), u0 + 2 * i + s + 1)
                    fn(QKV[:, ds(2 * i + s, 1), :].rearrange("p o (a b) -> p (o a) b", a=2), bk(2 * s, 2), ACT.Copy)\
                        .then_inc(S("ps_free"), 1)
                gemm("in1", evac)
                act.wait_ge(S("ps_free"), at["in1"][1] + 24)
                act.wait_ge(S("f_abs"), 1)
                fn(CUM[0:16, 1, :], CUM[0:16, 1, :], ACT.Exp, scale=-1.0).then_inc(S("f_exp"), 1)
                act.wait_ge(S("f_exp"), 1)
                fn(CUM[0:16, 1, :], CUM[0:16, 1, :], ACT.Ln, bias=ONES[0:16, 0:1]).then_inc(S("f_act"), 1)

                def qk_norm(i):
                    if some(i):
                        act.wait_ge(S("fx_sum"), i)
                    for e in range(2):
                        fn(FSQ[:, e:e + 1, :], QKV[:, ds(8 * e + i, 1), :], ACT.Square).then_inc(S("fx_sq"), 1)
                    act.wait_ge(S("fx_sum"), i + 1)
                    for e in range(2):
                        x = fn(FRS[:, ds(8 * e + i, 1), :].rearrange("p o (a b) -> p (o a) b", a=2), bk(2 * e, 2), ACT.Ln,
                               bias=EPS[:, 0:1])
                    x.then_inc(S("fx_ln"), 1)
                rounds(act, FOX_PAIRS, qk_norm, first=True, last=False)
                act.wait_ge(S("fx_ln"), FOX_PAIRS)

                def pair(i):
                    if some(i):
                        act.wait_ge(S("fx_k"), i)
                    for e in range(2):
                        fn(RQ[:, e:e + 1, :], FRS[:, ds(8 * e + i, 1), :], ACT.Exp, scale=-0.5).then_inc(S("fx_rs"), 1)
                    act.wait_ge(S("fx_vt"), i + 1)
                    for b in range(2):
                        x = fn(VS[0:QT, 3 * b:3 * b + 3, :], BK[0:QT, 4 + b, 0:3 * P].rearrange("p (k t) -> p k t", t=P), ACT.Copy)
                    x.then_inc(S("fx_vs"), 1)

                    def exps(t):
                        j = t % NQ
                        n = QT * (j + 1)
                        act.wait_ge(S("fx_mx"), 12 * i + t + 1)
                        if some(12 * i + t - 1):
                            act.wait_ge(S("fx_t"), 12 * i + t - 1)
                        fn(PR[0:QT, t % 2, 0:n], SS[0:QT, t % 2, 0:n], ACT.Exp, bias=MX[0:QT, t % 2:t % 2 + 1],
                           accum_out=SM[0:QT, t % 2:t % 2 + 1]).then_inc(S("fx_e"), 1)

                    def out_pt(t):
                        e, j = divmod(t, NQ)
                        act.wait_ge(S("fx_t"), 12 * i + t + 1)
                        q = slice(QT * j, QT * j + QT)
                        for b in range(2 if j >= 3 else 1):
                            n = min(3, j + 1 - 3 * b)
                            x = fn(PTT[0:QT, e, 3 * b:3 * b + n, q],
                                   BK[0:QT, 4 + b, 0:QT * n].rearrange("p (k t) -> p k t", t=QT), ACT.Copy)
                        x.then_inc(S("fx_pt"), 1)
                    exps(0)
                    for t in range(12):
                        if t < 11:
                            exps(t + 1)
                        out_pt(t)
                    act.wait_ge(S("fx_o"), 2 * i + 2)
                    act.wait_ge(S("x_lo"), x_ready["out1"] - KD + i)
                    fn(halves(OT[:, :]), bk(6, 2), ACT.Copy).then_inc(S("fx_oc"), 1)
                    act.wait_ge(S("fx_oc"), i + 1)
                    fn(XNH[:, ds(i, 1), :], OT[:, :].unsqueeze(1), ACT.Copy).then_inc(S("ot_hi"), 1)
                rounds(act, FOX_PAIRS, pair, first=True, last=False)
                split("out1", 0, 0)
                gemm("out1", nothing)
            if "ffn1" in stages:
                split("up1", 0, 0)
                norm(nn, h_ready.get("out1", 0)); nn += 1
                up(1)
                split("down1", 0, 0)
                gemm("down1", nothing)
            for i in range(1, 8, 2):
                act.wait_ge(S("o_t"), i + 1)
                act.wait_ge(S("o_cp"), i)
                fn(OUTB[:, i // 2, 512:1024], BK[:, 5, :], ACT.Copy).then_inc(S("o_cp"), 1)

        @block.vector
        def _(ve):
            od = Order(ve, "ve_order")

            def step(ins):
                od.done(ins)
                od.settle()

            def tt(o, x, y, op):
                return nc.vector.tensor_tensor(o, x, y, op)

            def ts(o, x, s1, s2, op0, op1=None):
                return nc.vector.tensor_scalar(o, x, s1, s2, op0, op1) if op1 is not None else \
                    nc.vector.tensor_scalar(o, x, s1, s2, op0)

            def stt(o, x, s, y, op0, op1):
                return nc.vector.scalar_tensor_tensor(out=o, in0=x, scalar=s, in1=y, op0=op0, op1=op1)

            def f32(ap):
                return ap.bitcast(F32)

            def split(g, i, s):
                u0, _, _, k = at[g]
                ve.wait_ge(S("w_hi"), u0 + 2 * i + s + 1)
                tt(WLO[:, s, 0:k, :], RAW[:, s, 0:k, :], f32(WHI[:, s, 0:k, :]), ALU.subtract).then_inc(S("w_lo"), 1)

            def norm(n, g, col):
                x0 = x_ready[g] - KD
                ve.wait_ge(S("rms"), n + 1)

                def scaled(k):
                    if some(KD * n + k - 1):
                        ve.wait_ge(S("nt_hi"), KD * n + k - 1)
                    if some(x0 + k - 1):
                        ve.wait_ge(S("x_lo"), x0 + k - 1)
                    stt(NT[:, k % 2, :], H[:, k, :], PRM[:, col + k:col + k + 1], RST[:, :, :].rearrange("p a b -> p (a b)"),
                        ALU.mult, ALU.mult).then_inc(S("nt"), 1)
                scaled(0)
                for k in range(KD):
                    if k + 1 < KD:
                        scaled(k + 1)
                    ve.wait_ge(S("nt_hi"), KD * n + k + 1)
                    tt(XNL[:, k, :], NT[:, k % 2, :], f32(XNH[:, k, :]), ALU.subtract).then_inc(S("x_lo"), 1)

            def gemm(g, use, peel=False):
                n = at[g][2] // 2

                def body(i):
                    last = isinstance(i, int) and i == n - 1
                    split(g, i, 1)
                    use(i, 0)
                    if not last:
                        split(g, i + 1, 0)
                    use(i, 1)
                rounds(ve, n, body, first=peel or at[g][0] == 0)

            def residual(g):
                u0, _, units, _ = at[g]
                h0 = h_ready[g] - KD
                if g.startswith("down"):
                    def body(ii, last=False):
                        for r in range(2):
                            i = 2 * ii + r
                            split(g, i, 1)
                            if not (last and r == 1):
                                split(g, i + 1, 0)
                            ve.wait_ge(S("w_used"), u0 + 2 * i + 2)
                            hm = H[:, ds(i, 1), :].rearrange("p o (a b) -> p (o a) b", a=2)
                            tt(hm, hm, bk(2 * r, 2), ALU.add).then_inc(S("ps_free"), 1)
                    with ve.Fori(0, 3) as ii:
                        body(ii)
                    body(3, True)
                else:
                    def use(i, s):
                        ve.wait_ge(S("w_used"), u0 + 2 * i + s + 1)
                        hm = H[:, ds(2 * i + s, 1), :].rearrange("p o (a b) -> p (o a) b", a=2)
                        tt(hm, hm, bk(2 * s, 2), ALU.add).then_inc(S("ps_free"), 1)
                    gemm(g, use)

            def up(l):
                g = f"up{l}"
                u0 = at[g][0]
                uc = 2 * KF * l if "ffn0" in stages else 0
                mc = uc // 2
                x0 = x_ready[f"down{l}"] - KF
                ve.wait_ge(S("x_lo"), x_ready[g])
                ve.memset(CP[:, :, 0:2], 0.0).then_inc(S("cp0"), 1)
                ve.wait_ge(S("cp0"), l + 1 if "ffn0" in stages else 1)

                def use(i, s):
                    n = uc + 2 * i + s
                    q = at[g][1] + 2 * i + s
                    ve.wait_ge(S("ps_free"), q + 1)
                    col = PC_CONV + CONV_COLS * l + KF * s + i
                    stt(CA[:, s, :], CP[:, s, 1:T + 1], PRM[:, ds(col + 2 * KF, 1)], CA[:, s, :], ALU.mult, ALU.add)\
                        .then_inc(S("conv_a"), 1)
                    ve.wait_ge(S("conv_a"), n + 1)
                    stt(CA[:, s, :], CP[:, s, 0:T], PRM[:, ds(col, 1)], CA[:, s, :], ALU.mult, ALU.add)\
                        .then_inc(S("conv"), 1)
                    if s == 1:
                        ve.wait_ge(S("silu"), mc + i + 1)
                        ve.wait_ge(S("conv"), n + 1)
                        ve.wait_ge(S("x_lo"), x0 + i)
                        tt(GT[:, :], SG[:, :], CA[:, 1, :], ALU.mult).then_inc(S("mlp_mul"), 1)
                        ve.wait_ge(S("mlp_hi"), mc + i + 1)
                        gm = GH[:, ds(i, 1), :]
                        tt(GL[:, ds(i, 1), :], GT[:, :].unsqueeze(1), f32(gm), ALU.subtract).then_inc(S("x_lo"), 1)
                gemm(g, use)

            ve.wait_ge(S("prm_in"), 16 * (N_PRM_LOADS + 1))
            ve.tensor_copy(PRAW[0:8, 5, :].rearrange("p (g n) -> p g n", g=2),
                           S5V[0:8, 15, 0:2].unsqueeze(2).to_broadcast([8, 2, 64])).then_inc(S("ldt"), 1)
            ve.wait_ge(S("prm_t"), 1)
            col = 0
            for t, n in enumerate((114, 88, 88, 88, 88)):
                od.done(ve.tensor_copy(PRM[:, col:col + n], BK[:, t // 4, P * (t % 4):P * (t % 4) + n]))
                col += n
            ve.tensor_copy(S5V[:, 0, :], BK[:, 1, P:P + 8]).then_inc(S("s5_ldt"), 1)
            for i in range(0, 10, 2):
                j, b = divmod(i, 2)
                n, t0 = (N_META, 0) if j == 0 else (P, N_META + P * (j - 1))
                ve.wait_ge(S("x_t"), i + 1)
                if some(i):
                    ve.wait_ge(S("x_cp"), i)
                ve.tensor_copy(H[:, 4 * b:4 * b + 4, t0:t0 + n], BK[:, 2, :].rearrange("p (k t) -> p k t", k=4)[:, :, 0:n])\
                    .then_inc(S("x_cp"), 1)
            od.settle()
            ve.wait_ge(S("s5_ldt"), 1)
            ve.wait_ge(S("x_cp"), 10)
            ve.wait_ge(S("consts"), 1)
            nn = 0
            if "mix0" in stages:
                v = lambda i: S5V[:, i, :]
                are, aim = PRM[:, PC_ARE:PC_ARE + 8], PRM[:, PC_AIM:PC_AIM + 8]
                ve.wait_ge(S("s5_dt"), 1)
                step(tt(v(1), are, v(0), ALU.mult))
                step(tt(v(2), aim, v(0), ALU.mult))
                big = 1.5 * 2.0 ** 23
                turn = 2 * math.pi
                c1 = 6.28125
                c2 = float.fromhex("0x1.fb4p-10")
                c3 = turn - c1 - c2
                for dst, quarter in ((4, 0.0), (5, 0.25)):
                    step(ts(v(3), v(2), 1.0 / turn, quarter, ALU.mult, ALU.add))
                    step(ts(v(3), v(3), big, None, ALU.add))
                    step(ts(v(3), v(3), big, None, ALU.subtract))
                    step(stt(v(dst), v(3), -c1, v(2), ALU.mult, ALU.add))
                    step(stt(v(dst), v(3), -c2, v(dst), ALU.mult, ALU.add))
                    step(stt(v(dst), v(3), -c3, v(dst), ALU.mult, ALU.add))
                    step(ts(v(dst), v(dst), quarter * turn, None, ALU.add))
                    x = ts(v(dst), v(dst), 3.1415925, -3.1415925, ALU.min, ALU.max)
                    if quarter:
                        x.then_inc(S("s5_ph"), 1)
                    else:
                        step(x)
                ve.wait_ge(S("s5_mag"), 3)
                cs, sn = v(5), v(4)
                step(tt(v(6), MAG[:, :], cs, ALU.mult))
                step(tt(v(7), MAG[:, :], sn, ALU.mult))
                step(ts(v(6), v(6), 1.0, None, ALU.subtract))
                step(tt(v(8), are, are, ALU.mult))
                step(tt(v(9), aim, aim, ALU.mult))
                step(tt(v(8), v(8), v(9), ALU.add))
                step(nc.vector.reciprocal(v(8), v(8)))
                step(tt(v(9), v(6), are, ALU.mult))
                step(tt(v(10), v(7), aim, ALU.mult))
                step(tt(v(9), v(9), v(10), ALU.add))
                step(tt(v(9), v(9), v(8), ALU.mult))
                step(tt(v(10), v(7), are, ALU.mult))
                step(tt(v(11), v(6), aim, ALU.mult))
                step(tt(v(10), v(10), v(11), ALU.subtract))
                step(tt(v(10), v(10), v(8), ALU.mult))
                step(ve.tensor_copy(POW[:, :, 0, 0], cs))
                step(ve.tensor_copy(POW[:, :, 0, 1], sn))
                for n in range(9):
                    step(tt(v(12), POW[:, :, n, 0], POW[:, :, n, 0], ALU.mult))
                    step(tt(v(13), POW[:, :, n, 1], POW[:, :, n, 1], ALU.mult))
                    step(tt(POW[:, :, n + 1, 0], v(12), v(13), ALU.subtract))
                    x = stt(POW[:, :, n + 1, 1], POW[:, :, n, 0], 2.0, POW[:, :, n, 1], ALU.mult, ALU.mult)
                    if n < 8:
                        step(x)
                x.then_inc(S("s5_pow"), 1)
                ve.wait_ge(S("b_in"), 32)
                zr = v(9).unsqueeze(2).to_broadcast([P, 8, 16])
                zi = v(10).unsqueeze(2).to_broadcast([P, 8, 16])
                t1 = BBM[:, 0, 0, :].rearrange("p (j c) -> p j c", c=16)
                step(tt(BB[:, 0], BR[:, 0], zr, ALU.mult))
                step(tt(t1, BR[:, 1], zi, ALU.mult))
                step(tt(BB[:, 0], BB[:, 0], t1, ALU.subtract))
                step(tt(BB[:, 1], BR[:, 1], zr, ALU.mult))
                step(tt(t1, BR[:, 0], zi, ALU.mult))
                step(tt(BB[:, 1], BB[:, 1], t1, ALU.add))
                ve.wait_ge(S("mk"), 8)
                for i in range(2):
                    for j in range(8):
                        x = tt(BBM[:, i, j, :].rearrange("p (s c) -> p s c", c=16),
                               BB[:, i, j, :].unsqueeze(1).to_broadcast([P, 8, 16]),
                               MK[:, j % 4, :].rearrange("p (s c) -> p s c", c=16), ALU.mult)
                x.then_inc(S("bbm"), 1)
                for n in range(4):
                    i, jh = divmod(n, 2)
                    ve.wait_ge(S("wb_t"), n + 1)
                    ve.tensor_copy(WB[:, i, 4 * jh:4 * jh + 4, :], BK[:, 6 + n % 2, :].rearrange("p (j c) -> p j c", j=4))\
                        .then_inc(S("wb_cp"), 1)
                ve.memset(PB[:, :, 0:1], 0.0).then_inc(S("pb0"), 1)
                split("in0", 0, 0)
                norm(nn, "in0", PC_MIX); nn += 1
                ve.wait_ge(S("pb0"), 1)

                def use(i, s):
                    u = 2 * i + s
                    ve.wait_ge(S("ps_free"), u + 1)
                    tt(DT[:, s, :], PB[:, s, 0:T], PB[:, s, 1:T + 1], ALU.subtract).then_inc(S("diff"), 1)
                    ve.wait_ge(S("diff"), u + 1)
                    stt(RKV[:, ds(u, 1), 0:T], DT[:, s, :].unsqueeze(1), PRM[:, ds(PC_MU + u, 1)],
                        PB[:, s, 1:T + 1].unsqueeze(1), ALU.mult, ALU.add).then_inc(S("shift"), 1)

                def body(i):
                    split("in0", i, 1)
                    use(i, 0)
                    split("in0", i + 1, 0)
                    use(i, 1)
                body(0)
                with ve.Fori(1, 10) as i:
                    body(i)
                split("in0", 10, 1)
                ve.wait_ge(S("shift"), 20)
                for m in range(PAIRS):
                    ts(KK[:, m, 0:T], RKV[:, PAIRS + m, 0:T], PRM[:, PC_KK + m:PC_KK + m + 1], None, ALU.mult)\
                        .then_inc(S("kk_raw"), 1)
                pp = PP[:, :, :, :].rearrange("p a b c -> p (a b c)")[:, 0:PAIRS * T].rearrange("p (m t) -> p m t", t=T)
                for m in range(PAIRS):
                    ve.wait_ge(S("kk_sum"), m + 1)
                    if m == 0:
                        ve.wait_ge(S("pads"), 4)
                    ts(pp[:, m, :].rearrange("p (a b) -> p a b", a=2), bk(4 + 2 * (m % 2), 2), 1e-24, None, ALU.max)\
                        .then_inc(S("kk_max"), 1)
                ve.wait_ge(S("kk_rn"), 1)
                ve.wait_ge(S("kk_raw"), PAIRS)
                tt(KK[:, :, 0:T], KK[:, :, 0:T], pp, ALU.mult).then_inc(S("kkn0"), 1)
                ve.wait_ge(S("kkn0"), 1)
                ve.memset(PP[:, :, :, 0:1], 1.0).then_inc(S("kkn"), 1)
                ve.wait_ge(S("reset"), 1)
                ve.wait_ge(S("lora_cp"), 2 * PAIRS)
                for m in range(PAIRS):
                    nc.vector.tensor_tensor_scan(CS[:, m, :], RESET[:, :], SIG[:, m, :], 0.0, ALU.mult, ALU.add)\
                        .then_inc(S("cs"), 1)
                ve.wait_ge(S("cs"), PAIRS)
                om = FT1[:, 0:PAIRS]
                ve.wait_ge(S("masks"), 5)
                step(ts(om, PRM[:, PC_KA:PC_KA + PAIRS], -1.0, 1.0, ALU.mult, ALU.add))
                for m in range(PAIRS):
                    od.done(ts(SIG[:, m, 0:T], AA[:, m, 0:T], PRM[:, PC_KA + m:PC_KA + m + 1], FT1[:, m:m + 1],
                               ALU.mult, ALU.add))
                od.settle()
                step(tt(RKV[:, PAIRS:2 * PAIRS, 0:T], RKV[:, PAIRS:2 * PAIRS, 0:T], SIG[:, :, 0:T], ALU.mult))
                step(tt(AA[:, :, 0:T], AA[:, :, 0:T], KK[:, :, 0:T], ALU.mult))
                for m in range(PAIRS):
                    stt(SIG[:, m, 0:T], RKV[:, m, 0:T], PRM[:, PC_RK + m:PC_RK + m + 1], RKV[:, PAIRS + m, 0:T],
                        ALU.mult, ALU.mult).then_inc(S("rk"), 1)
                for m in range(PAIRS):
                    ve.wait_ge(S("bonus_mm"), m + 1)
                    tt(halves(SIG[:, m, 0:T]), bk(2 * (m % 2), 2), halves(RKV[:, 2 * PAIRS + m, 0:T]), ALU.mult)\
                        .then_inc(S("bonus"), 1)
                ve.wait_ge(S("pinv"), 1)
                ve.wait_ge(S("kkn"), 1)
                ch = lambda ap: ap.rearrange("p m (c t) -> p m c t", t=C)
                for m in range(PAIRS):
                    r, k = RKV[:, m, :], RKV[:, PAIRS + m, :]
                    c4 = lambda ap: ap.rearrange("p (c t) -> p c t", t=C)
                    od.done(tt(c4(KK[:, m, :]), c4(KK[:, m, :]), PP[:, m, :, 0:C], ALU.mult))
                    od.done(tt(c4(r), c4(r), PP[:, m, :, 1:C + 1], ALU.mult))
                    od.done(tt(AA[:, m, :], AA[:, m, :], CS[:, m, :], ALU.mult))
                    od.done(tt(k, k, CS[:, m, :], ALU.mult))
                od.settle()
                ve.tensor_copy(PCH[:, :, :], PP[:, :, :, C]).then_inc(S("tilde"), 1)

                ve.wait_ge(S("tilde"), 1)
                o0 = od.at
                PER = 3 * PAIRS + 2 + 2

                def chunk(c, s5):
                    od.at = o0 + PER * c
                    for g in range(2):
                        if some(c):
                            ve.wait_ge(S(f"y_mm{g}"), c)
                        q = slice(G3 * g, G3 * g + G3)
                        t = ds(c * C, C)
                        ve.tensor_copy(KR[:, q, 0, :], KK[:, q, t])
                        ve.tensor_copy(KR[:, q, 1, :], RKV[:, q, t])
                        ve.tensor_copy(BH[:, q, :], AA[:, q, t])
                        ve.tensor_copy(KH[:, q, :], RKV[:, PAIRS + G3 * g:PAIRS + G3 * g + G3, t])\
                            .then_inc(S(f"stage{g}"), 1)
                    if isinstance(c, int) and c == 0:
                        ve.wait_ge(S("chunk_init"), 2 * PAIRS)
                    for p in range(PAIRS):
                        ve.wait_ge(S("ph"), PAIRS * c + p + 1)
                        ph = BK[:, p % 2, :]
                        two = lambda ap: ap.unsqueeze(1).to_broadcast([P, 2, C])
                        m2 = lambda t: t[:, :].rearrange("p (e t) -> p e t", e=2)
                        od.done(tt(AT[:, p], two(ph[:, 0:64]), m2(MU2), ALU.mult))
                        od.done(tt(XT[:, p], two(ph[:, 0:64]), m2(M1T), ALU.mult))
                        od.done(tt(XX[:, p], two(ph[:, 384:448]), m2(M1), ALU.mult))
                        tt(MQA[:, p], ph[:, 0:384].rearrange("p (a b t) -> p a b t", a=2, b=3)[:, :, 0:2, :],
                           MQ[:, :, :].unsqueeze(1).to_broadcast([P, 2, 2, C]), ALU.mult).then_inc(S("ph_dve"), 1)
                        if p % G3 == G3 - 1:
                            g = p // G3
                            q = slice(G3 * g, G3 * g + G3)
                            od.settle()
                            fl = lambda t: t[:, q].rearrange("p q e t -> p q (e t)")
                            idb = IDENT[:, :].unsqueeze(1).to_broadcast([P, G3, P])
                            od.done(tt(fl(XT), fl(XT), idb, ALU.add))
                            tt(fl(XX), fl(XX), idb, ALU.add).then_inc(S(f"x_up{g}"), 1)
                    for n in range(5):
                        for g in range(2):
                            q = slice(G3 * g, G3 * g + G3)
                            fl = lambda t: t[:, q].rearrange("p q e t -> p q (e t)")
                            pq = lambda b: BK[:, b + 3 * g, 0:G3 * P].rearrange("p (q t) -> p q t", t=P)
                            ve.wait_ge(S(f"t_mm{g}"), 5 * c + n + 1)
                            tt(fl(TM), pq(2), LVL[:, n, :].unsqueeze(1).to_broadcast([P, G3, P]), ALU.mult)\
                                .then_inc(S(f"t_mask{g}"), 1)
                        for g in range(2):
                            q = slice(G3 * g, G3 * g + G3)
                            fl = lambda t: t[:, q].rearrange("p q e t -> p q (e t)")
                            pq = lambda b: BK[:, b + 3 * g, 0:G3 * P].rearrange("p (q t) -> p q t", t=P)
                            ve.wait_ge(S(f"x_mm{g}"), 5 * c + n + 1)
                            if n < 4:
                                tt(fl(XX), fl(XX), pq(3), ALU.subtract)
                            tt(fl(XT), fl(XT), pq(4), ALU.subtract).then_inc(S(f"x_up{g}"), 1)
                    if s5:
                        ve.wait_ge(S("s5_in"), 2 * c + 2)
                        for i in range(2):
                            u = U[:, i, ds(c, 1), :].rearrange("p a t -> p (a t)")
                            nc.vector.tensor_tensor_scan(u, MAG[:, ds(c, 1)].to_broadcast([P, T]), u, 0.0,
                                                         ALU.mult, ALU.add).then_inc(S("s5_scan"), 1)
                    for g in range(2):
                        q = slice(G3 * g, G3 * g + G3)
                        ve.wait_ge(S(f"y_mm{g}"), c + 1)
                        od.done(tt(SS0[:, q, :], SS0[:, q, :],
                                   BK[:, 2 + 3 * g, 0:G3 * C].rearrange("p (q t) -> p q t", t=C), ALU.add))
                        od.settle()
                        tt(SS0[:, q, :], SS0[:, q, :], PCH[:, q, ds(c, 1)].to_broadcast([P, G3, C]), ALU.mult)\
                            .then_inc(S(f"state{g}"), 1)
                chunk(0, True)
                assert od.at == o0 + PER, (od.at, o0, PER)
                with ve.Fori(1, N_STATE_TILES) as c:
                    chunk(c, True)
                chunk(CHUNKS - 1, False)
                od.at = o0 + PER * CHUNKS
                for g in range(2):
                    ve.wait_ge(S(f"y_out{g}"), CHUNKS)
                    ve.wait_ge(S(f"state{g}"), CHUNKS)

                ve.wait_ge(S("c_t"), 1)
                ve.wait_ge(S("mk2"), 8)
                for i in range(2):
                    for t in range(2):
                        x = stt(WC[:, i, 4 * t:4 * t + 4, :],
                                BK[:, 0, P * (2 * i + t):P * (2 * i + t) + P].unsqueeze(1).to_broadcast([P, 4, P]),
                                -1.0 if i else 1.0, MK2[:, :, :], ALU.mult, ALU.mult)
                    x.then_inc(S("wc"), 1)
                for t in range(2):
                    ve.wait_ge(S("s5_ymm"), t + 1)
                    stt(halves(UIN[:, t, :]), halves(UIN[:, t, :]), PRM[:, PC_SD + t:PC_SD + t + 1], bk(1 + 2 * t, 2),
                        ALU.mult, ALU.add).then_inc(S("s5_y"), 1)

                def mixed(k, fill):
                    m = MIXED[k]
                    if some(k - 1):
                        ve.wait_ge(S("mx_hi"), k - 1)
                    fill()
                    ve.wait_ge(S("mx_hi"), k + 1)
                    tt(XNL[:, m, :], PT2[:, k % 2, :], f32(XNH[:, m, :]), ALU.subtract).then_inc(S("x_lo"), 1)
                for t in range(2):
                    ve.wait_ge(S("glu_sg"), t + 1)
                    mixed(t, lambda: tt(PT2[:, t, :], PT2[:, t, :], UIN[:, t, :], ALU.mult).then_inc(S("mx"), 1))
                for m in range(PAIRS):
                    ve.wait_ge(S("gn_mean"), m + 1)
                    tt(halves(KK[:, m, 0:T]), halves(KK[:, m, 0:T]), bk(6 if m % 2 == 0 else 4, 2), ALU.subtract)\
                        .then_inc(S("gn_d"), 1)
                ve.wait_ge(S("gn_rs"), 1)
                step(tt(KK[:, :, 0:T], KK[:, :, 0:T], RS6[:, :, :], ALU.mult))
                for m in range(PAIRS):
                    od.done(ts(KK[:, m, 0:T], KK[:, m, 0:T], PRM[:, PC_LNW + m:PC_LNW + m + 1],
                               PRM[:, PC_LNB + m:PC_LNB + m + 1], ALU.mult, ALU.add))
                od.settle()
                step(tt(KK[:, :, 0:T], KK[:, :, 0:T], SIG[:, :, 0:T], ALU.add))
                for m in range(PAIRS):
                    def gated():
                        ve.wait_ge(S("gate_mm"), m + 1)
                        ve.wait_ge(S("x_lo"), x_ready["out0"] - KD + 2 + m)
                        tt(halves(PT2[:, m % 2, :]), halves(KK[:, m, 0:T]), bk(4 + 2 * (m % 2), 2), ALU.mult)\
                            .then_inc(S("mx"), 1)
                    mixed(2 + m, gated)
                split("out0", 0, 0)
                residual("out0")
            if "ffn0" in stages:
                split("up0", 0, 0)
                norm(nn, "up0", PC_FFN); nn += 1
                up(0)
                split("down0", 0, 0)
                residual("down0")
            if "fox" in stages:
                split("in1", 0, 0)
                norm(nn, "in1", PC_MIX + KD); nn += 1
                gemm("in1", lambda i, s: None)
                ve.wait_ge(S("f_mm"), 1)
                step(ts(halves(CUM[0:16, 0, :]), BK[0:16, 4:6, 0:HT], BF[0:16, 0:1], None, ALU.add))
                step(ts(CUM[0:16, 1, :], CUM[0:16, 0, :], -1.0, None, ALU.mult))
                tt(CUM[0:16, 1, :], CUM[0:16, 1, :], CUM[0:16, 0, :], ALU.max).then_inc(S("f_abs"), 1)
                step(ts(CUM[0:16, 2, :], CUM[0:16, 0, :], 0.0, None, ALU.min))
                ve.wait_ge(S("f_act"), 1)
                step(tt(CUM[0:16, 1, :], CUM[0:16, 1, :], CUM[0:16, 2, :], ALU.subtract))
                nc.vector.tensor_tensor_scan(CUM[0:16, 0, :], ONES[0:16, 0:1].to_broadcast([16, T]), CUM[0:16, 1, :],
                                             0.0, ALU.mult, ALU.add).then_inc(S("cum"), 1)
                ve.wait_ge(S("gain_in"), 64)
                ve.wait_ge(S("fx_ln"), FOX_PAIRS)
                o0 = od.at
                PER = 12 * 1

                def pair(i):
                    od.at = o0 + PER * i
                    ve.wait_ge(S("fx_rs"), 2 * i + 2)
                    for e, dst in ((0, QS), (1, KS)):
                        x = stt(dst[:, :].unsqueeze(1), QKV[:, ds(8 * e + i, 1), :], GAINS[:, e:e + 1],
                                RQ[:, e:e + 1, :], ALU.mult, ALU.mult)
                    x.then_inc(S("fx_k"), 1)
                    ve.wait_ge(S("cb_in"), 32 * i + 32)

                    def maxima(t):
                        e, j = divmod(t, NQ)
                        n = QT * (j + 1)
                        ve.wait_ge(S("fx_s"), 12 * i + t + 1)
                        if some(12 * i + t - 1):
                            ve.wait_ge(S("fx_e"), 12 * i + t - 1)
                        s = t % 2
                        if j >= 3:
                            od_x = stt(SS[0:QT, s, HT:n], BK[0:QT, 2 * s + 1, 0:n - HT], 0.125, CB[0:QT, e, HT:n],
                                       ALU.mult, ALU.add)
                        m = min(n, HT)
                        stt(SS[0:QT, s, 0:m], BK[0:QT, 2 * s, 0:m], 0.125, CB[0:QT, e, 0:m], ALU.mult, ALU.add)\
                            .then_inc(S("fx_ss"), 1)
                        ve.wait_ge(S("fx_ss"), 12 * i + t + 1)
                        nc.vector.tensor_reduce(MX[0:QT, s:s + 1], SS[0:QT, s, 0:n], AXX, ALU.max, negate=True)\
                            .then_inc(S("fx_mx"), 1)

                    def normed(t):
                        n = QT * (t % NQ + 1)
                        s = t % 2
                        ve.wait_ge(S("fx_e"), 12 * i + t + 1)
                        step(nc.vector.reciprocal(RC[0:QT, s:s + 1], SM[0:QT, s:s + 1]))
                        ts(PR[0:QT, s, 0:n], PR[0:QT, s, 0:n], RC[0:QT, s:s + 1], None, ALU.mult).then_inc(S("fx_p"), 1)
                    maxima(0)
                    for t in range(12):
                        if t < 11:
                            maxima(t + 1)
                        normed(t)
                    ve.wait_ge(S("ot_hi"), i + 1)
                    tt(XNL[:, ds(i, 1), :], OT[:, :].unsqueeze(1), f32(XNH[:, ds(i, 1), :]), ALU.subtract)\
                        .then_inc(S("x_lo"), 1)
                rounds(ve, FOX_PAIRS, pair, first=True, last=False)
                od.at = o0 + PER * FOX_PAIRS
                split("out1", 0, 0)
                residual("out1")
            if "ffn1" in stages:
                split("up1", 0, 0)
                norm(nn, "up1", PC_FFN + KD); nn += 1
                up(1)
                split("down1", 0, 0)
                residual("down1")
            for i in range(0, 8, 2):
                ve.wait_ge(S("o_t"), i + 1)
                if some(i):
                    ve.wait_ge(S("o_cp"), i)
                ve.tensor_copy(OUTB[:, i // 2, 0:512], BK[:, 4, :]).then_inc(S("o_cp"), 1)


_INS = ['x', 'meta_tokens', 'mix_norm', 'ffn_norm', 'even_w_in', 'even_w_out', 'rwkv_mu', 'rwkv_w0', 'rwkv_w2',
        'rwkv_a0', 'rwkv_a2', 'rwkv_g2', 'rwkv_k_k', 'rwkv_k_a', 'rwkv_r_k', 'rwkv_ln_w', 'rwkv_ln_b', 's5_a_re',
        's5_a_im', 's5_log_dt', 's5_b_re', 's5_b_im', 's5_c_re', 's5_c_im', 's5_d', 's5_glu_w', 's5_glu_b',
        'odd_w_in', 'odd_w_out', 'fox_b_f', 'fox_q_gain', 'fox_k_gain', 'ffn_w_up', 'ffn_conv_w', 'ffn_conv_b',
        'ffn_w_down']
_OUTS = [((1, SEQ, D_MODEL), 'float32')]


def kernel(**inputs):
    import numpy as _np
    import concourse.bacc as _bacc
    from concourse import mybir as _mybir
    from concourse.bass_utils import run_bass_kernel_spmd as _run

    nc = _bacc.Bacc("TRN2", target_bir_lowering=False, num_devices=1)
    arrays, args = {}, {}
    for name in _INS:
        a = _np.ascontiguousarray(inputs[name])
        arrays[f"in_{name}_dram"] = a
        args[name] = nc.dram_tensor(f"in_{name}_dram", a.shape, _mybir.dt.from_np(a.dtype), kind="ExternalInput").ap()
    shape, dtype = _OUTS[0]
    o = nc.dram_tensor("out_0_dram", shape, _mybir.dt.from_np(_np.dtype(dtype)), kind="ExternalOutput").ap()
    decoder_trunk(nc, args, o)
    r = _run(nc, [arrays], core_ids=[0])
    return r.results[0]["out_0_dram"]
```

```python
from contextlib import ExitStack
import math

import concourse.bass as bass
from concourse import mybir

F32 = mybir.dt.float32
F32R = mybir.dt.float32r
ALU = mybir.AluOpType
ACT = mybir.ActivationFunctionType
AXX = mybir.AxisListType.X
ds = bass.ds

P = 128
D_MODEL = 1024
KD = D_MODEL // P
SEQ = 512
N_META = 16
T = SEQ + N_META
HT = T // 2
D_FF = 2816
KF = D_FF // P
RWKV_DIM = 768
PAIRS = RWKV_DIM // P
LORA = 64
S5_TILES = 2
N_STATE_TILES = 8
C = 64
CHUNKS = -(-T // C)
TP = CHUNKS * C
G3 = 3
FOX_PAIRS = 8
TILES = [(0, N_META)] + [(t, t + P) for t in range(N_META, T, P)]
NQ = len(TILES)
SLOT = (0, 0, 1, 0, 1)
BANKS_BACK = (2, 1, 3, 2, 2)
COLS_BACK = (5, 3, 3, 2, 2)
RMS_EPS = 1e-6
GN_EPS = 64e-5
DECAY = math.exp(-0.5)
LN_SHIFT = 2.0 ** 30
MASKED = -(2.0 ** 100)

PC_MIX, PC_FFN, PC_MU, PC_W0, PC_A0, PC_KK, PC_KA, PC_RK, PC_LNW, PC_LNB, PC_SD, PC_GLB, PC_ARE, PC_AIM = (
    0, 16, 32, 52, 58, 64, 70, 76, 82, 88, 94, 96, 98, 106)
PC_CONV = 114
CONV_COLS = 4 * 2 * KF
N_PRM = PC_CONV + 2 * CONV_COLS
N_PRM_LOADS = 24
MIXED = (6, 7, 0, 1, 2, 3, 4, 5)

GEMMS = [("in0", 22, KD, 22), ("out0", 8, KD, 8), ("up0", 2 * KF, KD, 2 * KF), ("down0", 16, KF // 2, 8),
         ("in1", 24, KD, 24), ("out1", 8, KD, 8), ("up1", 2 * KF, KD, 2 * KF), ("down1", 16, KF // 2, 8)]


def plan(stages):
    need = {"mix0": ("in0", "out0"), "ffn0": ("up0", "down0"), "fox": ("in1", "out1"), "ffn1": ("up1", "down1")}
    used = {g for s in stages if s in need for g in need[s]}
    u = q = 0
    at = {}
    for name, units, k, groups in GEMMS:
        if name in used:
            at[name] = (u, q, units, k)
            u += units
            q += groups
    return at


def decoder_trunk(nc, a, out, stages=("mix0", "ffn0", "fox", "ffn1")):
    at = plan(stages)
    ctx = ExitStack()
    with ctx:
        base = [16512]
        END = 229368
        used_to = [0]

        def put(name, shape, dt, offset):
            n = 4
            for d in shape[1:]:
                n *= d
            assert offset + n <= END, (name, offset, n)
            used_to[0] = max(used_to[0], offset + n)
            return nc.alloc_sbuf_tensor_at(name, shape, dt, offset=offset)

        def row(start):
            pos = [start]

            def place(name, *shape, dt=F32):
                n = 4
                for d in shape:
                    n *= d
                t = put(name, [P, *shape], dt, pos[0])
                pos[0] += -(-n // 32) * 32
                return t
            place.pos = pos
            return place

        keep = row(base[0])
        H = keep("H", KD, T)
        PRM = keep("PRM", N_PRM)
        IDENT = keep("IDENT", P)
        BONES = keep("BONES", P)
        BONES64 = keep("BONES64", P)
        ONES = keep("ONES", P)
        EPS = keep("EPS", 4)
        GAINS = keep("GAINS", 2)
        MAG = keep("MAG", N_STATE_TILES)
        POW = keep("POW", N_STATE_TILES, 10, 2)
        PCH = keep("PCH", PAIRS, CHUNKS)
        RAW = keep("RAW", 2, KF // 2, P)
        wpos = keep.pos[0]
        WHI = keep("WHI", 2, KF // 2, P, dt=F32R)
        WLO = keep("WLO", 2, KF // 2, P, dt=F32R)
        wend = keep.pos[0]
        hpos = keep.pos[0]
        XNH = keep("XNH", KD, T, dt=F32R)
        XNL = keep("XNL", KD, T, dt=F32R)
        zpos = keep.pos[0]
        z = row(zpos)
        XIN = z("XIN", 5, D_MODEL)
        PRAW = z("PRAW", 6, P)
        SQ = z("SQ", 2, T)
        RST = z("RST", 2, HT)
        NT = z("NT", 2, T)
        z = row(zpos)
        GH = z("GH", KF, T, dt=F32R)
        GL = z("GL", KF, T, dt=F32R)
        CP = z("CP", 2, T + 2)
        CA = z("CA", 2, T)
        SG = z("SG", T)
        GT = z("GT", T)
        z = row(zpos)
        RKV = z("RKV", 20, TP)
        KK = z("KK", PAIRS, TP)
        AA = z("AA", PAIRS, TP)
        SIG = z("SIG", PAIRS, TP)
        r6 = z.pos[0]
        CS = z("CS", PAIRS, TP)
        PP = z("PP", PAIRS, CHUNKS, C + 1)
        UIN = z("UIN", S5_TILES, T)
        tail = z.pos[0]
        PB = put("PB", [P, 2, T + 1], F32, r6)
        DT = put("DT", [P, 2, T], F32, r6 + 2 * (T + 1) * 4 + 24)
        z = row(r6 + 9216)
        WB = z("WB", 2, N_STATE_TILES, P)
        BR = z("BR", 2, N_STATE_TILES, 16)
        BB = z("BB", 2, N_STATE_TILES, 16)
        S5V = z("S5V", 16, N_STATE_TILES)
        assert z.pos[0] <= tail - 4 * S5_TILES * T
        BBM = put("BBM", [P, 2, N_STATE_TILES, P], F32, zpos + 36864)
        U = put("U", [P, 2, N_STATE_TILES, T], F32, hpos)
        W2A2 = put("W2A2", [P, RWKV_DIM], F32, wpos)
        RESET = put("RESET", [P, TP], F32, wpos + 4 * RWKV_DIM)
        G2 = put("G2", [P, RWKV_DIM], F32, wpos)
        GLW = put("GLW", [P, 2, 2 * P], F32, wpos + 4 * RWKV_DIM)
        z = row(wpos)
        KR = z("KR", PAIRS, 3, C)
        BH = z("BH", PAIRS, C)
        KH = z("KH", PAIRS, C)
        VH = z("VH", PAIRS, C)
        MQA = z("MQA", PAIRS, 2, 2, C)
        SS0 = z("SS0", PAIRS, C)
        LVL = z("LVL", 5, P)
        M1 = z("M1", P)
        M1T = z("M1T", P)
        MU2 = z("MU2", P)
        MQ = z("MQ", 2, C)
        assert z.pos[0] <= wend
        z = row(r6)
        AT = z("AT", PAIRS, 2, C)
        XX = z("XX", PAIRS, 2, C)
        XT = z("XT", PAIRS, 2, C)
        TM = z("TM", PAIRS, 2, C)
        BKT = z("BKT", PAIRS, 2, C)
        VT = z("VT", PAIRS, C)
        NG = z("NG", PAIRS, C)
        SA = z("SA", PAIRS, C)
        assert z.pos[0] <= tail - 4 * S5_TILES * T - 8 * T
        FC = put("FC", [P, 2, T], F32, tail - 4 * S5_TILES * T - 8 * T)
        z = row(tail)
        FT2 = z("FT2", T)
        FT1 = put("FT1", [P, T], F32, zpos + 18 * 4 * TP)
        MK = put("MK", [P, 4, P], F32, zpos + 20 * 4 * TP)
        BOTH = put("BOTH", [P, P], F32, wpos + 4 * RWKV_DIM + 4 * TP)
        z = row(r6)
        RS6 = z("RS6", PAIRS, T)
        WC = z("WC", 2, N_STATE_TILES, P)
        CRAW = z("CRAW", 2, 2, 2, C)
        MK2 = z("MK2", 4, P)
        assert z.pos[0] <= tail - 4 * S5_TILES * T
        PT2 = put("PT2", [P, 2, T], F32, zpos)
        z = row(zpos)
        QKV = z("QKV", 24, T)
        FRS = z("FRS", 16, T)
        PTT = z("PTT", 2, NQ, T)
        PR = z("PR", 2, 2, T)
        MX = z("MX", NQ, 2)
        SM = z("SM", NQ, 2)
        RC = z("RC", NQ, 2)
        CM = z("CM", P)
        fpos = zpos + 24 * T * 4 + 16 * T * 4
        CUM = put("CUM", [P, 3, T], F32, fpos)
        FSQ = put("FSQ", [P, 2, T], F32, fpos + 3 * T * 4)
        z = row(zpos + 106112)
        WF = z("WF", KD, 16)
        WFH = z("WFH", KD, 16, dt=F32R)
        WFL = z("WFL", KD, 16, dt=F32R)
        BF = z("BF", 1)
        z = row(wpos)
        QZ = z("QZ", 2, T)
        KS = z("KS", T)
        VF = z("VF", T)
        VS = z("VS", NQ, P)
        SS = z("SS", 2, 2, T)
        OT = z("OT", T)
        assert z.pos[0] <= wend
        CB = put("CB", [P, 2, FOX_PAIRS, T], F32, hpos)
        OUTB = put("OUTB", [P, 4, D_MODEL], F32, zpos)
        BK = ctx.enter_context(nc.psum_tensor("BK", [P, 8, 512], F32))
        cum_dram = nc.dram_tensor("cum_dram", [16, T], F32, kind="Internal").ap()

        sems = {}

        def S(name):
            if name not in sems:
                sems[name] = ctx.enter_context(nc.semaphore(name))
            return sems[name]

        def some(count):
            return not isinstance(count, int) or count > 0

        class Order:

            def __init__(self, eng, name):
                self.eng, self.name, self.at = eng, name, 0

            def done(self, ins):
                ins.then_inc(S(self.name), 1)
                self.at = self.at + 1

            def settle(self):
                if some(self.at):
                    self.eng.wait_ge(S(self.name), self.at)

        def rounds(eng, n, body, first=False, last=True):
            lo, hi = (1 if first else 0), (n - 1 if last else n)
            if first:
                body(0)
            if hi > lo:
                with eng.Fori(lo, hi) as i:
                    body(i)
            if last:
                body(n - 1)

        def bk(lo, n):
            return BK[:, lo:lo + n, 0:HT]

        def halves(ap):
            return ap.rearrange("p (a b) -> p a b", a=2)

        w_src = {
            "in0": a["even_w_in"][0], "out0": a["even_w_out"][0], "in1": a["odd_w_in"][0], "out1": a["odd_w_out"][0],
            "up0": a["ffn_w_up"][0], "up1": a["ffn_w_up"][1], "down0": a["ffn_w_down"][0], "down1": a["ffn_w_down"][1],
        }
        x_in = {g: (XNH, XNL) for g in ("in0", "out0", "in1", "out1", "up0", "up1")}
        x_in["down0"] = x_in["down1"] = (GH, GL)
        x_ready, n_x = {}, 0
        for g, _, _, _ in GEMMS:
            if g in at:
                n_x += KF if g.startswith("down") else KD
                x_ready[g] = n_x
        h_ready = {g: at[g][1] + KD for g in ("out0", "down0", "out1", "down1") if g in at}
        n_groups = max([0] + list(h_ready.values()))

        block = ctx.enter_context(nc.Block())

        @block.sync
        def _(sp):
            def rows(src, n, tile, r0):
                sp.dma_start(PRAW[r0:r0 + n, tile, :], src.rearrange("(m p) -> m p", p=P)).then_inc(S("prm_in"), 16)
                return 1
            n = 0
            for l in range(2):
                n += rows(a["mix_norm"][l], KD, 0, PC_MIX + KD * l)
                n += rows(a["ffn_norm"][l], KD, 0, PC_FFN + KD * l)
            for key, col, m in (("rwkv_mu", PC_MU, 20), ("rwkv_w0", PC_W0, 6), ("rwkv_a0", PC_A0, 6),
                                ("rwkv_k_k", PC_KK, 6), ("rwkv_k_a", PC_KA, 6), ("rwkv_ln_w", PC_LNW, 6),
                                ("rwkv_ln_b", PC_LNB, 6), ("s5_d", PC_SD, 2), ("s5_glu_b", PC_GLB, 2)):
                n += rows(a[key][0], m, 0, col)
            n += rows(a["rwkv_r_k"][0].rearrange("h d -> (h d)"), 6, 0, PC_RK)
            n += rows(a["s5_a_re"][0].rearrange("g n -> (g n)"), 8, 0, PC_ARE)
            n += rows(a["s5_a_im"][0].rearrange("g n -> (g n)"), 8, 0, PC_AIM)
            for l in range(2):
                for t in range(2):
                    n += rows(a["ffn_conv_w"][l, t], 2 * KF, 1 + 2 * l, 2 * KF * t)
                n += rows(a["ffn_conv_w"][l, 2], 2 * KF, 2 + 2 * l, 0)
                n += rows(a["ffn_conv_b"][l], 2 * KF, 2 + 2 * l, 2 * KF)
            sp.dma_start(S5V[0:8, 15, 0:2], a["s5_log_dt"][0].rearrange("(j g) -> j g", g=2)).then_inc(S("prm_in"), 16)
            assert n == N_PRM_LOADS
            for i, key in enumerate(("s5_b_re", "s5_b_im")):
                sp.dma_start(BR[:, i, :, :], a[key][0].rearrange("(j g) n c -> (g n) j c", g=2)).then_inc(S("b_in"), 16)
            for e in range(2):
                for i, key in enumerate(("fox_q_gain", "fox_k_gain")):
                    sp.dma_start(GAINS[64 * e:64 * e + 64, i:i + 1],
                                 a[key][0].rearrange("(d o) -> d o", o=1)).then_inc(S("gain_in"), 16)
            sp.dma_start(XIN[0:N_META, 0, :], a["meta_tokens"]).then_inc(S("x_in"), 16)
            for j in range(4):
                sp.dma_start(XIN[:, 1 + j, :], a["x"][0, P * j:P * j + P, :]).then_inc(S("x_in"), 16)

            def load(g, i, s):
                u0, _, _, k = at[g]
                if some(u0 + 2 * i + s - 1):
                    sp.wait_ge(S("w_lo"), u0 + 2 * i + s - 1)
                w = w_src[g]
                if g.startswith("down"):
                    src = w.rearrange("(s k p) n -> s p k n", s=2, p=P)[s, :, :, ds(i * P, P)]
                elif g.startswith("up"):
                    src = w.rearrange("(k p) n -> p k n", p=P)[:, :, ds(i * P + s * D_FF, P)]
                else:
                    src = w.rearrange("(k p) n -> p k n", p=P)[:, :, ds((2 * i + s) * P, P)]
                sp.dma_start(RAW[:, s, 0:k, :], src).then_inc(S(f"w_in{s}"), 16)

            def loads(g, lo=0):
                first = at[g][0] == 0
                n = at[g][2] // 2
                if first or lo:
                    for s in range(2):
                        load(g, lo, s)
                    lo += 1
                with sp.Fori(lo, n) as i:
                    for s in range(2):
                        load(g, i, s)

            if "mix0" in stages:
                loads("in0")
                sp.wait_ge(S("w_used"), 22)
                sp.dma_start(W2A2[0:LORA, :], a["rwkv_w2"][0]).then_inc(S("lora_in"), 16)
                sp.dma_start(W2A2[LORA:2 * LORA, :], a["rwkv_a2"][0]).then_inc(S("lora_in"), 16)
                for s in range(2):
                    load("out0", 0, s)
                for g in range(2):
                    sp.wait_ge(S(f"y_out{g}"), CHUNKS)
                    sp.wait_ge(S(f"state{g}"), CHUNKS)
                sp.dma_start(G2[:, :], a["rwkv_g2"][0]).then_inc(S("post_in"), 16)
                sp.dma_start(GLW[:, :, :], a["s5_glu_w"][0].rearrange("(k p) n -> p k n", p=P)).then_inc(S("post_in"), 16)
                for i, key in enumerate(("s5_c_re", "s5_c_im")):
                    src = a[key][0].rearrange("g c n -> (g c) n").rearrange("(t r) n -> r t n", r=P)
                    for e in range(2):
                        sp.dma_start(CRAW[:, i, :, e, :], src).then_inc(S("post_in"), 16)
                u0 = at["out0"][0]
                with sp.Fori(1, 4) as i:
                    for s in range(2):
                        load("out0", i, s)
            if "ffn0" in stages:
                loads("up0")
                loads("down0")
            if "fox" in stages:
                sp.dma_start(WF[:, :, :], a["odd_w_in"][0].rearrange("(k p) n -> p k n", p=P)[:, :, 3 * D_MODEL:])\
                    .then_inc(S("wf_in"), 16)
                sp.dma_start(BF[0:16, :], a["fox_b_f"][0].rearrange("(h o) -> h o", o=1)).then_inc(S("wf_in"), 16)
                loads("in1")
                for s in range(2):
                    load("out1", 0, s)
                sp.wait_ge(S("cum"), 1)
                sp.dma_start(cum_dram, CUM[0:16, 0, :]).then_inc(S("cum_out"), 16)
                sp.wait_ge(S("cum_out"), 16)
                sp.wait_ge(S("w_used"), at["in1"][0] + 24)
                for i in range(FOX_PAIRS):
                    sp.dma_start(CB[:, :, i, :], cum_dram[2 * i:2 * i + 2, :].unsqueeze(0).to_broadcast([P, 2, T]))\
                        .then_inc(S("cb_in"), 16)
                with sp.Fori(1, 4) as i:
                    for s in range(2):
                        load("out1", i, s)
            if "ffn1" in stages:
                loads("up1")
                loads("down1")
            for j in range(4):
                sp.wait_ge(S("o_cp"), 2 * j + 2)
                sp.dma_start(out[0, P * j:P * j + P, :], OUTB[:, j, :]).then_inc(S("stored"), 16)
            sp.wait_ge(S("stored"), 64)

        @block.gpsimd
        def _(po):
            od = Order(po, "po_order")

            def step(ins):
                od.done(ins)
                od.settle()

            step(po.memset(IDENT[:, :], 0.0))
            po.affine_select(out=IDENT[:, :], in_=IDENT[:, :], compare_op=ALU.not_equal, fill=1.0, base=0,
                             pattern=[[-1, P]], channel_multiplier=1).then_inc(S("ident"), 1)
            po.wait_ge(S("ident"), 1)
            for t, v in ((BONES, 1.0), (BONES64, 1.0 / 64)):
                step(po.memset(t[:, :], 0.0))
                step(po.memset(t[0:64, 0:64], v))
                step(po.memset(t[64:128, 64:128], v))
            for i, v in enumerate((RMS_EPS, GN_EPS, 0.5 * math.log(LN_SHIFT))):
                step(po.memset(EPS[:, i:i + 1], v))

            def channel_masks(mk, name):
                step(po.memset(mk[:, :, :], 0.0))
                for e in range(2):
                    for jj in range(4):
                        po.memset(mk[64 * e:64 * e + 64, jj, 16 * (2 * jj + e):16 * (2 * jj + e) + 16], 1.0)\
                            .then_inc(S(name), 1)
                        po.wait_ge(S(name), 4 * e + jj + 1)
            channel_masks(MK, "mk")
            po.memset(ONES[:, :], 1.0).then_inc(S("consts"), 1)
            po.wait_ge(S("consts"), 1)
            if "mix0" in stages:
                po.wait_ge(S("w_used"), 22)
                step(po.memset(MU2[:, :], 1.0))
                step(po.affine_select(out=MU2[:, :], in_=MU2[:, :], compare_op=ALU.is_gt, fill=0.0, base=0,
                                      pattern=[[1, P]], channel_multiplier=-1))
                step(po.memset(MU2[0:64, 64:128], 0.0))
                incl = BOTH[:, :]
                step(po.memset(incl, 1.0))
                step(po.affine_select(out=incl, in_=incl, compare_op=ALU.is_ge, fill=0.0, base=0,
                                      pattern=[[1, P]], channel_multiplier=-1))
                for e in range(2):
                    h = slice(64 * e, 64 * e + 64)
                    step(po.tensor_copy(MQ[h, 0, :], MU2[h, 64 * e:64 * e + 64]))
                    step(po.tensor_copy(MQ[h, 1, :], BOTH[h, 64 * e:64 * e + 64]))
                step(po.memset(M1[:, :], 0.0))
                step(po.memset(M1T[:, :], 0.0))
                m1 = M1[:, :].rearrange("p (q r) -> p q r", r=2)
                m1t = M1T[:, :].rearrange("p (q r) -> p q r", r=2)
                step(po.affine_select(out=m1[:, :, 0], in_=m1[:, :, 0], compare_op=ALU.not_equal, fill=-1.0, base=-1,
                                      pattern=[[-2, 64]], channel_multiplier=1))
                step(po.affine_select(out=m1t[:, :, 1], in_=m1t[:, :, 1], compare_op=ALU.not_equal, fill=-1.0, base=0,
                                      pattern=[[-2, 64]], channel_multiplier=1))
                for n in range(5):
                    b = 2 << n
                    m = LVL[:, n, :].rearrange("p (q r c) -> p q r c", r=2, c=b)
                    step(po.memset(LVL[:, n, :], 0.0))
                    step(po.memset(m[:, :, 0, :], 1.0))
                    step(po.affine_select(out=m[:, :, 0, :], in_=m[:, :, 0, :], compare_op=ALU.is_ge, fill=0.0, base=-b,
                                          pattern=[[-2 * b, 64 // b], [0, b]], channel_multiplier=1))
                    po.affine_select(out=m[:, :, 0, :], in_=m[:, :, 0, :], compare_op=ALU.is_ge, fill=0.0,
                                     base=2 * b - 1, pattern=[[2 * b, 64 // b], [0, b]], channel_multiplier=-1)\
                        .then_inc(S("masks"), 1)
                    po.wait_ge(S("masks"), n + 1)
                step(po.memset(RESET[:, :], 1.0))
                po.memset(RESET[:, :].rearrange("p (c t) -> p c t", t=C)[:, :, 0:1], 0.0).then_inc(S("reset"), 1)
                po.wait_ge(S("reset"), 1)
                for n, t in enumerate((RKV[:, 0:3 * PAIRS, T:TP], KK[:, :, T:TP], AA[:, :, T:TP], SIG[:, :, T:TP])):
                    po.memset(t, 0.0).then_inc(S("pads"), 1)
                    po.wait_ge(S("pads"), n + 1)
                po.wait_ge(S("tilde"), 1)
                step(po.memset(SS0[:, :, :], 0.0))
                for e in range(2):
                    h = slice(64 * e, 64 * e + 64)
                    for p in range(PAIRS):
                        po.tensor_copy(KR[h, p, 2, :], IDENT[h, 64 * e:64 * e + 64]).then_inc(S("chunk_init"), 1)
                        po.wait_ge(S("chunk_init"), PAIRS * e + p + 1)
                po.wait_ge(S("s5_pow"), 1)
                po.wait_ge(S("s5_ucp"), 2 * N_STATE_TILES)
                od_loop = od.at

                def own_wait():
                    po.sem_inc(S("po_turn"), 1)

                def s5_tile(j):
                    od.at = od_loop + PER * j
                    cos, sin = FC[:, 0, :], FC[:, 1, :]
                    t1, t2 = FT1[:, :], FT2[:, :]
                    if some(2 * j):
                        po.wait_ge(S("s5_out"), 2 * j)
                    own_wait()
                    step(po.memset(FC[:, 0, 0:1], 1.0))
                    own_wait()
                    step(po.memset(FC[:, 1, 0:1], 0.0))
                    n = 1
                    for lev in range(10):
                        m = min(n, T - n)
                        pc = POW[:, ds(j, 1), lev, 0:1].rearrange("p a b -> p (a b)").to_broadcast([P, m])
                        ps = POW[:, ds(j, 1), lev, 1:2].rearrange("p a b -> p (a b)").to_broadcast([P, m])
                        own_wait()
                        step(po.tensor_tensor(t1[:, 0:m], cos[:, 0:m], pc, ALU.mult))
                        own_wait()
                        step(po.tensor_tensor(t2[:, 0:m], sin[:, 0:m], ps, ALU.mult))
                        step(po.tensor_tensor(cos[:, n:n + m], t1[:, 0:m], t2[:, 0:m], ALU.subtract))
                        own_wait()
                        step(po.tensor_tensor(t1[:, 0:m], sin[:, 0:m], pc, ALU.mult))
                        own_wait()
                        step(po.tensor_tensor(t2[:, 0:m], cos[:, 0:m], ps, ALU.mult))
                        step(po.tensor_tensor(sin[:, n:n + m], t1[:, 0:m], t2[:, 0:m], ALU.add))
                        n += m
                    ur = U[:, 0, ds(j, 1), :].rearrange("p a t -> p (a t)")
                    ui = U[:, 1, ds(j, 1), :].rearrange("p a t -> p (a t)")
                    own_wait()
                    step(po.tensor_tensor(t1, ur, sin, ALU.mult))
                    own_wait()
                    step(po.tensor_tensor(t2, ui, sin, ALU.mult))
                    own_wait()
                    step(po.tensor_tensor(ur, ur, cos, ALU.mult))
                    own_wait()
                    step(po.tensor_tensor(ui, ui, cos, ALU.mult))
                    own_wait()
                    po.tensor_tensor(ur, ur, t2, ALU.add).then_inc(S("s5_in"), 1)
                    po.wait_ge(S("s5_in"), 2 * j + 1)
                    own_wait()
                    po.tensor_tensor(ui, ui, t1, ALU.subtract).then_inc(S("s5_in"), 1)
                    po.wait_ge(S("s5_scan"), 2 * j + 2)
                    own_wait()
                    step(po.tensor_tensor(t1, ur, sin, ALU.mult))
                    own_wait()
                    step(po.tensor_tensor(t2, ui, sin, ALU.mult))
                    own_wait()
                    step(po.tensor_tensor(ur, ur, cos, ALU.mult))
                    own_wait()
                    step(po.tensor_tensor(ui, ui, cos, ALU.mult))
                    own_wait()
                    po.tensor_tensor(ur, ur, t2, ALU.subtract).then_inc(S("s5_out"), 1)
                    po.wait_ge(S("s5_out"), 2 * j + 1)
                    own_wait()
                    po.tensor_tensor(ui, ui, t1, ALU.add).then_inc(S("s5_out"), 1)

                PER = 2 + 10 * 6 + 4 + 4
                rounds(po, N_STATE_TILES, s5_tile, first=True, last=False)
                od.at = od_loop + PER * N_STATE_TILES
                for g in range(2):
                    po.wait_ge(S(f"y_out{g}"), CHUNKS)
                    po.wait_ge(S(f"state{g}"), CHUNKS)
                channel_masks(MK2, "mk2")
            if "fox" in stages:
                po.wait_ge(S("fx_rs"), FOX_PAIRS)
                step(po.memset(CM[:, :], 0.0))
                po.affine_select(out=CM[:, :], in_=CM[:, :], compare_op=ALU.is_ge, fill=MASKED, base=0,
                                 pattern=[[-1, P]], channel_multiplier=1).then_inc(S("causal"), 1)
                po.wait_ge(S("w_used"), at["in1"][0] + 24)
                po.wait_ge(S("ps_free"), at["in1"][1] + 24)

                po.wait_ge(S("causal"), 1)
                for e in range(2):
                    po.memset(QZ[64 - 64 * e:128 - 64 * e, e, :], 0.0).then_inc(S("qz"), 1)
                    po.wait_ge(S("qz"), e + 1)

                def values(i):
                    if some(i):
                        po.wait_ge(S("fx_vt"), i)
                    po.tensor_copy(VF[:, :], QKV[:, ds(16 + i, 1), :].rearrange("p a t -> p (a t)")).then_inc(S("fx_vf"), 1)
                rounds(po, FOX_PAIRS, values, first=True, last=False)

        @block.tensor
        def _(pe):
            def mm(o, l, r, start=True, stop=True, check=False):
                return pe.matmul(o, l, r, start=start, stop=stop, skip_group_check=check)

            def own_wait():
                pe.sem_inc(S("pe_turn"), 1)

            def norm_sums(n):
                for k in range(KD):
                    pe.wait_ge(S("sq"), KD * n + k + 1)
                    for h in range(2):
                        x = mm(BK[:, 4 + h, 0:HT], ONES[:, :], SQ[:, k % 2, h * HT:h * HT + HT], k == 0, k == KD - 1)
                    x.then_inc(S("sq_used"), 1)

            def unit(g, i, s, group, slot, start, stop):
                u0, _, _, kn = at[g]
                xh, xl = x_in[g]
                k0 = s * kn if g.startswith("down") else 0
                pe.wait_ge(S("w_lo"), u0 + 2 * i + s + 1)
                if start:
                    if some(group - 1):
                        pe.wait_ge(S("ps_free"), group - 1)
                for k in range(kn):
                    for n, (w, x) in enumerate(((WHI, xh), (WHI, xl), (WLO, xh))):
                        for h in range(2):
                            last = mm(BK[:, 2 * slot + h, 0:HT], w[:, s, k, :], x[:, k0 + k, h * HT:h * HT + HT],
                                      start and k == 0 and n == 0, stop and k == kn - 1 and n == 2)
                last.then_inc(S("w_used"), 1)

            def gemm(g):
                u0, q0, units, _ = at[g]
                pe.wait_ge(S("x_lo"), x_ready[g])
                if g.startswith("down"):
                    def body(ii):
                        for r in range(2):
                            for s in range(2):
                                unit(g, 2 * ii + r, s, q0 + 2 * ii + r, r, s == 0, s == 1)
                    rounds(pe, KD // 2, body, last=False, first=q0 == 0)
                else:
                    def body(i):
                        for s in range(2):
                            unit(g, i, s, q0 + 2 * i + s, s, True, True)
                    rounds(pe, units // 2, body, last=False, first=q0 == 0)

            pe.wait_ge(S("ident"), 1)
            pe.wait_ge(S("consts"), 1)
            pe.wait_ge(S("prm_in"), 16 * (N_PRM_LOADS + 1))
            pe.wait_ge(S("ldt"), 1)
            sizes = (114, 88, 88, 88, 88)
            for t, n in enumerate(sizes):
                pe.transpose(BK[:, t // 4, P * (t % 4):P * (t % 4) + n], PRAW[0:n, t, :], IDENT[0:n, 0:n])
            pe.transpose(BK[:, 1, P:P + 8], PRAW[0:8, 5, :], IDENT[0:8, 0:8]).then_inc(S("prm_t"), 1)
            pe.wait_ge(S("x_in"), 80)
            for j in range(5):
                n = N_META if j == 0 else P
                for b in range(2):
                    i = 2 * j + b
                    if some(i - 1):
                        pe.wait_ge(S("x_cp"), i - 1)
                    for k in range(4):
                        x = pe.transpose(BK[:, 2 + i % 2, P * k:P * k + n], XIN[0:n, j, P * (4 * b + k):P * (4 * b + k) + P],
                                         IDENT[0:n, 0:n])
                    x.then_inc(S("x_t"), 1)

            nn = 0
            if "mix0" in stages:
                pe.wait_ge(S("bbm"), 1)
                for i in range(2):
                    for j in range(0, N_STATE_TILES, 4):
                        b = 6 + (2 * i + j // 4) % 2
                        if some(2 * i + j // 4 - 1):
                            pe.wait_ge(S("wb_cp"), 2 * i + j // 4 - 1)
                        for jj in range(4):
                            x = pe.transpose(BK[:, b, P * jj:P * jj + P], BBM[:, i, j + jj, :], IDENT[:, :])
                        x.then_inc(S("wb_t"), 1)
                norm_sums(nn); nn += 1
                gemm("in0")
                pe.wait_ge(S("wb_cp"), 4)
                pe.wait_ge(S("ps_free"), 22)
                for j in range(N_STATE_TILES):
                    for i in range(2):
                        n = 2 * j + i
                        if some(n - 1):
                            pe.wait_ge(S("s5_ucp"), n - 1)
                        for h in range(2):
                            x = mm(BK[:, 4 + 2 * (n % 2) + h, 0:HT], WB[:, i, j, :], UIN[:, j // 4, h * HT:h * HT + HT])
                        x.then_inc(S("s5_bum"), 1)
                pe.wait_ge(S("lora_in"), 32)
                pe.wait_ge(S("lora_act"), 1)
                for m in range(PAIRS):
                    for i in range(2):
                        n = 2 * m + i
                        if some(n - 1):
                            pe.wait_ge(S("lora_cp"), n - 1)
                        r = slice(LORA * i, LORA * i + LORA)
                        for h in range(2):
                            x = mm(BK[:, 2 * (n % 2) + h, 0:HT], W2A2[r, P * m:P * m + P], RKV[r, 18, h * HT:h * HT + HT])
                        x.then_inc(S("lora_mm"), 1)
                for m in range(PAIRS):
                    pe.wait_ge(S("kk_sq"), m + 1)
                    if some(m - 1):
                        pe.wait_ge(S("kk_max"), m - 1)
                    for h in range(2):
                        x = mm(BK[:, 4 + 2 * (m % 2) + h, 0:HT], BONES[:, :], CS[:, m, h * HT:h * HT + HT])
                    x.then_inc(S("kk_sum"), 1)
                for m in range(PAIRS):
                    pe.wait_ge(S("rk"), m + 1)
                    if some(m - 1):
                        pe.wait_ge(S("bonus"), m - 1)
                    for h in range(2):
                        x = mm(BK[:, 2 * (m % 2) + h, 0:HT], BONES[:, :], SIG[:, m, h * HT:h * HT + HT])
                    x.then_inc(S("bonus_mm"), 1)

                pe.wait_ge(S("chunk_init"), 2 * PAIRS)

                def chunk(c):
                    for p in range(PAIRS):
                        g = p // G3
                        if p % G3 == 0:
                            pe.wait_ge(S(f"stage{g}"), c + 1)
                        if p == 0:
                            pe.wait_ge(S("v_stage"), c + 1)
                        if isinstance(c, int) and c == 0:
                            if some(p - 1):
                                pe.wait_ge(S("ph_out"), p - 1)
                        else:
                            pe.wait_ge(S("ph_out"), PAIRS * c + p - 1)
                        own_wait()
                        b = p % 2
                        for e in range(2):
                            h = slice(64 * e, 64 * e + 64)
                            mm(BK[h, b, 0:192], BH[h, p, :], KR[h, p, :, :])
                            mm(BK[h, b, 192:384], KH[h, p, :], KR[h, p, :, :])
                            mm(BK[h, b, 384:448], KR[h, p, 0, :], BH[h, p, :])
                            x = mm(BK[h, b, 448:512], VH[h, p, :], KR[h, p, 2, :])
                        x.then_inc(S("ph"), 1)
                    for n in range(5):
                        for g in range(2):
                            pe.wait_ge(S(f"x_up{g}"), 6 * c + n + 1)
                            for q in range(G3):
                                p = G3 * g + q
                                x = mm(BK[:, 2 + 3 * g, P * q:P * q + P], AT[:, p, :, :], XX[:, p, :, :])
                            x.then_inc(S(f"t_mm{g}"), 1)
                        for g in range(2):
                            pe.wait_ge(S(f"t_mask{g}"), 5 * c + n + 1)
                            for q in range(G3):
                                p = G3 * g + q
                                if n < 4:
                                    mm(BK[:, 3 + 3 * g, P * q:P * q + P], XT[:, p, :, :], TM[:, p, :, :])
                                x = mm(BK[:, 4 + 3 * g, P * q:P * q + P], TM[:, p, :, :], XT[:, p, :, :])
                            x.then_inc(S(f"x_mm{g}"), 1)
                    for g in range(2):
                        pe.wait_ge(S(f"x_up{g}"), 6 * c + 6)
                        if some(c):
                            pe.wait_ge(S(f"state{g}"), c)
                        pe.wait_ge(S("ph_out"), PAIRS * c + G3 * (g + 1))
                        own_wait()
                        for q in range(G3):
                            p = G3 * g + q
                            for e in range(2):
                                h = slice(64 * e, 64 * e + 64)
                                o = BK[h, 2 + 3 * g, C * q:C * q + C]
                                mm(o, KR[h, p, 0, :], SS0[h, p, :], True, False)
                                x = mm(o, MQA[h, p, 1, 0, :], VT[h, p, :], False, True)
                        x.then_inc(S(f"g_mm{g}"), 1)
                    for g in range(2):
                        pe.wait_ge(S(f"g_cp{g}"), c + 1)
                        own_wait()
                        for q in range(G3):
                            p = G3 * g + q
                            for e in range(2):
                                h = slice(64 * e, 64 * e + 64)
                                x = mm(BK[h, 3 + 3 * g, C * q:C * q + C], XT[h, p, e, :], NG[h, p, :])
                        x.then_inc(S(f"sa_mm{g}"), 1)
                    for g in range(2):
                        pe.wait_ge(S(f"sa_cp{g}"), c + 1)
                        own_wait()
                        for q in range(G3):
                            p = G3 * g + q
                            for e in range(2):
                                h = slice(64 * e, 64 * e + 64)
                                o = BK[h, 4 + 3 * g, C * q:C * q + C]
                                mm(o, SS0[h, p, :], KR[h, p, 1, :], True, False)
                                mm(o, SA[h, p, :], MQA[h, p, 0, 1, :], False, False)
                                mm(o, VT[h, p, :], MQA[h, p, 1, 1, :], False, True)
                                o = BK[h, 2 + 3 * g, C * q:C * q + C]
                                mm(o, BKT[h, p, 0, :], SA[h, p, :], True, False)
                                x = mm(o, BKT[h, p, 1, :], VT[h, p, :], False, True)
                        x.then_inc(S(f"y_mm{g}"), 1)
                rounds(pe, CHUNKS, chunk, first=True, last=False)

                pe.wait_ge(S("post_in"), 16 * 6)
                for i in range(2):
                    for t in range(2):
                        x = pe.transpose(BK[:, 0, P * (2 * i + t):P * (2 * i + t) + P],
                                         CRAW[:, i, t, :, :], IDENT[:, :])
                x.then_inc(S("c_t"), 1)
                pe.wait_ge(S("wc"), 2)
                pe.wait_ge(S("s5_out"), 2 * N_STATE_TILES)
                for t in range(2):
                    for h in range(2):
                        n = 0
                        for jj in range(4):
                            for i in range(2):
                                x = mm(BK[:, 1 + 2 * t + h, 0:HT], WC[:, i, 4 * t + jj, :],
                                       U[:, i, 4 * t + jj, h * HT:h * HT + HT], n == 0, n == 7)
                                n += 1
                    x.then_inc(S("s5_ymm"), 1)
                pe.wait_ge(S("s5_gelu"), 2)
                for t in range(2):
                    for h in range(2):
                        for k in range(2):
                            x = mm(BK[:, 1 + 2 * t + h, 0:HT], GLW[:, k, P * t:P * t + P], UIN[:, k, h * HT:h * HT + HT],
                                   k == 0, k == 1)
                    x.then_inc(S("glu_mm"), 1)
                pe.wait_ge(S("y_out0"), CHUNKS)
                pe.wait_ge(S("y_out1"), CHUNKS)
                for m in range(PAIRS):
                    if some(m - 1):
                        pe.wait_ge(S("gn_d"), m - 1)
                    if m == 1:
                        pe.wait_ge(S("glu_sg"), 2)
                    for h in range(2):
                        x = mm(BK[:, (6 if m % 2 == 0 else 4) + h, 0:HT], BONES64[:, :], KK[:, m, h * HT:h * HT + HT])
                    x.then_inc(S("gn_mean"), 1)
                for m in range(PAIRS):
                    pe.wait_ge(S("gn_sq"), m + 1)
                    if some(m - 1):
                        pe.wait_ge(S("gn_ln"), m - 1)
                    for h in range(2):
                        x = mm(BK[:, 2 * (m % 2) + h, 0:HT], BONES64[:, :], AA[:, m, h * HT:h * HT + HT])
                    x.then_inc(S("gn_var"), 1)
                for m in range(PAIRS):
                    pe.wait_ge(S("mx"), m + 1)
                    for h in range(2):
                        x = mm(BK[:, 4 + 2 * (m % 2) + h, 0:HT], G2[:, P * m:P * m + P], RKV[:, 19, h * HT:h * HT + HT])
                    x.then_inc(S("gate_mm"), 1)
                gemm("out0")
            if "ffn0" in stages:
                norm_sums(nn); nn += 1
                gemm("up0")
                gemm("down0")
            if "fox" in stages:
                norm_sums(nn); nn += 1
                pe.wait_ge(S("x_lo"), x_ready["in1"])
                q0 = at["in1"][1]

                def qk_sum(u, b):
                    pe.wait_ge(S("fx_sq"), u + 1)
                    if some(u - 1):
                        pe.wait_ge(S("fx_ln"), u - 1)
                    for h in range(2):
                        x = mm(BK[:, b + h, 0:HT], BONES64[:, :], FSQ[:, (b - 4) // 2, h * HT:h * HT + HT])
                    x.then_inc(S("fx_sum"), 1)

                def projections(i, sums=True):
                    for s in range(2):
                        unit("in1", i, s, q0 + 2 * i + s, s, True, True)
                        if sums:
                            qk_sum(2 * i - 2 + s, 4 + 2 * s)
                projections(0, sums=False)
                pe.wait_ge(S("wf_lo"), 1)
                for h in range(2):
                    n = 0
                    for k in range(KD):
                        for w, x_part in ((WFH, XNH), (WFH, XNL), (WFL, XNH)):
                            x = mm(BK[0:16, 4 + h, 0:HT], w[:, k, :], x_part[:, k, h * HT:h * HT + HT],
                                   n == 0, n == 3 * KD - 1)
                            n += 1
                x.then_inc(S("f_mm"), 1)
                pe.wait_ge(S("f_rd"), 1)
                projections(1)
                with pe.Fori(2, 9) as i:
                    projections(i)
                with pe.Fori(9, 12) as i:
                    projections(i, sums=False)
                pe.wait_ge(S("causal"), 1)
                pe.wait_ge(S("qz"), 2)
                pe.wait_ge(S("ps_free"), q0 + 24)
                pe.wait_ge(S("fx_ln"), 16)

                def scores(i, j):
                    if j == 0:
                        pe.wait_ge(S("fx_k"), i + 1)
                    if some(NQ * i + j - BANKS_BACK[j] + 1):
                        pe.wait_ge(S("fx_ss"), NQ * i + j - BANKS_BACK[j] + 1)
                    b = 2 * SLOT[j]
                    lo, n = TILES[j]
                    w = n - lo
                    m = min(n, 512)
                    c = 0 if j else 512 - w
                    for e in range(2):
                        mm(BK[0:w, b + e, c:c + m], QZ[:, e, lo:n], KS[:, 0:m], True, False)
                        x = mm(BK[0:w, b + e, c + lo:c + m], IDENT[:, 0:w], CM[:, 0:m - lo], False, True)
                    if n > m:
                        pe.wait_ge(S("fx_vs"), i + 1)
                        for e in range(2):
                            mm(BK[0:w, 6 + e, 0:n - m], QZ[:, e, lo:n], KS[:, m:n], True, False)
                            x = mm(BK[0:w, 6 + e, 0:n - m], IDENT[:, 0:w], CM[:, m - lo:w], False, True)
                    x.then_inc(S("fx_s"), 1)

                def turn(i, j):
                    pe.wait_ge(S("fx_d"), NQ * i + j + 1)
                    if some(NQ * i + j):
                        pe.wait_ge(S("fx_pt"), NQ * i + j)
                    if j == 0:
                        own_wait()
                    w = TILES[j][1] - TILES[j][0]
                    c = 0 if j else 512
                    for e in range(2):
                        for k in range(j + 1):
                            k0, k1 = TILES[k]
                            if k:
                                o = BK[:, 4 + e, P * (k - 1):P * k]
                            elif j < NQ - 1:
                                o = BK[0:N_META, 4 + e, 512 - P:512 - P + w]
                            else:
                                o = BK[0:N_META, 6 + e, P:2 * P]
                            x = pe.transpose(o, PR[0:w, SLOT[j], e, c + k0:c + k1], IDENT[0:w, 0:w])
                    x.then_inc(S("fx_t"), 1)

                def values(i):
                    pe.wait_ge(S("fx_vf"), i + 1)
                    if some(i):
                        pe.wait_ge(S("fx_oc"), i)
                    for k, (lo, n) in enumerate(TILES):
                        o = BK[:, 6, P * (k - 1):P * k] if k else BK[0:N_META, 7, 0:P]
                        x = pe.transpose(o, VF[:, lo:n], IDENT[:, :])
                    x.then_inc(S("fx_vt"), 1)

                def mix(i):
                    pe.wait_ge(S("fx_pt"), NQ * i + NQ)
                    for b in range(2):
                        blocks = [k for k in range(NQ) if TILES[k][0] < HT * (b + 1)]
                        for k in blocks:
                            lo = max(TILES[k][0], HT * b)
                            w = TILES[k][1] - TILES[k][0]
                            for e in range(2):
                                h = slice(64 * e, 64 * e + 64)
                                x = mm(BK[h, 6 + b, lo - HT * b:HT], VS[0:w, k, h], PTT[0:w, e, k, lo:HT * (b + 1)],
                                       k == 0, k == blocks[-1])
                    x.then_inc(S("fx_o"), 1)

                def pair(i):
                    last = isinstance(i, int) and i == FOX_PAIRS - 1
                    for j in range(NQ):
                        if j < NQ - 2:
                            scores(i, j + 2)
                        turn(i, j)
                        if j == 0:
                            values(i)
                        if j >= NQ - 2 and not last:
                            scores(i + 1, j - NQ + 2)
                    mix(i)
                scores(0, 0)
                scores(0, 1)
                rounds(pe, FOX_PAIRS, pair, first=True)
                gemm("out1")
            if "ffn1" in stages:
                norm_sums(nn); nn += 1
                gemm("up1")
                gemm("down1")
            if some(n_groups):
                pe.wait_ge(S("ps_free"), n_groups)
            for j in range(4):
                for b in range(2):
                    i = 2 * j + b
                    if some(i - 1):
                        pe.wait_ge(S("o_cp"), i - 1)
                    for k in range(4):
                        t0 = N_META + P * j
                        x = pe.transpose(BK[:, 4 + i % 2, P * k:P * k + P], H[:, 4 * b + k, t0:t0 + P], IDENT[:, :])
                    x.then_inc(S("o_t"), 1)

        @block.scalar
        def _(act):
            def fn(o, i, f, **kw):
                return nc.scalar.activation(o, i, f, **kw)

            def split(g, i, s):
                u0, _, _, k = at[g]
                u = u0 + 2 * i + s
                act.wait_ge(S(f"w_in{s}"), 16 * (u0 // 2 + i + 1))
                if some(u - 1):
                    act.wait_ge(S("w_used"), u - 1)
                fn(WHI[:, s, 0:k, :], RAW[:, s, 0:k, :], ACT.Copy).then_inc(S("w_hi"), 1)

            def norm(n, h_done):
                if some(h_done):
                    act.wait_ge(S("ps_free"), h_done)
                for k in range(KD):
                    if some(KD * n + k - 1):
                        act.wait_ge(S("sq_used"), KD * n + k - 1)
                    fn(SQ[:, k % 2, :], H[:, k, :], ACT.Square).then_inc(S("sq"), 1)
                act.wait_ge(S("sq_used"), KD * n + KD)
                fn(RST[:, :, :], bk(4, 2), ACT.Ln, scale=1.0 / D_MODEL, bias=EPS[:, 0:1]).then_inc(S("rms_ln"), 1)
                act.wait_ge(S("rms_ln"), n + 1)
                fn(RST[:, :, :], RST[:, :, :], ACT.Exp, scale=-0.5).then_inc(S("rms"), 1)
                for k in range(KD):
                    act.wait_ge(S("nt"), KD * n + k + 1)
                    fn(XNH[:, k, :], NT[:, k % 2, :], ACT.Copy).then_inc(S("nt_hi"), 1)

            def gemm(g, evac, late=None):
                n = at[g][2] // 2

                def body(i):
                    last = isinstance(i, int) and i == n - 1
                    split(g, i, 1)
                    if late and some(i):
                        late(i - 1)
                    evac(i, 0)
                    if not last:
                        split(g, i + 1, 0)
                    evac(i, 1)
                rounds(act, n, body, first=late is not None or at[g][0] == 0)
                if late:
                    late(n - 1)

            def nothing(i, s):
                pass

            def up(l):
                g = f"up{l}"
                u0 = at[g][0]
                uc = 2 * KF * l if "ffn0" in stages else 0
                mc = uc // 2

                def evac(i, s):
                    act.wait_ge(S("w_used"), u0 + 2 * i + s + 1)
                    if some(uc + 2 * i + s - 1):
                        act.wait_ge(S("conv"), uc + 2 * i + s - 1)
                    if s == 0:
                        if some(mc + i):
                            act.wait_ge(S("mlp_mul"), mc + i)
                    src = bk(2 * s, 2)
                    fn(halves(CP[:, s, 2:T + 2]), src, ACT.Copy).then_inc(S("cp"), 1)
                    col = PC_CONV + CONV_COLS * l + KF * s + i
                    fn(halves(CA[:, s, :]), src, ACT.Identity, scale=PRM[:, ds(col + 4 * KF, 1)],
                       bias=PRM[:, ds(col + 6 * KF, 1)]).then_inc(S("ps_free"), 1)

                def late(i):
                    act.wait_ge(S("conv"), uc + 2 * i + 1)
                    fn(SG[:, :], CA[:, 0, :], ACT.Silu).then_inc(S("silu"), 1)
                    act.wait_ge(S("mlp_mul"), mc + i + 1)
                    fn(GH[:, ds(i, 1), :], GT[:, :].unsqueeze(1), ACT.Copy).then_inc(S("mlp_hi"), 1)
                gemm(g, evac, late)

            act.wait_ge(S("prm_t"), 1)
            act.wait_ge(S("x_t"), 1)
            for i in range(1, 10, 2):
                j, b = divmod(i, 2)
                n, t0 = (N_META, 0) if j == 0 else (P, N_META + P * (j - 1))
                act.wait_ge(S("x_t"), i + 1)
                act.wait_ge(S("x_cp"), i)
                fn(H[:, 4 * b:4 * b + 4, t0:t0 + n], BK[:, 3, :].rearrange("p (k t) -> p k t", k=4)[:, :, 0:n],
                   ACT.Copy).then_inc(S("x_cp"), 1)
            act.wait_ge(S("x_cp"), 10)
            act.wait_ge(S("consts"), 1)
            nn = 0
            if "mix0" in stages:
                v = lambda i: S5V[:, i, :]
                act.wait_ge(S("s5_ldt"), 1)
                fn(v(0), v(0), ACT.Exp).then_inc(S("s5_dt"), 1)
                act.wait_ge(S("s5_ph"), 1)
                fn(MAG[:, :], v(1), ACT.Exp).then_inc(S("s5_mag"), 1)
                fn(v(4), v(4), ACT.Sin).then_inc(S("s5_mag"), 1)
                fn(v(5), v(5), ACT.Sin).then_inc(S("s5_mag"), 1)
                split("in0", 0, 0)
                norm(nn, 0); nn += 1

                def evac(i, s):
                    u = 2 * i + s
                    act.wait_ge(S("w_used"), u + 1)
                    if some(u - 1):
                        act.wait_ge(S("shift"), u - 1)
                    fn(halves(PB[:, s, 1:T + 1]), bk(2 * s, 2), ACT.Copy).then_inc(S("ps_free"), 1)

                def body(i):
                    split("in0", i, 1)
                    evac(i, 0)
                    split("in0", i + 1, 0)
                    evac(i, 1)
                act.wait_ge(S("pb0"), 1)
                body(0)
                with act.Fori(1, 10) as i:
                    body(i)
                split("in0", 10, 1)
                for s in range(2):
                    act.wait_ge(S("w_used"), 21 + s)
                    if s == 0:
                        act.wait_ge(S("shift"), 20)
                    fn(halves(UIN[:, s, :]), bk(2 * s, 2), ACT.Copy).then_inc(S("ps_free"), 1)
                for n in range(16):
                    j, i = divmod(n, 2)
                    act.wait_ge(S("s5_bum"), n + 1)
                    fn(halves(U[:, i, j, :]), bk(4 + 2 * (n % 2), 2), ACT.Copy).then_inc(S("s5_ucp"), 1)
                    if n == 0:
                        act.wait_ge(S("shift"), 20)
                        fn(RKV[0:LORA, 18, 0:T], RKV[0:LORA, 18, 0:T], ACT.Tanh).then_inc(S("lora_act"), 1)
                        fn(RKV[:, 19, 0:T], RKV[:, 19, 0:T], ACT.Sigmoid).then_inc(S("g_act"), 1)
                act.wait_ge(S("s5_ucp"), 16)
                for n in range(2 * PAIRS):
                    m, i = divmod(n, 2)
                    act.wait_ge(S("lora_mm"), n + 1)
                    fn(halves((AA if i else SIG)[:, m, 0:T]), bk(2 * (n % 2), 2), ACT.Sigmoid,
                       bias=PRM[:, (PC_A0 if i else PC_W0) + m:(PC_A0 if i else PC_W0) + m + 1]).then_inc(S("lora_cp"), 1)
                for m in range(PAIRS):
                    act.wait_ge(S("kk_raw"), m + 1)
                    fn(CS[:, m, 0:T], KK[:, m, 0:T], ACT.Square).then_inc(S("kk_sq"), 1)
                act.wait_ge(S("kk_max"), PAIRS)
                pp = PP[:, :, :, :].rearrange("p a b c -> p (a b c)")[:, 0:PAIRS * T].rearrange("p (m t) -> p m t", t=T)
                fn(pp, pp, ACT.Ln, scale=LN_SHIFT).then_inc(S("kk_ln"), 1)
                act.wait_ge(S("kk_ln"), 1)
                fn(pp, pp, ACT.Exp, scale=-0.5, bias=EPS[:, 2:3]).then_inc(S("kk_rn"), 1)
                act.wait_ge(S("cs"), PAIRS)
                act.wait_ge(S("kkn"), 1)
                act.wait_ge(S("pads"), 4)
                csv = CS[:, :, :].rearrange("p m (c t) -> p m c t", t=C)
                for m in range(PAIRS):
                    fn(PP[:, m, :, 1:C + 1], csv[:, m], ACT.Exp, scale=-DECAY).then_inc(S("dec"), 1)
                act.wait_ge(S("dec"), PAIRS)
                fn(CS[:, :, :], CS[:, :, :], ACT.Exp, scale=DECAY).then_inc(S("pinv"), 1)

                def chunk(c):
                    if some(PAIRS * c):
                        act.wait_ge(S("ph"), PAIRS * c)
                    fn(VH[:, :, :], RKV[:, 2 * PAIRS:3 * PAIRS, ds(c * C, C)], ACT.Copy).then_inc(S("v_stage"), 1)
                    for p in range(PAIRS):
                        act.wait_ge(S("ph_dve"), PAIRS * c + p + 1)
                        ph = BK[:, p % 2, :]
                        fn(BKT[:, p, :, :], ph[:, 0:384].rearrange("p (a b t) -> p a b t", a=2, b=3)[:, :, 2, :],
                           ACT.Copy).then_inc(S("bk_cp"), 1)
                        fn(VT[:, p, :], ph[:, 448:512], ACT.Copy).then_inc(S("ph_out"), 1)
                    for g in range(2):
                        q = slice(G3 * g, G3 * g + G3)
                        act.wait_ge(S(f"g_mm{g}"), c + 1)
                        fn(NG[:, q, :], BK[:, 2 + 3 * g, 0:G3 * C].rearrange("p (q t) -> p q t", t=C), ACT.Copy,
                           scale=-1.0).then_inc(S(f"g_cp{g}"), 1)
                    for g in range(2):
                        q = slice(G3 * g, G3 * g + G3)
                        act.wait_ge(S(f"sa_mm{g}"), c + 1)
                        fn(SA[:, q, :], BK[:, 3 + 3 * g, 0:G3 * C].rearrange("p (q t) -> p q t", t=C),
                           ACT.Copy).then_inc(S(f"sa_cp{g}"), 1)
                    for g in range(2):
                        q = slice(G3 * g, G3 * g + G3)
                        act.wait_ge(S(f"y_mm{g}"), c + 1)
                        fn(KK[:, q, ds(c * C, C)], BK[:, 4 + 3 * g, 0:G3 * C].rearrange("p (q t) -> p q t", t=C),
                           ACT.Copy).then_inc(S(f"y_out{g}"), 1)
                act.wait_ge(S("tilde"), 1)
                rounds(act, CHUNKS, chunk, first=True, last=False)

                for t in range(2):
                    act.wait_ge(S("s5_y"), t + 1)
                    fn(UIN[:, t, :], UIN[:, t, :], ACT.Gelu_apprx_tanh).then_inc(S("s5_gelu"), 1)
                for t in range(2):
                    act.wait_ge(S("glu_mm"), t + 1)
                    fn(halves(PT2[:, t, :]), bk(1 + 2 * t, 2), ACT.Sigmoid, bias=PRM[:, PC_GLB + t:PC_GLB + t + 1])\
                        .then_inc(S("glu_sg"), 1)
                def mixed(k):
                    act.wait_ge(S("mx"), k + 1)
                    fn(XNH[:, MIXED[k], :], PT2[:, k % 2, :], ACT.Copy).then_inc(S("mx_hi"), 1)
                for k in range(2):
                    mixed(k)
                for m in range(PAIRS):
                    act.wait_ge(S("gn_d"), m + 1)
                    fn(AA[:, m, 0:T], KK[:, m, 0:T], ACT.Square).then_inc(S("gn_sq"), 1)
                for m in range(PAIRS):
                    act.wait_ge(S("gn_var"), m + 1)
                    fn(halves(RS6[:, m, :]), bk(2 * (m % 2), 2), ACT.Ln, bias=EPS[:, 1:2]).then_inc(S("gn_ln"), 1)
                act.wait_ge(S("gn_ln"), PAIRS)
                fn(RS6[:, :, :], RS6[:, :, :], ACT.Exp, scale=-0.5).then_inc(S("gn_rs"), 1)
                for k in range(2, KD):
                    mixed(k)
                split("out0", 0, 0)
                gemm("out0", nothing)
            if "ffn0" in stages:
                split("up0", 0, 0)
                norm(nn, h_ready.get("out0", 0)); nn += 1
                up(0)
                split("down0", 0, 0)
                gemm("down0", nothing)
            if "fox" in stages:
                split("in1", 0, 0)
                norm(nn, h_ready.get("down0", 0)); nn += 1
                u0 = at["in1"][0]

                def evac(i, s):
                    act.wait_ge(S("w_used"), u0 + 2 * i + s + 1)
                    fn(QKV[:, ds(2 * i + s, 1), :].rearrange("p o (a b) -> p (o a) b", a=2), bk(2 * s, 2), ACT.Copy)\
                        .then_inc(S("ps_free"), 1)

                def own_wait():
                    act.sem_inc(S("act_turn"), 1)

                def inverse_rms(i):
                    for s in range(2):
                        act.wait_ge(S("fx_sum"), 2 * i + s + 1)
                        fn(FRS[:, ds(2 * i + s, 1), :].rearrange("p o (a b) -> p (o a) b", a=2), bk(4 + 2 * s, 2),
                           ACT.Ln, bias=EPS[:, 0:1]).then_inc(S("fx_ln"), 1)
                    act.wait_ge(S("fx_ln"), 2 * i + 2)
                    own_wait()
                    fn(FRS[:, ds(2 * i, 2), :], FRS[:, ds(2 * i, 2), :], ACT.Exp, scale=-0.5).then_inc(S("fx_rs"), 1)

                def body(i, squares=True, sums=True, more=True):
                    for s in range(2):
                        u = 2 * i + s
                        if s == 0:
                            split("in1", i, 1)
                            if sums:
                                inverse_rms(i - 2)
                        elif more:
                            split("in1", i + 1, 0)
                        evac(i, s)
                        if squares:
                            act.wait_ge(S("ps_free"), at["in1"][1] + u + 1)
                            if some(u - 1):
                                act.wait_ge(S("fx_sum"), u - 1)
                            own_wait()
                            fn(FSQ[:, s:s + 1, :], QKV[:, ds(u, 1), :], ACT.Square).then_inc(S("fx_sq"), 1)
                act.wait_ge(S("wf_in"), 32)
                fn(WFH[:, :, :], WF[:, :, :], ACT.Copy).then_inc(S("wf_hi"), 1)
                body(0, sums=False)
                body(1, sums=False)
                act.wait_ge(S("f_abs"), 1)
                fn(CUM[0:16, 1, :], CUM[0:16, 1, :], ACT.Exp, scale=-1.0).then_inc(S("f_exp"), 1)
                act.wait_ge(S("f_exp"), 1)
                fn(CUM[0:16, 1, :], CUM[0:16, 1, :], ACT.Ln, bias=ONES[0:16, 0:1]).then_inc(S("f_act"), 1)
                with act.Fori(2, 8) as i:
                    body(i)
                for i in (8, 9):
                    body(i, squares=False)
                body(10, squares=False, sums=False)
                body(11, squares=False, sums=False, more=False)

                def exps(i, j):
                    lo, n = TILES[j]
                    w = n - lo
                    c = 0 if j else 512
                    act.wait_ge(S("fx_mx"), NQ * i + j + 1)
                    if some(NQ * i + j - COLS_BACK[j] + 1):
                        act.wait_ge(S("fx_t"), NQ * i + j - COLS_BACK[j] + 1)
                    for e in range(2):
                        x = fn(PR[0:w, SLOT[j], e, c:c + n], SS[0:w, SLOT[j], e, c:c + n], ACT.Exp,
                               bias=MX[0:w, j, e:e + 1], accum_out=SM[0:w, j, e:e + 1])
                    x.then_inc(S("fx_e"), 1)

                def out_pt(i, j):
                    act.wait_ge(S("fx_t"), NQ * i + j + 1)
                    lo, n = TILES[j]
                    w = n - lo
                    if j == 0 and some(i):
                        act.wait_ge(S("fx_o"), i)
                    if j:
                        fn(PTT[:, :, 1:j + 1, lo:n], BK[:, 4:6, 0:P * j].rearrange("p e (k t) -> p e k t", t=P), ACT.Copy)
                    meta = BK[0:N_META, 4:6, 512 - P:512 - P + w] if j < NQ - 1 else BK[0:N_META, 6:8, P:2 * P]
                    fn(PTT[0:N_META, :, 0, lo:n], meta, ACT.Copy).then_inc(S("fx_pt"), 1)

                def out(i):
                    act.wait_ge(S("fx_o"), i + 1)
                    if some(i):
                        act.wait_ge(S("x_lo"), x_ready["out1"] - KD + i)
                    fn(halves(OT[:, :]), bk(6, 2), ACT.Copy).then_inc(S("fx_oc"), 1)
                    act.wait_ge(S("fx_oc"), i + 1)
                    fn(XNH[:, ds(i, 1), :], OT[:, :].unsqueeze(1), ACT.Copy).then_inc(S("ot_hi"), 1)

                def pair(i):
                    last = isinstance(i, int) and i == FOX_PAIRS - 1
                    for j in range(NQ):
                        if j < NQ - 1:
                            exps(i, j + 1)
                        elif not last:
                            exps(i + 1, 0)
                        if j == 0 and some(i):
                            out(i - 1)
                        out_pt(i, j)
                        if j == 0:
                            act.wait_ge(S("fx_vt"), i + 1)
                            fn(VS[:, 1:NQ, :], BK[:, 6, :].rearrange("p (k t) -> p k t", t=P), ACT.Copy)
                            fn(VS[0:N_META, 0, :], BK[0:N_META, 7, 0:P], ACT.Copy).then_inc(S("fx_vs"), 1)
                exps(0, 0)
                rounds(act, FOX_PAIRS, pair, first=True)
                out(FOX_PAIRS - 1)
                split("out1", 0, 0)
                gemm("out1", nothing)
            if "ffn1" in stages:
                split("up1", 0, 0)
                norm(nn, h_ready.get("out1", 0)); nn += 1
                up(1)
                split("down1", 0, 0)
                gemm("down1", nothing)
            for i in range(1, 8, 2):
                act.wait_ge(S("o_t"), i + 1)
                act.wait_ge(S("o_cp"), i)
                fn(OUTB[:, i // 2, 512:1024], BK[:, 5, :], ACT.Copy).then_inc(S("o_cp"), 1)

        @block.vector
        def _(ve):
            od = Order(ve, "ve_order")

            def step(ins):
                od.done(ins)
                od.settle()

            def tt(o, x, y, op):
                return nc.vector.tensor_tensor(o, x, y, op)

            def ts(o, x, s1, s2, op0, op1=None):
                return nc.vector.tensor_scalar(o, x, s1, s2, op0, op1) if op1 is not None else \
                    nc.vector.tensor_scalar(o, x, s1, s2, op0)

            def stt(o, x, s, y, op0, op1):
                return nc.vector.scalar_tensor_tensor(out=o, in0=x, scalar=s, in1=y, op0=op0, op1=op1)

            def f32(ap):
                return ap.bitcast(F32)

            def split(g, i, s):
                u0, _, _, k = at[g]
                ve.wait_ge(S("w_hi"), u0 + 2 * i + s + 1)
                tt(WLO[:, s, 0:k, :], RAW[:, s, 0:k, :], f32(WHI[:, s, 0:k, :]), ALU.subtract).then_inc(S("w_lo"), 1)

            def norm(n, g, col):
                x0 = x_ready[g] - KD
                ve.wait_ge(S("rms"), n + 1)

                def scaled(k):
                    if some(KD * n + k - 1):
                        ve.wait_ge(S("nt_hi"), KD * n + k - 1)
                    if some(x0 + k - 1):
                        ve.wait_ge(S("x_lo"), x0 + k - 1)
                    stt(NT[:, k % 2, :], H[:, k, :], PRM[:, col + k:col + k + 1], RST[:, :, :].rearrange("p a b -> p (a b)"),
                        ALU.mult, ALU.mult).then_inc(S("nt"), 1)
                scaled(0)
                for k in range(KD):
                    if k + 1 < KD:
                        scaled(k + 1)
                    ve.wait_ge(S("nt_hi"), KD * n + k + 1)
                    tt(XNL[:, k, :], NT[:, k % 2, :], f32(XNH[:, k, :]), ALU.subtract).then_inc(S("x_lo"), 1)

            def gemm(g, use, late=None):
                n = at[g][2] // 2

                def body(i):
                    last = isinstance(i, int) and i == n - 1
                    split(g, i, 1)
                    if late and some(i):
                        late(i - 1)
                    use(i, 0)
                    if not last:
                        split(g, i + 1, 0)
                    use(i, 1)
                rounds(ve, n, body, first=late is not None or at[g][0] == 0)
                if late:
                    late(n - 1)

            def residual(g):
                u0, _, units, _ = at[g]
                h0 = h_ready[g] - KD
                if g.startswith("down"):
                    def body(ii, last=False):
                        for r in range(2):
                            i = 2 * ii + r
                            split(g, i, 1)
                            if not (last and r == 1):
                                split(g, i + 1, 0)
                            ve.wait_ge(S("w_used"), u0 + 2 * i + 2)
                            hm = H[:, ds(i, 1), :].rearrange("p o (a b) -> p (o a) b", a=2)
                            tt(hm, hm, bk(2 * r, 2), ALU.add).then_inc(S("ps_free"), 1)
                    with ve.Fori(0, 3) as ii:
                        body(ii)
                    body(3, True)
                else:
                    def use(i, s):
                        ve.wait_ge(S("w_used"), u0 + 2 * i + s + 1)
                        hm = H[:, ds(2 * i + s, 1), :].rearrange("p o (a b) -> p (o a) b", a=2)
                        tt(hm, hm, bk(2 * s, 2), ALU.add).then_inc(S("ps_free"), 1)
                    gemm(g, use)

            def up(l):
                g = f"up{l}"
                u0 = at[g][0]
                uc = 2 * KF * l if "ffn0" in stages else 0
                mc = uc // 2
                x0 = x_ready[f"down{l}"] - KF
                ve.wait_ge(S("x_lo"), x_ready[g])
                ve.memset(CP[:, :, 0:2], 0.0).then_inc(S("cp0"), 1)
                ve.wait_ge(S("cp0"), l + 1 if "ffn0" in stages else 1)

                def use(i, s):
                    n = uc + 2 * i + s
                    q = at[g][1] + 2 * i + s
                    ve.wait_ge(S("ps_free"), q + 1)
                    col = PC_CONV + CONV_COLS * l + KF * s + i
                    stt(CA[:, s, :], CP[:, s, 1:T + 1], PRM[:, ds(col + 2 * KF, 1)], CA[:, s, :], ALU.mult, ALU.add)\
                        .then_inc(S("conv_a"), 1)
                    ve.wait_ge(S("conv_a"), n + 1)
                    stt(CA[:, s, :], CP[:, s, 0:T], PRM[:, ds(col, 1)], CA[:, s, :], ALU.mult, ALU.add)\
                        .then_inc(S("conv"), 1)

                def late(i):
                    ve.wait_ge(S("silu"), mc + i + 1)
                    ve.wait_ge(S("conv"), uc + 2 * i + 2)
                    ve.wait_ge(S("x_lo"), x0 + i)
                    tt(GT[:, :], SG[:, :], CA[:, 1, :], ALU.mult).then_inc(S("mlp_mul"), 1)
                    ve.wait_ge(S("mlp_hi"), mc + i + 1)
                    gm = GH[:, ds(i, 1), :]
                    tt(GL[:, ds(i, 1), :], GT[:, :].unsqueeze(1), f32(gm), ALU.subtract).then_inc(S("x_lo"), 1)
                gemm(g, use, late)

            ve.wait_ge(S("prm_in"), 16 * (N_PRM_LOADS + 1))
            ve.tensor_copy(PRAW[0:8, 5, :].rearrange("p (g n) -> p g n", g=2),
                           S5V[0:8, 15, 0:2].unsqueeze(2).to_broadcast([8, 2, 64])).then_inc(S("ldt"), 1)
            ve.wait_ge(S("prm_t"), 1)
            col = 0
            for t, n in enumerate((114, 88, 88, 88, 88)):
                od.done(ve.tensor_copy(PRM[:, col:col + n], BK[:, t // 4, P * (t % 4):P * (t % 4) + n]))
                col += n
            ve.tensor_copy(S5V[:, 0, :], BK[:, 1, P:P + 8]).then_inc(S("s5_ldt"), 1)
            for i in range(0, 10, 2):
                j, b = divmod(i, 2)
                n, t0 = (N_META, 0) if j == 0 else (P, N_META + P * (j - 1))
                ve.wait_ge(S("x_t"), i + 1)
                if some(i):
                    ve.wait_ge(S("x_cp"), i)
                ve.tensor_copy(H[:, 4 * b:4 * b + 4, t0:t0 + n], BK[:, 2, :].rearrange("p (k t) -> p k t", k=4)[:, :, 0:n])\
                    .then_inc(S("x_cp"), 1)
            od.settle()
            ve.wait_ge(S("s5_ldt"), 1)
            ve.wait_ge(S("x_cp"), 10)
            ve.wait_ge(S("consts"), 1)
            nn = 0
            if "mix0" in stages:
                v = lambda i: S5V[:, i, :]
                are, aim = PRM[:, PC_ARE:PC_ARE + 8], PRM[:, PC_AIM:PC_AIM + 8]
                ve.wait_ge(S("s5_dt"), 1)
                step(tt(v(1), are, v(0), ALU.mult))
                step(tt(v(2), aim, v(0), ALU.mult))
                big = 1.5 * 2.0 ** 23
                turn = 2 * math.pi
                c1 = 6.28125
                c2 = float.fromhex("0x1.fb4p-10")
                c3 = turn - c1 - c2
                for dst, quarter in ((4, 0.0), (5, 0.25)):
                    step(ts(v(3), v(2), 1.0 / turn, quarter, ALU.mult, ALU.add))
                    step(ts(v(3), v(3), big, None, ALU.add))
                    step(ts(v(3), v(3), big, None, ALU.subtract))
                    step(stt(v(dst), v(3), -c1, v(2), ALU.mult, ALU.add))
                    step(stt(v(dst), v(3), -c2, v(dst), ALU.mult, ALU.add))
                    step(stt(v(dst), v(3), -c3, v(dst), ALU.mult, ALU.add))
                    step(ts(v(dst), v(dst), quarter * turn, None, ALU.add))
                    x = ts(v(dst), v(dst), 3.1415925, -3.1415925, ALU.min, ALU.max)
                    if quarter:
                        x.then_inc(S("s5_ph"), 1)
                    else:
                        step(x)
                ve.wait_ge(S("s5_mag"), 3)
                cs, sn = v(5), v(4)
                step(tt(v(6), MAG[:, :], cs, ALU.mult))
                step(tt(v(7), MAG[:, :], sn, ALU.mult))
                step(ts(v(6), v(6), 1.0, None, ALU.subtract))
                step(tt(v(8), are, are, ALU.mult))
                step(tt(v(9), aim, aim, ALU.mult))
                step(tt(v(8), v(8), v(9), ALU.add))
                step(nc.vector.reciprocal(v(8), v(8)))
                step(tt(v(9), v(6), are, ALU.mult))
                step(tt(v(10), v(7), aim, ALU.mult))
                step(tt(v(9), v(9), v(10), ALU.add))
                step(tt(v(9), v(9), v(8), ALU.mult))
                step(tt(v(10), v(7), are, ALU.mult))
                step(tt(v(11), v(6), aim, ALU.mult))
                step(tt(v(10), v(10), v(11), ALU.subtract))
                step(tt(v(10), v(10), v(8), ALU.mult))
                step(ve.tensor_copy(POW[:, :, 0, 0], cs))
                step(ve.tensor_copy(POW[:, :, 0, 1], sn))
                for n in range(9):
                    step(tt(v(12), POW[:, :, n, 0], POW[:, :, n, 0], ALU.mult))
                    step(tt(v(13), POW[:, :, n, 1], POW[:, :, n, 1], ALU.mult))
                    step(tt(POW[:, :, n + 1, 0], v(12), v(13), ALU.subtract))
                    x = stt(POW[:, :, n + 1, 1], POW[:, :, n, 0], 2.0, POW[:, :, n, 1], ALU.mult, ALU.mult)
                    if n < 8:
                        step(x)
                x.then_inc(S("s5_pow"), 1)
                ve.wait_ge(S("b_in"), 32)
                zr = v(9).unsqueeze(2).to_broadcast([P, 8, 16])
                zi = v(10).unsqueeze(2).to_broadcast([P, 8, 16])
                t1 = BBM[:, 0, 0, :].rearrange("p (j c) -> p j c", c=16)
                step(tt(BB[:, 0], BR[:, 0], zr, ALU.mult))
                step(tt(t1, BR[:, 1], zi, ALU.mult))
                step(tt(BB[:, 0], BB[:, 0], t1, ALU.subtract))
                step(tt(BB[:, 1], BR[:, 1], zr, ALU.mult))
                step(tt(t1, BR[:, 0], zi, ALU.mult))
                step(tt(BB[:, 1], BB[:, 1], t1, ALU.add))
                ve.wait_ge(S("mk"), 8)
                for i in range(2):
                    for j in range(8):
                        x = tt(BBM[:, i, j, :].rearrange("p (s c) -> p s c", c=16),
                               BB[:, i, j, :].unsqueeze(1).to_broadcast([P, 8, 16]),
                               MK[:, j % 4, :].rearrange("p (s c) -> p s c", c=16), ALU.mult)
                x.then_inc(S("bbm"), 1)
                for n in range(4):
                    i, jh = divmod(n, 2)
                    ve.wait_ge(S("wb_t"), n + 1)
                    ve.tensor_copy(WB[:, i, 4 * jh:4 * jh + 4, :], BK[:, 6 + n % 2, :].rearrange("p (j c) -> p j c", j=4))\
                        .then_inc(S("wb_cp"), 1)
                ve.memset(PB[:, :, 0:1], 0.0).then_inc(S("pb0"), 1)
                split("in0", 0, 0)
                norm(nn, "in0", PC_MIX); nn += 1
                ve.wait_ge(S("pb0"), 1)

                def use(i, s):
                    u = 2 * i + s
                    ve.wait_ge(S("ps_free"), u + 1)
                    tt(DT[:, s, :], PB[:, s, 0:T], PB[:, s, 1:T + 1], ALU.subtract).then_inc(S("diff"), 1)
                    ve.wait_ge(S("diff"), u + 1)
                    stt(RKV[:, ds(u, 1), 0:T], DT[:, s, :].unsqueeze(1), PRM[:, ds(PC_MU + u, 1)],
                        PB[:, s, 1:T + 1].unsqueeze(1), ALU.mult, ALU.add).then_inc(S("shift"), 1)

                def body(i):
                    split("in0", i, 1)
                    use(i, 0)
                    split("in0", i + 1, 0)
                    use(i, 1)
                body(0)
                with ve.Fori(1, 10) as i:
                    body(i)
                split("in0", 10, 1)
                ve.wait_ge(S("shift"), 20)
                for m in range(PAIRS):
                    ts(KK[:, m, 0:T], RKV[:, PAIRS + m, 0:T], PRM[:, PC_KK + m:PC_KK + m + 1], None, ALU.mult)\
                        .then_inc(S("kk_raw"), 1)
                pp = PP[:, :, :, :].rearrange("p a b c -> p (a b c)")[:, 0:PAIRS * T].rearrange("p (m t) -> p m t", t=T)
                for m in range(PAIRS):
                    ve.wait_ge(S("kk_sum"), m + 1)
                    if m == 0:
                        ve.wait_ge(S("pads"), 4)
                    ts(pp[:, m, :].rearrange("p (a b) -> p a b", a=2), bk(4 + 2 * (m % 2), 2), 1e-24, None, ALU.max)\
                        .then_inc(S("kk_max"), 1)
                ve.wait_ge(S("kk_rn"), 1)
                ve.wait_ge(S("kk_raw"), PAIRS)
                tt(KK[:, :, 0:T], KK[:, :, 0:T], pp, ALU.mult).then_inc(S("kkn0"), 1)
                ve.wait_ge(S("kkn0"), 1)
                ve.memset(PP[:, :, :, 0:1], 1.0).then_inc(S("kkn"), 1)
                ve.wait_ge(S("reset"), 1)
                ve.wait_ge(S("lora_cp"), 2 * PAIRS)
                for m in range(PAIRS):
                    nc.vector.tensor_tensor_scan(CS[:, m, :], RESET[:, :], SIG[:, m, :], 0.0, ALU.mult, ALU.add)\
                        .then_inc(S("cs"), 1)
                ve.wait_ge(S("cs"), PAIRS)
                om = FT1[:, 0:PAIRS]
                ve.wait_ge(S("masks"), 5)
                step(ts(om, PRM[:, PC_KA:PC_KA + PAIRS], -1.0, 1.0, ALU.mult, ALU.add))
                for m in range(PAIRS):
                    od.done(ts(SIG[:, m, 0:T], AA[:, m, 0:T], PRM[:, PC_KA + m:PC_KA + m + 1], FT1[:, m:m + 1],
                               ALU.mult, ALU.add))
                od.settle()
                step(tt(RKV[:, PAIRS:2 * PAIRS, 0:T], RKV[:, PAIRS:2 * PAIRS, 0:T], SIG[:, :, 0:T], ALU.mult))
                step(tt(AA[:, :, 0:T], AA[:, :, 0:T], KK[:, :, 0:T], ALU.mult))
                for m in range(PAIRS):
                    stt(SIG[:, m, 0:T], RKV[:, m, 0:T], PRM[:, PC_RK + m:PC_RK + m + 1], RKV[:, PAIRS + m, 0:T],
                        ALU.mult, ALU.mult).then_inc(S("rk"), 1)
                for m in range(PAIRS):
                    ve.wait_ge(S("bonus_mm"), m + 1)
                    tt(halves(SIG[:, m, 0:T]), bk(2 * (m % 2), 2), halves(RKV[:, 2 * PAIRS + m, 0:T]), ALU.mult)\
                        .then_inc(S("bonus"), 1)
                ve.wait_ge(S("pinv"), 1)
                ve.wait_ge(S("kkn"), 1)
                ch = lambda ap: ap.rearrange("p m (c t) -> p m c t", t=C)
                for m in range(PAIRS):
                    r, k = RKV[:, m, :], RKV[:, PAIRS + m, :]
                    c4 = lambda ap: ap.rearrange("p (c t) -> p c t", t=C)
                    od.done(tt(c4(KK[:, m, :]), c4(KK[:, m, :]), PP[:, m, :, 0:C], ALU.mult))
                    od.done(tt(c4(r), c4(r), PP[:, m, :, 1:C + 1], ALU.mult))
                    od.done(tt(AA[:, m, :], AA[:, m, :], CS[:, m, :], ALU.mult))
                    od.done(tt(k, k, CS[:, m, :], ALU.mult))
                od.settle()
                ve.tensor_copy(PCH[:, :, :], PP[:, :, :, C]).then_inc(S("tilde"), 1)

                ve.wait_ge(S("tilde"), 1)
                o0 = od.at
                PER = 3 * PAIRS + 2 + 2

                def chunk(c, s5):
                    od.at = o0 + PER * c
                    for g in range(2):
                        if some(c):
                            ve.wait_ge(S(f"y_mm{g}"), c)
                        q = slice(G3 * g, G3 * g + G3)
                        t = ds(c * C, C)
                        ve.tensor_copy(KR[:, q, 0, :], KK[:, q, t])
                        ve.tensor_copy(KR[:, q, 1, :], RKV[:, q, t])
                        ve.tensor_copy(BH[:, q, :], AA[:, q, t])
                        ve.tensor_copy(KH[:, q, :], RKV[:, PAIRS + G3 * g:PAIRS + G3 * g + G3, t])\
                            .then_inc(S(f"stage{g}"), 1)
                    if isinstance(c, int) and c == 0:
                        ve.wait_ge(S("chunk_init"), 2 * PAIRS)
                    for p in range(PAIRS):
                        ve.wait_ge(S("ph"), PAIRS * c + p + 1)
                        ph = BK[:, p % 2, :]
                        two = lambda ap: ap.unsqueeze(1).to_broadcast([P, 2, C])
                        m2 = lambda t: t[:, :].rearrange("p (e t) -> p e t", e=2)
                        od.done(tt(AT[:, p], two(ph[:, 0:64]), m2(MU2), ALU.mult))
                        od.done(tt(XT[:, p], two(ph[:, 0:64]), m2(M1T), ALU.mult))
                        od.done(tt(XX[:, p], two(ph[:, 384:448]), m2(M1), ALU.mult))
                        tt(MQA[:, p], ph[:, 0:384].rearrange("p (a b t) -> p a b t", a=2, b=3)[:, :, 0:2, :],
                           MQ[:, :, :].unsqueeze(1).to_broadcast([P, 2, 2, C]), ALU.mult).then_inc(S("ph_dve"), 1)
                        if p % G3 == G3 - 1:
                            g = p // G3
                            q = slice(G3 * g, G3 * g + G3)
                            od.settle()
                            fl = lambda t: t[:, q].rearrange("p q e t -> p q (e t)")
                            idb = IDENT[:, :].unsqueeze(1).to_broadcast([P, G3, P])
                            od.done(tt(fl(XT), fl(XT), idb, ALU.add))
                            tt(fl(XX), fl(XX), idb, ALU.add).then_inc(S(f"x_up{g}"), 1)
                    for n in range(5):
                        for g in range(2):
                            q = slice(G3 * g, G3 * g + G3)
                            fl = lambda t: t[:, q].rearrange("p q e t -> p q (e t)")
                            pq = lambda b: BK[:, b + 3 * g, 0:G3 * P].rearrange("p (q t) -> p q t", t=P)
                            ve.wait_ge(S(f"t_mm{g}"), 5 * c + n + 1)
                            tt(fl(TM), pq(2), LVL[:, n, :].unsqueeze(1).to_broadcast([P, G3, P]), ALU.mult)\
                                .then_inc(S(f"t_mask{g}"), 1)
                        for g in range(2):
                            q = slice(G3 * g, G3 * g + G3)
                            fl = lambda t: t[:, q].rearrange("p q e t -> p q (e t)")
                            pq = lambda b: BK[:, b + 3 * g, 0:G3 * P].rearrange("p (q t) -> p q t", t=P)
                            ve.wait_ge(S(f"x_mm{g}"), 5 * c + n + 1)
                            if n < 4:
                                tt(fl(XX), fl(XX), pq(3), ALU.subtract)
                            tt(fl(XT), fl(XT), pq(4), ALU.subtract).then_inc(S(f"x_up{g}"), 1)
                    if s5:
                        ve.wait_ge(S("s5_in"), 2 * c + 2)
                        for i in range(2):
                            u = U[:, i, ds(c, 1), :].rearrange("p a t -> p (a t)")
                            nc.vector.tensor_tensor_scan(u, MAG[:, ds(c, 1)].to_broadcast([P, T]), u, 0.0,
                                                         ALU.mult, ALU.add).then_inc(S("s5_scan"), 1)
                    for g in range(2):
                        q = slice(G3 * g, G3 * g + G3)
                        ve.wait_ge(S(f"y_mm{g}"), c + 1)
                        od.done(tt(SS0[:, q, :], SS0[:, q, :],
                                   BK[:, 2 + 3 * g, 0:G3 * C].rearrange("p (q t) -> p q t", t=C), ALU.add))
                        od.settle()
                        tt(SS0[:, q, :], SS0[:, q, :], PCH[:, q, ds(c, 1)].to_broadcast([P, G3, C]), ALU.mult)\
                            .then_inc(S(f"state{g}"), 1)
                chunk(0, True)
                assert od.at == o0 + PER, (od.at, o0, PER)
                with ve.Fori(1, N_STATE_TILES) as c:
                    chunk(c, True)
                chunk(CHUNKS - 1, False)
                od.at = o0 + PER * CHUNKS
                for g in range(2):
                    ve.wait_ge(S(f"y_out{g}"), CHUNKS)
                    ve.wait_ge(S(f"state{g}"), CHUNKS)

                ve.wait_ge(S("c_t"), 1)
                ve.wait_ge(S("mk2"), 8)
                for i in range(2):
                    for t in range(2):
                        x = stt(WC[:, i, 4 * t:4 * t + 4, :],
                                BK[:, 0, P * (2 * i + t):P * (2 * i + t) + P].unsqueeze(1).to_broadcast([P, 4, P]),
                                -1.0 if i else 1.0, MK2[:, :, :], ALU.mult, ALU.mult)
                    x.then_inc(S("wc"), 1)
                for t in range(2):
                    ve.wait_ge(S("s5_ymm"), t + 1)
                    stt(halves(UIN[:, t, :]), halves(UIN[:, t, :]), PRM[:, PC_SD + t:PC_SD + t + 1], bk(1 + 2 * t, 2),
                        ALU.mult, ALU.add).then_inc(S("s5_y"), 1)

                def mixed(k, fill):
                    m = MIXED[k]
                    if some(k - 1):
                        ve.wait_ge(S("mx_hi"), k - 1)
                    fill()
                    ve.wait_ge(S("mx_hi"), k + 1)
                    tt(XNL[:, m, :], PT2[:, k % 2, :], f32(XNH[:, m, :]), ALU.subtract).then_inc(S("x_lo"), 1)
                for t in range(2):
                    ve.wait_ge(S("glu_sg"), t + 1)
                    mixed(t, lambda: tt(PT2[:, t, :], PT2[:, t, :], UIN[:, t, :], ALU.mult).then_inc(S("mx"), 1))
                for m in range(PAIRS):
                    ve.wait_ge(S("gn_mean"), m + 1)
                    tt(halves(KK[:, m, 0:T]), halves(KK[:, m, 0:T]), bk(6 if m % 2 == 0 else 4, 2), ALU.subtract)\
                        .then_inc(S("gn_d"), 1)
                ve.wait_ge(S("gn_rs"), 1)
                step(tt(KK[:, :, 0:T], KK[:, :, 0:T], RS6[:, :, :], ALU.mult))
                for m in range(PAIRS):
                    od.done(ts(KK[:, m, 0:T], KK[:, m, 0:T], PRM[:, PC_LNW + m:PC_LNW + m + 1],
                               PRM[:, PC_LNB + m:PC_LNB + m + 1], ALU.mult, ALU.add))
                od.settle()
                step(tt(KK[:, :, 0:T], KK[:, :, 0:T], SIG[:, :, 0:T], ALU.add))
                for m in range(PAIRS):
                    def gated():
                        ve.wait_ge(S("gate_mm"), m + 1)
                        ve.wait_ge(S("x_lo"), x_ready["out0"] - KD + 2 + m)
                        tt(halves(PT2[:, m % 2, :]), halves(KK[:, m, 0:T]), bk(4 + 2 * (m % 2), 2), ALU.mult)\
                            .then_inc(S("mx"), 1)
                    mixed(2 + m, gated)
                split("out0", 0, 0)
                residual("out0")
            if "ffn0" in stages:
                split("up0", 0, 0)
                norm(nn, "up0", PC_FFN); nn += 1
                up(0)
                split("down0", 0, 0)
                residual("down0")
            if "fox" in stages:
                split("in1", 0, 0)
                norm(nn, "in1", PC_MIX + KD); nn += 1
                ve.wait_ge(S("wf_hi"), 1)
                tt(WFL[:, :, :], WF[:, :, :], f32(WFH[:, :, :]), ALU.subtract).then_inc(S("wf_lo"), 1)
                split("in1", 0, 1)
                split("in1", 1, 0)
                ve.wait_ge(S("f_mm"), 1)
                ts(halves(CUM[0:16, 0, :]), BK[0:16, 4:6, 0:HT], BF[0:16, 0:1], None, ALU.add).then_inc(S("f_rd"), 1)
                ve.wait_ge(S("f_rd"), 1)
                step(ts(CUM[0:16, 1, :], CUM[0:16, 0, :], -1.0, None, ALU.mult))
                tt(CUM[0:16, 1, :], CUM[0:16, 1, :], CUM[0:16, 0, :], ALU.max).then_inc(S("f_abs"), 1)
                step(ts(CUM[0:16, 2, :], CUM[0:16, 0, :], 0.0, None, ALU.min))
                split("in1", 1, 1)
                split("in1", 2, 0)
                split("in1", 2, 1)
                split("in1", 3, 0)
                ve.wait_ge(S("f_act"), 1)
                step(tt(CUM[0:16, 1, :], CUM[0:16, 1, :], CUM[0:16, 2, :], ALU.subtract))
                nc.vector.tensor_tensor_scan(CUM[0:16, 0, :], ONES[0:16, 0:1].to_broadcast([16, T]), CUM[0:16, 1, :],
                                             0.0, ALU.mult, ALU.add).then_inc(S("cum"), 1)
                with ve.Fori(3, 11) as i:
                    split("in1", i, 1)
                    split("in1", i + 1, 0)
                split("in1", 11, 1)
                ve.wait_ge(S("gain_in"), 64)
                ve.wait_ge(S("fx_rs"), FOX_PAIRS)
                ve.wait_ge(S("qz"), 2)
                ve.wait_ge(S("w_used"), at["in1"][0] + 24)
                ve.wait_ge(S("ps_free"), at["in1"][1] + 24)
                o0 = od.at

                def operands(i):
                    if some(NQ * i):
                        ve.wait_ge(S("fx_s"), NQ * i)
                    for e in range(2):
                        h = slice(64 * e, 64 * e + 64)
                        stt(QZ[h, e:e + 1, :], QKV[h, ds(i, 1), :], GAINS[h, 0:1], FRS[h, ds(i, 1), :], ALU.mult, ALU.mult)
                    stt(KS[:, :].unsqueeze(1), QKV[:, ds(8 + i, 1), :], GAINS[:, 1:2], FRS[:, ds(8 + i, 1), :],
                        ALU.mult, ALU.mult).then_inc(S("fx_k"), 1)

                def maxima(i, j):
                    lo, n = TILES[j]
                    w = n - lo
                    m = min(n, 512)
                    b = 2 * SLOT[j]
                    ss = SS[0:w, SLOT[j], :, 0:n] if j else SS[0:w, SLOT[j], :, 512:512 + n]
                    c = 0 if j else 512 - w
                    bias = CB[0:w, :, ds(i, 1), :].rearrange("p e o t -> p (e o) t")
                    ve.wait_ge(S("fx_s"), NQ * i + j + 1)
                    if some(NQ * i + j - COLS_BACK[j] + 1):
                        ve.wait_ge(S("fx_e"), NQ * i + j - COLS_BACK[j] + 1)
                    if n > m:
                        stt(ss[:, :, m:n], BK[0:w, 6:8, 0:n - m], 0.125, bias[:, :, m:n], ALU.mult, ALU.add)
                    stt(ss[:, :, 0:m], BK[0:w, b:b + 2, c:c + m], 0.125, bias[:, :, 0:m], ALU.mult, ALU.add)\
                        .then_inc(S("fx_ss"), 1)
                    ve.wait_ge(S("fx_ss"), NQ * i + j + 1)
                    nc.vector.tensor_reduce(MX[0:w, j, :], ss, AXX, ALU.max, negate=True).then_inc(S("fx_mx"), 1)

                def weights(i, j):
                    n = TILES[j][1]
                    w = n - TILES[j][0]
                    c = 0 if j else 512
                    ve.wait_ge(S("fx_e"), NQ * i + j + 1)
                    step(nc.vector.reciprocal(RC[0:w, j, :], SM[0:w, j, :]))
                    for e in range(2):
                        pr = PR[0:w, SLOT[j], e, c:c + n]
                        x = ts(pr, pr, RC[0:w, j, e:e + 1], None, ALU.mult)
                    x.then_inc(S("fx_d"), 1)

                def low(i):
                    ve.wait_ge(S("ot_hi"), i + 1)
                    tt(XNL[:, ds(i, 1), :], OT[:, :].unsqueeze(1), f32(XNH[:, ds(i, 1), :]), ALU.subtract)\
                        .then_inc(S("x_lo"), 1)

                def pair(i):
                    last = isinstance(i, int) and i == FOX_PAIRS - 1
                    od.at = o0 + NQ * i
                    for j in range(NQ):
                        weights(i, j)
                        if j == NQ - 2 and not last:
                            operands(i + 1)
                        if j < NQ - 2:
                            maxima(i, j + 2)
                        elif not last:
                            maxima(i + 1, j - NQ + 2)
                        if j == 0 and some(i):
                            low(i - 1)
                operands(0)
                ve.wait_ge(S("cb_in"), 16 * FOX_PAIRS)
                maxima(0, 0)
                maxima(0, 1)
                rounds(ve, FOX_PAIRS, pair, first=True)
                low(FOX_PAIRS - 1)
                ve.wait_ge(S("x_lo"), x_ready["out1"])
                od.at = o0 + NQ * FOX_PAIRS
                split("out1", 0, 0)
                residual("out1")
            if "ffn1" in stages:
                split("up1", 0, 0)
                norm(nn, "up1", PC_FFN + KD); nn += 1
                up(1)
                split("down1", 0, 0)
                residual("down1")
            for i in range(0, 8, 2):
                ve.wait_ge(S("o_t"), i + 1)
                if some(i):
                    ve.wait_ge(S("o_cp"), i)
                ve.tensor_copy(OUTB[:, i // 2, 0:512], BK[:, 4, :]).then_inc(S("o_cp"), 1)


_INS = ['x', 'meta_tokens', 'mix_norm', 'ffn_norm', 'even_w_in', 'even_w_out', 'rwkv_mu', 'rwkv_w0', 'rwkv_w2',
        'rwkv_a0', 'rwkv_a2', 'rwkv_g2', 'rwkv_k_k', 'rwkv_k_a', 'rwkv_r_k', 'rwkv_ln_w', 'rwkv_ln_b', 's5_a_re',
        's5_a_im', 's5_log_dt', 's5_b_re', 's5_b_im', 's5_c_re', 's5_c_im', 's5_d', 's5_glu_w', 's5_glu_b',
        'odd_w_in', 'odd_w_out', 'fox_b_f', 'fox_q_gain', 'fox_k_gain', 'ffn_w_up', 'ffn_conv_w', 'ffn_conv_b',
        'ffn_w_down']
_OUTS = [((1, SEQ, D_MODEL), 'float32')]


def kernel(**inputs):
    import numpy as _np
    import concourse.bacc as _bacc
    from concourse import mybir as _mybir
    from concourse.bass_utils import run_bass_kernel_spmd as _run

    nc = _bacc.Bacc("TRN2", target_bir_lowering=False, num_devices=1)
    arrays, args = {}, {}
    for name in _INS:
        a = _np.ascontiguousarray(inputs[name])
        arrays[f"in_{name}_dram"] = a
        args[name] = nc.dram_tensor(f"in_{name}_dram", a.shape, _mybir.dt.from_np(a.dtype), kind="ExternalInput").ap()
    shape, dtype = _OUTS[0]
    o = nc.dram_tensor("out_0_dram", shape, _mybir.dt.from_np(_np.dtype(dtype)), kind="ExternalOutput").ap()
    decoder_trunk(nc, args, o)
    r = _run(nc, [arrays], core_ids=[0])
    return r.results[0]["out_0_dram"]
```

```python
from contextlib import ExitStack
import math

import concourse.bass as bass
from concourse import mybir

F32 = mybir.dt.float32
F32R = mybir.dt.float32r
ALU = mybir.AluOpType
ACT = mybir.ActivationFunctionType
AXX = mybir.AxisListType.X
ds = bass.ds

P = 128
D_MODEL = 1024
KD = D_MODEL // P
SEQ = 512
N_META = 16
T = SEQ + N_META
HT = T // 2
D_FF = 2816
KF = D_FF // P
RWKV_DIM = 768
PAIRS = RWKV_DIM // P
LORA = 64
S5_TILES = 2
N_STATE_TILES = 8
C = 64
CHUNKS = -(-T // C)
TP = CHUNKS * C
G3 = 3
HEADS = (slice(0, 64), slice(64, 128))
FOX_PAIRS = 8
TILES = [(0, N_META)] + [(t, t + P) for t in range(N_META, T, P)]
NQ = len(TILES)
SLOT = (0, 0, 1, 0, 1)
BANKS_BACK = (2, 1, 3, 2, 2)
COLS_BACK = (5, 3, 3, 2, 2)
RMS_EPS = 1e-6
GN_EPS = 64e-5
DECAY = math.exp(-0.5)
LN_SHIFT = 2.0 ** 30
MASKED = -(2.0 ** 100)

PC_MIX, PC_FFN, PC_MU, PC_W0, PC_A0, PC_KK, PC_KA, PC_RK, PC_LNW, PC_LNB, PC_SD, PC_GLB, PC_ARE, PC_AIM = (
    0, 16, 32, 52, 58, 64, 70, 76, 82, 88, 94, 96, 98, 106)
PC_CONV = 114
CONV_COLS = 4 * 2 * KF
N_PRM = PC_CONV + 2 * CONV_COLS
N_PRM_LOADS = 24

GEMMS = [("in0", 22, KD, 22), ("out0", 8, KD, 8), ("up0", 2 * KF, KD, 2 * KF), ("down0", 16, KF // 2, 8),
         ("in1", 24, KD, 24), ("out1", 8, KD, 8), ("up1", 2 * KF, KD, 2 * KF), ("down1", 16, KF // 2, 8)]


def plan(stages):
    need = {"mix0": ("in0", "out0"), "ffn0": ("up0", "down0"), "fox": ("in1", "out1"), "ffn1": ("up1", "down1")}
    used = {g for s in stages if s in need for g in need[s]}
    u = q = 0
    at = {}
    for name, units, k, groups in GEMMS:
        if name in used:
            at[name] = (u, q, units, k)
            u += units
            q += groups
    return at


def decoder_trunk(nc, a, out, stages=("mix0", "ffn0", "fox", "ffn1")):
    at = plan(stages)
    ctx = ExitStack()
    with ctx:
        base = [16512]
        END = 229368
        used_to = [0]

        def put(name, shape, dt, offset):
            n = 4
            for d in shape[1:]:
                n *= d
            assert offset + n <= END, (name, offset, n)
            used_to[0] = max(used_to[0], offset + n)
            return nc.alloc_sbuf_tensor_at(name, shape, dt, offset=offset)

        def row(start):
            pos = [start]

            def place(name, *shape, dt=F32):
                n = 4
                for d in shape:
                    n *= d
                t = put(name, [P, *shape], dt, pos[0])
                pos[0] += -(-n // 32) * 32
                return t
            place.pos = pos
            return place

        keep = row(base[0])
        H = keep("H", KD, T)
        PRM = keep("PRM", N_PRM)
        IDENT = keep("IDENT", P)
        BONES = keep("BONES", P)
        BONES64 = keep("BONES64", P)
        ONES = keep("ONES", P)
        EPS = keep("EPS", 4)
        GAINS = keep("GAINS", 2)
        MAG = keep("MAG", N_STATE_TILES)
        POW = keep("POW", N_STATE_TILES, 10, 2)
        PCH = keep("PCH", PAIRS, CHUNKS)
        RAW = keep("RAW", 2, KF // 2, P)
        wpos = keep.pos[0]
        WHI = keep("WHI", 2, KF // 2, P, dt=F32R)
        WLO = keep("WLO", 2, KF // 2, P, dt=F32R)
        wend = keep.pos[0]
        hpos = keep.pos[0]
        XNH = keep("XNH", KD, T, dt=F32R)
        XNL = keep("XNL", KD, T, dt=F32R)
        zpos = keep.pos[0]
        z = row(zpos)
        XIN = z("XIN", 5, D_MODEL)
        PRAW = z("PRAW", 6, P)
        RST = z("RST", 2, HT)
        NT = z("NT", 2, T)
        SQ = put("SQ", [P, 2, T], F32, (END - 8 * T) // 32 * 32)
        z = row(zpos)
        GH = z("GH", KF, T, dt=F32R)
        GL = z("GL", KF, T, dt=F32R)
        CP = z("CP", 2, T + 2)
        CA = z("CA", 2, T)
        SG = z("SG", T)
        GT = z("GT", T)
        z = row(zpos)
        RKV = z("RKV", 20, TP)
        KK = z("KK", PAIRS, TP)
        AA = z("AA", PAIRS, TP)
        SIG = z("SIG", PAIRS, TP)
        r6 = z.pos[0]
        CS = z("CS", PAIRS, TP)
        PP = z("PP", PAIRS, CHUNKS, C + 1)
        UIN = z("UIN", S5_TILES, T)
        tail = z.pos[0]
        PB = put("PB", [P, 2, T + 1], F32, r6)
        DT = put("DT", [P, 2, T], F32, r6 + 2 * (T + 1) * 4 + 24)
        z = row(r6 + 9216)
        BBM = z("BBM", 2, N_STATE_TILES, P)
        BR = z("BR", 2, N_STATE_TILES, 16)
        BB = z("BB", 2, N_STATE_TILES, 16)
        S5V = z("S5V", 16, N_STATE_TILES)
        assert z.pos[0] <= tail - 4 * S5_TILES * T
        U = put("U", [P, 2, N_STATE_TILES, T], F32, hpos)
        G2 = put("G2", [P, RWKV_DIM], F32, wpos)
        GLW = put("GLW", [P, 2, 2 * P], F32, wpos + 4 * RWKV_DIM)
        z = row(wpos)
        KR = z("KR", PAIRS, 3, C)
        BHD = z("BHD", PAIRS, 2, C)
        KHD = z("KHD", PAIRS, 2, C)
        VH = z("VH", PAIRS, C)
        MQA = z("MQA", PAIRS, 2, 2, C)
        SS0 = z("SS0", PAIRS, C)
        LVL = z("LVL", 5, P)
        assert z.pos[0] <= wend
        rpos = wpos - 4 * 2 * (KF // 2) * P
        WB = put("WB", [P, 2, N_STATE_TILES, P], F32, rpos)
        z = row(rpos + 4 * 2 * N_STATE_TILES * P)
        M1T = z("M1T", P)
        MU2 = z("MU2", P)
        MQ = z("MQ", 2, C)
        z = row(r6)
        AT = z("AT", PAIRS, 2, C)
        XX = z("XX", PAIRS, 2, C)
        XT = z("XT", PAIRS, 2, C)
        TM = z("TM", PAIRS, 2, C)
        BKT = z("BKT", PAIRS, 2, C)
        VT = z("VT", PAIRS, C)
        NG = z("NG", PAIRS, C)
        SA = z("SA", PAIRS, C)
        assert z.pos[0] <= tail - 4 * S5_TILES * T - 8 * T
        FC = put("FC", [P, 2, T], F32, tail - 4 * S5_TILES * T - 8 * T)
        z = row(tail)
        FT2 = z("FT2", T)
        FT1 = put("FT1", [P, T], F32, zpos + 18 * 4 * TP)
        MK = put("MK", [P, 4, P], F32, zpos + 20 * 4 * TP)
        z = row(hpos)
        W2A2 = z("W2A2", 2, RWKV_DIM)
        RESET = z("RESET", TP)
        BOTH = z("BOTH", P)
        z = row(r6)
        RS6 = z("RS6", PAIRS, T)
        WC = z("WC", 2, N_STATE_TILES, P)
        CRAW = z("CRAW", 2, 2, 2, C)
        MK2 = z("MK2", 4, P)
        assert z.pos[0] <= tail - 4 * S5_TILES * T
        z = row(zpos)
        PT2 = z("PT2", 2, T)
        GLS = z("GLS", 2, T)
        z = row(zpos)
        QKV = z("QKV", 24, T)
        FRS = z("FRS", 16, T)
        PTT = z("PTT", 2, NQ, T)
        PR = z("PR", 2, 2, T)
        MX = z("MX", NQ, 2)
        SM = z("SM", NQ, 2)
        RC = z("RC", NQ, 2)
        CM = z("CM", P)
        fpos = zpos + 24 * T * 4 + 16 * T * 4
        CUM = put("CUM", [P, 3, T], F32, fpos)
        FSQ = put("FSQ", [P, 2, T], F32, fpos + 3 * T * 4)
        z = row(zpos + 106112)
        WF = z("WF", KD, 16)
        WFH = z("WFH", KD, 16, dt=F32R)
        WFL = z("WFL", KD, 16, dt=F32R)
        BF = z("BF", 1)
        z = row(wpos)
        QZ = z("QZ", 2, T)
        KS = z("KS", T)
        VF = z("VF", T)
        VS = z("VS", NQ, P)
        SS = z("SS", 2, 2, T)
        OT = z("OT", T)
        assert z.pos[0] <= wend
        CB = put("CB", [P, 2, FOX_PAIRS, T], F32, hpos)
        OUTB = put("OUTB", [P, 4, D_MODEL], F32, zpos)
        BK = ctx.enter_context(nc.psum_tensor("BK", [P, 8, 512], F32))
        cum_dram = nc.dram_tensor("cum_dram", [16, T], F32, kind="Internal").ap()

        sems = {}

        def S(name):
            if name not in sems:
                sems[name] = ctx.enter_context(nc.semaphore(name))
            return sems[name]

        def some(count):
            return not isinstance(count, int) or count > 0

        class Order:

            def __init__(self, eng, name):
                self.eng, self.name, self.at = eng, name, 0

            def done(self, ins):
                ins.then_inc(S(self.name), 1)
                self.at = self.at + 1

            def settle(self):
                if some(self.at):
                    self.eng.wait_ge(S(self.name), self.at)

        def rounds(eng, n, body, first=False, last=True):
            lo, hi = (1 if first else 0), (n - 1 if last else n)
            if first:
                body(0)
            if hi > lo:
                with eng.Fori(lo, hi) as i:
                    body(i)
            if last:
                body(n - 1)

        def bk(lo, n):
            return BK[:, lo:lo + n, 0:HT]

        def halves(ap):
            return ap.rearrange("p (a b) -> p a b", a=2)

        w_src = {
            "in0": a["even_w_in"][0], "out0": a["even_w_out"][0], "in1": a["odd_w_in"][0], "out1": a["odd_w_out"][0],
            "up0": a["ffn_w_up"][0], "up1": a["ffn_w_up"][1], "down0": a["ffn_w_down"][0], "down1": a["ffn_w_down"][1],
        }
        x_in = {g: (XNH, XNL) for g in ("in0", "out0", "in1", "out1", "up0", "up1")}
        x_in["down0"] = x_in["down1"] = (GH, GL)
        x_ready, n_x = {}, 0
        for g, _, _, _ in GEMMS:
            if g in at:
                n_x += KF if g.startswith("down") else KD
                x_ready[g] = n_x
        h_ready = {g: at[g][1] + KD for g in ("out0", "down0", "out1", "down1") if g in at}
        n_groups = max([0] + list(h_ready.values()))
        order = [g for g, _, _, _ in GEMMS if g in at]
        after = dict(zip(order, order[1:] + [None]))
        norm_of = {"in0": 0}
        for g in ("up0", "in1", "up1"):
            if g in at:
                norm_of[g] = len([q for q in ("in0", "up0", "in1", "up1") if q in at and order.index(q) < order.index(g)])

        block = ctx.enter_context(nc.Block())

        @block.sync
        def _(sp):
            def load(g, i, s):
                u0, _, _, k = at[g]
                if some(u0 + 2 * i + s - 1):
                    sp.wait_ge(S("w_lo"), u0 + 2 * i + s - 1)
                w = w_src[g]
                if g.startswith("down"):
                    src = w.rearrange("(s k p) n -> s p k n", s=2, p=P)[s, :, :, ds(i * P, P)]
                elif g.startswith("up"):
                    src = w.rearrange("(k p) n -> p k n", p=P)[:, :, ds(i * P + s * D_FF, P)]
                else:
                    src = w.rearrange("(k p) n -> p k n", p=P)[:, :, ds((2 * i + s) * P, P)]
                sp.dma_start(RAW[:, s, 0:k, :], src).then_inc(S(f"w_in{s}"), 16)

            for s in range(2):
                load(order[0], 0, s)
            def rows(src, n, tile, r0):
                sp.dma_start(PRAW[r0:r0 + n, tile, :], src.rearrange("(m p) -> m p", p=P)).then_inc(S("prm_in"), 16)
                return 1
            n = 0
            for l in range(2):
                n += rows(a["mix_norm"][l], KD, 0, PC_MIX + KD * l)
                n += rows(a["ffn_norm"][l], KD, 0, PC_FFN + KD * l)
            for key, col, m in (("rwkv_mu", PC_MU, 20), ("rwkv_w0", PC_W0, 6), ("rwkv_a0", PC_A0, 6),
                                ("rwkv_k_k", PC_KK, 6), ("rwkv_k_a", PC_KA, 6), ("rwkv_ln_w", PC_LNW, 6),
                                ("rwkv_ln_b", PC_LNB, 6), ("s5_d", PC_SD, 2), ("s5_glu_b", PC_GLB, 2)):
                n += rows(a[key][0], m, 0, col)
            n += rows(a["rwkv_r_k"][0].rearrange("h d -> (h d)"), 6, 0, PC_RK)
            n += rows(a["s5_a_re"][0].rearrange("g n -> (g n)"), 8, 0, PC_ARE)
            n += rows(a["s5_a_im"][0].rearrange("g n -> (g n)"), 8, 0, PC_AIM)
            for l in range(2):
                for t in range(2):
                    n += rows(a["ffn_conv_w"][l, t], 2 * KF, 1 + 2 * l, 2 * KF * t)
                n += rows(a["ffn_conv_w"][l, 2], 2 * KF, 2 + 2 * l, 0)
                n += rows(a["ffn_conv_b"][l], 2 * KF, 2 + 2 * l, 2 * KF)
            sp.dma_start(S5V[0:8, 15, 0:2], a["s5_log_dt"][0].rearrange("(j g) -> j g", g=2)).then_inc(S("prm_in"), 16)
            assert n == N_PRM_LOADS
            for i, key in enumerate(("s5_b_re", "s5_b_im")):
                sp.dma_start(BR[:, i, :, :], a[key][0].rearrange("(j g) n c -> (g n) j c", g=2)).then_inc(S("b_in"), 16)
            for e in range(2):
                for i, key in enumerate(("fox_q_gain", "fox_k_gain")):
                    sp.dma_start(GAINS[64 * e:64 * e + 64, i:i + 1],
                                 a[key][0].rearrange("(d o) -> d o", o=1)).then_inc(S("gain_in"), 16)
            def loads(g):
                with sp.Fori(1 if g == order[0] else 0, at[g][2] // 2) as i:
                    for s in range(2):
                        load(g, i, s)

            if "mix0" in stages:
                loads("in0")
                sp.wait_ge(S("w_used"), 22)
                sp.dma_start(W2A2[0:LORA, 0, :], a["rwkv_w2"][0]).then_inc(S("lora_in"), 16)
                sp.dma_start(W2A2[LORA:2 * LORA, 1, :], a["rwkv_a2"][0]).then_inc(S("lora_in"), 16)
                sp.wait_ge(S("s5_bum"), 16)
                load("out0", 0, 0)
                for g in range(2):
                    sp.wait_ge(S(f"y_out{g}"), CHUNKS)
                    sp.wait_ge(S(f"state{g}"), CHUNKS - 1)
                sp.dma_start(G2[:, :], a["rwkv_g2"][0]).then_inc(S("post_in"), 16)
                sp.dma_start(GLW[:, :, :], a["s5_glu_w"][0].rearrange("(k p) n -> p k n", p=P)).then_inc(S("post_in"), 16)
                for i, key in enumerate(("s5_c_re", "s5_c_im")):
                    src = a[key][0].rearrange("g c n -> (g c) n").rearrange("(t r) n -> r t n", r=P)
                    for e in range(2):
                        sp.dma_start(CRAW[:, i, :, e, :], src).then_inc(S("post_in"), 16)
                load("out0", 0, 1)
                with sp.Fori(1, 4) as i:
                    for s in range(2):
                        load("out0", i, s)
            if "ffn0" in stages:
                loads("up0")
                loads("down0")
            if "fox" in stages:
                sp.dma_start(WF[:, :, :], a["odd_w_in"][0].rearrange("(k p) n -> p k n", p=P)[:, :, 3 * D_MODEL:])\
                    .then_inc(S("wf_in"), 16)
                sp.dma_start(BF[0:16, :], a["fox_b_f"][0].rearrange("(h o) -> h o", o=1)).then_inc(S("wf_in"), 16)
                loads("in1")
                for s in range(2):
                    load("out1", 0, s)
                sp.wait_ge(S("cum"), 1)
                sp.dma_start(cum_dram, CUM[0:16, 0, :]).then_inc(S("cum_out"), 16)
                sp.wait_ge(S("cum_out"), 16)
                sp.wait_ge(S("w_used"), at["in1"][0] + 24)
                for i in range(FOX_PAIRS):
                    sp.dma_start(CB[:, :, i, :], cum_dram[2 * i:2 * i + 2, :].unsqueeze(0).to_broadcast([P, 2, T]))\
                        .then_inc(S("cb_in" if i else "cb0_in"), 16)
                with sp.Fori(1, 4) as i:
                    for s in range(2):
                        load("out1", i, s)
            if "ffn1" in stages:
                loads("up1")
                loads("down1")
            for j in range(4):
                sp.wait_ge(S("o_cp"), 2 * j + 2)
                sp.dma_start(out[0, P * j:P * j + P, :], OUTB[:, j, :]).then_inc(S("stored"), 16)
            sp.wait_ge(S("stored"), 64)

        @block.gpsimd
        def _(po):
            od = Order(po, "po_order")

            def step(ins):
                od.done(ins)
                od.settle()

            step(po.memset(IDENT[:, :], 0.0))
            po.affine_select(out=IDENT[:, :], in_=IDENT[:, :], compare_op=ALU.not_equal, fill=1.0, base=0,
                             pattern=[[-1, P]], channel_multiplier=1).then_inc(S("consts"), 1)
            po.wait_ge(S("consts"), 1)
            for t, v in ((BONES, 1.0), (BONES64, 1.0 / 64)):
                step(po.memset(t[:, :], 0.0))
                step(po.memset(t[0:64, 0:64], v))
                step(po.memset(t[64:128, 64:128], v))
            for i, v in enumerate((RMS_EPS, GN_EPS, 0.5 * math.log(LN_SHIFT))):
                step(po.memset(EPS[:, i:i + 1], v))

            def channel_masks(mk, n):
                step(po.memset(mk[:, :, :], 0.0))
                for e in range(2):
                    for jj in range(4):
                        po.memset(mk[64 * e:64 * e + 64, jj, 16 * (2 * jj + e):16 * (2 * jj + e) + 16], 1.0)\
                            .then_inc(S("mk"), 1)
                        po.wait_ge(S("mk"), n + 4 * e + jj + 1)
            channel_masks(MK, 0)
            po.memset(ONES[:, :], 1.0).then_inc(S("consts"), 1)
            po.wait_ge(S("consts"), 2)
            if "mix0" in stages:
                po.wait_ge(S("w_used"), 22)
                for e in range(2):
                    po.memset(W2A2[64 - 64 * e:128 - 64 * e, e, :], 0.0).then_inc(S("cleared"), 1)
                    po.wait_ge(S("cleared"), e + 1)
                step(po.memset(RESET[:, :], 1.0))
                po.memset(RESET[:, :].rearrange("p (c t) -> p c t", t=C)[:, :, 0:1], 0.0).then_inc(S("cleared"), 1)
                po.wait_ge(S("cleared"), 3)
                for n, t in enumerate((RKV[:, 0:3 * PAIRS, T:TP], KK[:, :, T:TP], AA[:, :, T:TP], SIG[:, :, T:TP])):
                    po.memset(t, 0.0).then_inc(S("cleared"), 1)
                    po.wait_ge(S("cleared"), n + 4)
                step(po.memset(MU2[:, :], 1.0))
                step(po.affine_select(out=MU2[:, :], in_=MU2[:, :], compare_op=ALU.is_gt, fill=0.0, base=0,
                                      pattern=[[1, P]], channel_multiplier=-1))
                step(po.memset(MU2[0:64, 64:128], 0.0))
                incl = BOTH[:, :]
                step(po.memset(incl, 1.0))
                step(po.affine_select(out=incl, in_=incl, compare_op=ALU.is_ge, fill=0.0, base=0,
                                      pattern=[[1, P]], channel_multiplier=-1))
                for e in range(2):
                    h = slice(64 * e, 64 * e + 64)
                    step(po.tensor_copy(MQ[h, 0, :], MU2[h, 64 * e:64 * e + 64]))
                    step(po.tensor_copy(MQ[h, 1, :], BOTH[h, 64 * e:64 * e + 64]))
                step(po.memset(M1T[:, :], 0.0))
                m1t = M1T[:, :].rearrange("p (q r) -> p q r", r=2)
                step(po.affine_select(out=m1t[:, :, 1], in_=m1t[:, :, 1], compare_op=ALU.not_equal, fill=-1.0, base=0,
                                      pattern=[[-2, 64]], channel_multiplier=1))
                step(po.tensor_tensor(M1T[:, :], M1T[:, :], IDENT[:, :], ALU.subtract))
                for n in range(5):
                    b = 2 << n
                    m = LVL[:, n, :].rearrange("p (q r c) -> p q r c", r=2, c=b)
                    step(po.memset(LVL[:, n, :], 0.0))
                    step(po.memset(m[:, :, 0, :], 1.0))
                    step(po.affine_select(out=m[:, :, 0, :], in_=m[:, :, 0, :], compare_op=ALU.is_ge, fill=0.0, base=-b,
                                          pattern=[[-2 * b, 64 // b], [0, b]], channel_multiplier=1))
                    po.affine_select(out=m[:, :, 0, :], in_=m[:, :, 0, :], compare_op=ALU.is_ge, fill=0.0,
                                     base=2 * b - 1, pattern=[[2 * b, 64 // b], [0, b]], channel_multiplier=-1)\
                        .then_inc(S("po_order"), 1)
                    od.at = od.at + 1
                    od.settle()
                    po.tensor_tensor(LVL[:, n, :], LVL[:, n, :], IDENT[:, :], ALU.add).then_inc(S("masks"), 1)
                    po.wait_ge(S("masks"), n + 1)
                step(po.memset(SS0[:, :, :], 0.0))
                for t in (BHD, KHD):
                    for e in range(2):
                        step(po.memset(t[64 * e:64 * e + 64, :, 1 - e, :], 0.0))
                for e in range(2):
                    h = slice(64 * e, 64 * e + 64)
                    for p in range(PAIRS):
                        po.tensor_copy(KR[h, p, 2, :], IDENT[h, 64 * e:64 * e + 64]).then_inc(S("chunk_init"), 1)
                        po.wait_ge(S("chunk_init"), PAIRS * e + p + 1)
                po.wait_ge(S("kkn"), 2)
                for m in range(PAIRS):
                    po.wait_ge(S("k_mod"), m + 1)
                    po.tensor_tensor(AA[:, m, 0:T], AA[:, m, 0:T], KK[:, m, 0:T], ALU.mult).then_inc(S("b_ops"), 1)
                    po.wait_ge(S("b_ops"), m + 1)
                po.wait_ge(S("dec"), PAIRS + 1)
                for m in range(PAIRS):
                    po.tensor_tensor(AA[:, m, :], AA[:, m, :], CS[:, m, :], ALU.mult).then_inc(S("b_ops"), 1)
                    po.wait_ge(S("b_ops"), PAIRS + m + 1)
                po.wait_ge(S("tilde"), 1)
                po.wait_ge(S("s5_pow"), 1)
                po.wait_ge(S("s5_ucp"), 2 * N_STATE_TILES)
                od_loop = od.at

                def own_wait():
                    po.sem_inc(S("own_wait"), 1)

                def s5_tile(j):
                    od.at = od_loop + PER * j
                    cos, sin = FC[:, 0, :], FC[:, 1, :]
                    t1, t2 = FT1[:, :], FT2[:, :]
                    if some(2 * j):
                        po.wait_ge(S("s5_out"), 2 * j)
                    own_wait()
                    step(po.memset(FC[:, 0, 0:1], 1.0))
                    own_wait()
                    step(po.memset(FC[:, 1, 0:1], 0.0))
                    n = 1
                    for lev in range(10):
                        m = min(n, T - n)
                        pc = POW[:, ds(j, 1), lev, 0:1].rearrange("p a b -> p (a b)").to_broadcast([P, m])
                        ps = POW[:, ds(j, 1), lev, 1:2].rearrange("p a b -> p (a b)").to_broadcast([P, m])
                        own_wait()
                        step(po.tensor_tensor(t1[:, 0:m], cos[:, 0:m], pc, ALU.mult))
                        own_wait()
                        step(po.tensor_tensor(t2[:, 0:m], sin[:, 0:m], ps, ALU.mult))
                        step(po.tensor_tensor(cos[:, n:n + m], t1[:, 0:m], t2[:, 0:m], ALU.subtract))
                        own_wait()
                        step(po.tensor_tensor(t1[:, 0:m], sin[:, 0:m], pc, ALU.mult))
                        own_wait()
                        step(po.tensor_tensor(t2[:, 0:m], cos[:, 0:m], ps, ALU.mult))
                        step(po.tensor_tensor(sin[:, n:n + m], t1[:, 0:m], t2[:, 0:m], ALU.add))
                        n += m
                    ur = U[:, 0, ds(j, 1), :].rearrange("p a t -> p (a t)")
                    ui = U[:, 1, ds(j, 1), :].rearrange("p a t -> p (a t)")
                    own_wait()
                    step(po.tensor_tensor(t1, ur, sin, ALU.mult))
                    own_wait()
                    step(po.tensor_tensor(t2, ui, sin, ALU.mult))
                    own_wait()
                    step(po.tensor_tensor(ur, ur, cos, ALU.mult))
                    own_wait()
                    step(po.tensor_tensor(ui, ui, cos, ALU.mult))
                    own_wait()
                    po.tensor_tensor(ur, ur, t2, ALU.add).then_inc(S("s5_in"), 1)
                    po.wait_ge(S("s5_in"), 2 * j + 1)
                    own_wait()
                    po.tensor_tensor(ui, ui, t1, ALU.subtract).then_inc(S("s5_in"), 1)
                    po.wait_ge(S("s5_scan"), 2 * j + 2)
                    own_wait()
                    step(po.tensor_tensor(t1, ur, sin, ALU.mult))
                    own_wait()
                    step(po.tensor_tensor(t2, ui, sin, ALU.mult))
                    own_wait()
                    step(po.tensor_tensor(ur, ur, cos, ALU.mult))
                    own_wait()
                    step(po.tensor_tensor(ui, ui, cos, ALU.mult))
                    own_wait()
                    po.tensor_tensor(ur, ur, t2, ALU.subtract).then_inc(S("s5_out"), 1)
                    po.wait_ge(S("s5_out"), 2 * j + 1)
                    own_wait()
                    po.tensor_tensor(ui, ui, t1, ALU.add).then_inc(S("s5_out"), 1)

                PER = 2 + 10 * 6 + 4 + 4
                rounds(po, N_STATE_TILES, s5_tile, first=True, last=False)
                od.at = od_loop + PER * N_STATE_TILES
                for g in range(2):
                    po.wait_ge(S(f"y_out{g}"), CHUNKS)
                    po.wait_ge(S(f"state{g}"), CHUNKS - 1)
                channel_masks(MK2, 8)
            if "fox" in stages:
                po.wait_ge(S("fx_rs"), FOX_PAIRS)
                step(po.memset(CM[:, :], 0.0))
                po.affine_select(out=CM[:, :], in_=CM[:, :], compare_op=ALU.is_ge, fill=MASKED, base=0,
                                 pattern=[[-1, P]], channel_multiplier=1).then_inc(S("fx_const"), 1)
                po.wait_ge(S("w_used"), at["in1"][0] + 24)
                po.wait_ge(S("ps_free"), at["in1"][1] + 24)

                po.wait_ge(S("fx_const"), 1)
                for e in range(2):
                    po.memset(QZ[64 - 64 * e:128 - 64 * e, e, :], 0.0).then_inc(S("fx_const"), 1)
                    po.wait_ge(S("fx_const"), e + 2)

                def values(i):
                    if some(i):
                        po.wait_ge(S("fx_vt"), i)
                    po.tensor_copy(VF[:, :], QKV[:, ds(16 + i, 1), :].rearrange("p a t -> p (a t)")).then_inc(S("fx_vf"), 1)
                rounds(po, FOX_PAIRS, values, first=True, last=False)

        @block.tensor
        def _(pe):
            def mm(o, l, r, start=True, stop=True, check=False):
                return pe.matmul(o, l, r, start=start, stop=stop, skip_group_check=check)

            def own_wait():
                pe.sem_inc(S("own_wait"), 1)

            def norm_sum(n, k, slot):
                pe.wait_ge(S("sq"), KD * n + k + 1)
                for h in range(2):
                    x = mm(BK[:, 4 + h, 0:HT], ONES[:, :], SQ[:, slot, h * HT:h * HT + HT],
                           not some(k), isinstance(k, int) and k == KD - 1, check=True)
                x.then_inc(S("sq_used"), 1)

            def unit(g, i, s, group, slot, start, stop):
                u0, _, _, kn = at[g]
                xh, xl = x_in[g]
                k0 = s * kn if g.startswith("down") else 0
                pe.wait_ge(S("w_lo"), u0 + 2 * i + s + 1)
                if start:
                    if some(group - 1):
                        pe.wait_ge(S("ps_free"), group - 1)
                for k in range(kn):
                    for n, (w, x) in enumerate(((WHI, xh), (WHI, xl), (WLO, xh))):
                        for h in range(2):
                            last = mm(BK[:, 2 * slot + h, 0:HT], w[:, s, k, :], x[:, k0 + k, h * HT:h * HT + HT],
                                      start and k == 0 and n == 0, stop and k == kn - 1 and n == 2)
                last.then_inc(S("w_used"), 1)

            def first_pair(g):
                u0, q0, _, _ = at[g]
                xh, xl = x_in[g]
                pe.wait_ge(S("w_lo"), u0 + 2)
                if q0:
                    pe.wait_ge(S("ps_free"), q0)
                for k in range(KD):
                    pe.wait_ge(S("x_lo"), x_ready[g] - KD + k + 1)
                    for s in range(2):
                        for n, (w, x) in enumerate(((WHI, xh), (WHI, xl), (WLO, xh))):
                            for h in range(2):
                                last = mm(BK[:, 2 * s + h, 0:HT], w[:, s, k, :], x[:, k, h * HT:h * HT + HT],
                                          k == 0 and n == 0, k == KD - 1 and n == 2)
                        if k == KD - 1:
                            last.then_inc(S("w_used"), 1)

            def gemm(g):
                u0, q0, units, _ = at[g]
                norm = norm_of[after[g]] if after[g] in norm_of else None
                if g.startswith("down"):
                    def body(ii):
                        for r in range(2):
                            i = 2 * ii + r
                            for s in range(2):
                                if not some(ii) and r == 0:
                                    pe.wait_ge(S("x_lo"), x_ready[g] - (KF // 2 if s == 0 else 0))
                                unit(g, i, s, q0 + i, r, s == 0, s == 1)
                                if s == 0 and norm is not None and some(i):
                                    norm_sum(norm, i - 1, 1 - r)
                    rounds(pe, KD // 2, body, last=False, first=True)
                elif g.startswith("up"):
                    def body(i):
                        for s in range(2):
                            unit(g, i, s, q0 + 2 * i + s, s, True, True)
                    first_pair(g)
                    with pe.Fori(1, units // 2) as i:
                        body(i)
                else:
                    pe.wait_ge(S("x_lo"), x_ready[g])

                    def body(i):
                        for s in range(2):
                            unit(g, i, s, q0 + 2 * i + s, s, True, True)
                            if norm is not None and some(2 * i + s):
                                norm_sum(norm, 2 * i + s - 1, 1 - s)
                    rounds(pe, units // 2, body, last=False, first=True)
                if norm is not None:
                    norm_sum(norm, KD - 1, 1)

            pe.wait_ge(S("consts"), 2)
            for j in range(5):
                n = N_META if j == 0 else P
                pe.wait_ge(S("x_in"), 80)
                for b in range(2):
                    if j:
                        pe.wait_ge(S(f"x_out{b}"), j)
                    for k in range(4):
                        x = pe.transpose(BK[:, 2 + b, P * k:P * k + n], XIN[0:n, j, P * (4 * b + k):P * (4 * b + k) + P],
                                         IDENT[0:n, 0:n])
                    x.then_inc(S(f"x_t{b}"), 1)
            pe.wait_ge(S("prm_in"), 16 * (N_PRM_LOADS + 1))
            pe.wait_ge(S("ldt"), 1)
            sizes = (114, 88, 88, 88, 88)
            for t, n in enumerate(sizes):
                pe.transpose(BK[:, t // 4, P * (t % 4):P * (t % 4) + n], PRAW[0:n, t, :], IDENT[0:n, 0:n])
            pe.transpose(BK[:, 1, P:P + 8], PRAW[0:8, 5, :], IDENT[0:8, 0:8]).then_inc(S("prm_t"), 1)
            if norm_of and order[0] in norm_of:
                for k in range(KD):
                    norm_sum(0, k, k % 2)
            if "mix0" in stages:
                u0, q0, units, _ = at["in0"]
                first_pair("in0")
                with pe.Fori(1, units // 2) as i:
                    for s in range(2):
                        unit("in0", i, s, q0 + 2 * i + s, s, True, True)
                pe.wait_ge(S("bbm"), 1)
                for i in range(2):
                    for j in range(0, N_STATE_TILES, 4):
                        b = 6 + (2 * i + j // 4) % 2
                        if some(2 * i + j // 4 - 1):
                            pe.wait_ge(S("wb_cp"), 2 * i + j // 4 - 1)
                        for jj in range(4):
                            x = pe.transpose(BK[:, b, P * jj:P * jj + P], BBM[:, i, j + jj, :], IDENT[:, :])
                        x.then_inc(S("wb_t"), 1)
                for m in range(PAIRS):
                    pe.wait_ge(S("kk_sq"), m + 1)
                    if m == 0:
                        pe.wait_ge(S("wb_cp"), 4)
                    if some(m - 1):
                        pe.wait_ge(S("kk_max"), m - 1)
                    for h in range(2):
                        x = mm(BK[:, 4 + 2 * (m % 2) + h, 0:HT], BONES[:, :], SIG[:, m, h * HT:h * HT + HT])
                    x.then_inc(S("kk_sum"), 1)
                pe.wait_ge(S("lora_in"), 32)
                pe.wait_ge(S("cleared"), 2)
                pe.wait_ge(S("lora_act"), 1)
                pe.wait_ge(S("ps_free"), 22)
                for m in range(PAIRS):
                    for i in range(2):
                        n = 2 * m + i
                        if some(n - 1):
                            pe.wait_ge(S("lora_cp"), n - 1)
                        for h in range(2):
                            x = mm(BK[:, 2 * (n % 2) + h, 0:HT], W2A2[:, i, P * m:P * m + P],
                                   RKV[:, 18, h * HT:h * HT + HT])
                        x.then_inc(S("lora_mm"), 1)
                for m in range(PAIRS):
                    pe.wait_ge(S("rk"), m + 1)
                    if some(m - 1):
                        pe.wait_ge(S("bonus"), m - 1)
                    for h in range(2):
                        x = mm(BK[:, 2 * (m % 2) + h, 0:HT], BONES[:, :], SIG[:, m, h * HT:h * HT + HT])
                    x.then_inc(S("bonus_mm"), 1)

                pe.wait_ge(S("wb_cp"), 4)
                pe.wait_ge(S("kk_max"), PAIRS)
                for j in range(N_STATE_TILES):
                    for i in range(2):
                        n = 2 * j + i
                        if some(n - 1):
                            pe.wait_ge(S("s5_ucp"), n - 1)
                        for h in range(2):
                            x = mm(BK[:, 4 + 2 * (n % 2) + h, 0:HT], WB[:, i, j, :], UIN[:, j // 4, h * HT:h * HT + HT])
                        x.then_inc(S("s5_bum"), 1)
                pe.wait_ge(S("chunk_init"), 2 * PAIRS)

                def transposed(c, g):
                    pe.wait_ge(S(f"xt_up{g}"), 6 * c + 1)
                    for q in range(G3):
                        x = pe.transpose(BK[:, 3 + 3 * g, P * q:P * q + P], XT[:, G3 * g + q, :, :], IDENT[:, :])
                    x.then_inc(S(f"xx_mm{g}"), 1)

                def chunk(c):
                    short = isinstance(c, int) and c == CHUNKS - 1
                    for p in range(PAIRS):
                        g = p // G3
                        if p % G3 == 0:
                            pe.wait_ge(S(f"stage{g}"), c + 1)
                        if p == 0:
                            pe.wait_ge(S("bv_stage"), c + 1)
                        if isinstance(c, int) and c == 0:
                            if some(p - 1):
                                pe.wait_ge(S("ph_out"), p - 1)
                        else:
                            pe.wait_ge(S("ph_out"), PAIRS * c + p - 1)
                        b = p % 2
                        mm(BK[:, b, 0:192], BHD[:, p, :, :], KR[:, p, :, :])
                        mm(BK[:, b, 192:384], KHD[:, p, :, :], KR[:, p, :, :])
                        for h in HEADS:
                            x = mm(BK[h, b, 384:448], VH[h, p, :], KR[h, p, 2, :])
                        x.then_inc(S("ph"), 1)
                        if p == PAIRS - 2:
                            transposed(c, 0)
                    levels = 3 if short else 5
                    for n in range(levels):
                        for g in range(2):
                            if n == 0 and g == 1:
                                transposed(c, 1)
                            pe.wait_ge(S(f"x_up{g}"), 5 * c + n + 1)
                            for q in range(G3):
                                p = G3 * g + q
                                x = mm(BK[:, 2 + 3 * g, P * q:P * q + P], AT[:, p, :, :], XX[:, p, :, :])
                            x.then_inc(S(f"t_mm{g}"), 1)
                        for g in range(2):
                            pe.wait_ge(S(f"t_mask{g}"), 5 * c + n + 1)
                            pe.wait_ge(S(f"xt_up{g}"), 6 * c + n + 1)
                            if n < levels - 1:
                                for q in range(G3):
                                    p = G3 * g + q
                                    x = mm(BK[:, 3 + 3 * g, P * q:P * q + P], XT[:, p, :, :], TM[:, p, :, :])
                                x.then_inc(S(f"xx_mm{g}"), 1)
                            for q in range(G3):
                                p = G3 * g + q
                                x = mm(BK[:, 4 + 3 * g, P * q:P * q + P], TM[:, p, :, :], XT[:, p, :, :])
                            x.then_inc(S(f"x_mm{g}"), 1)
                    for g in range(2):
                        pe.wait_ge(S(f"xt_up{g}"), 6 * c + levels + 1)
                        if some(c):
                            pe.wait_ge(S(f"state{g}"), c)
                        pe.wait_ge(S("ph_out"), PAIRS * c + G3 * (g + 1))
                        own_wait()
                        for q in range(G3):
                            p = G3 * g + q
                            o = lambda h: BK[h, 2 + 3 * g, C * q:C * q + C]
                            for h in HEADS:
                                mm(o(h), KR[h, p, 0, :], SS0[h, p, :], True, False)
                            for h in HEADS:
                                x = mm(o(h), MQA[h, p, 1, 0, :], VT[h, p, :], False, True)
                        x.then_inc(S(f"g_mm{g}"), 1)
                    for g in range(2):
                        pe.wait_ge(S(f"g_cp{g}"), c + 1)
                        own_wait()
                        for q in range(G3):
                            p = G3 * g + q
                            for e in range(2):
                                h = slice(64 * e, 64 * e + 64)
                                x = mm(BK[h, 3 + 3 * g, C * q:C * q + C], XT[h, p, e, :], NG[h, p, :])
                        x.then_inc(S(f"sa_mm{g}"), 1)
                    for g in range(2):
                        pe.wait_ge(S(f"sa_cp{g}"), c + 1)
                        own_wait()
                        for q in range(G3):
                            p = G3 * g + q
                            y = lambda h: BK[h, 4 + 3 * g, C * q:C * q + C]
                            o = lambda h: BK[h, 2 + 3 * g, C * q:C * q + C]
                            for h in HEADS:
                                mm(y(h), SS0[h, p, :], KR[h, p, 1, :], True, False)
                            for h in HEADS:
                                mm(y(h), SA[h, p, :], MQA[h, p, 0, 1, :], False, False)
                            for h in HEADS:
                                x = mm(y(h), VT[h, p, :], MQA[h, p, 1, 1, :], False, True)
                            if not short:
                                for h in HEADS:
                                    mm(o(h), BKT[h, p, 0, :], SA[h, p, :], True, False)
                                for h in HEADS:
                                    x = mm(o(h), BKT[h, p, 1, :], VT[h, p, :], False, True)
                        x.then_inc(S(f"y_mm{g}"), 1)
                rounds(pe, CHUNKS, chunk, first=True)

                pe.wait_ge(S("post_in"), 16 * 6)
                for i in range(2):
                    for t in range(2):
                        x = pe.transpose(BK[:, 0, P * (2 * i + t):P * (2 * i + t) + P],
                                         CRAW[:, i, t, :, :], IDENT[:, :])
                x.then_inc(S("c_t"), 1)
                pe.wait_ge(S("y_out0"), CHUNKS)
                pe.wait_ge(S("y_out1"), CHUNKS)
                for m in range(PAIRS):
                    if some(m - 1):
                        pe.wait_ge(S("gn_d"), m - 1)
                    for h in range(2):
                        x = mm(BK[:, 4 + 2 * (m % 2) + h, 0:HT], BONES64[:, :], KK[:, m, h * HT:h * HT + HT])
                    x.then_inc(S("gn_mean"), 1)

                def states_out(t):
                    for h in range(2):
                        n = 0
                        for jj in range(4):
                            for i in range(2):
                                x = mm(BK[:, 2 - 2 * t + h, 0:HT], WC[:, i, 4 * t + jj, :],
                                       U[:, i, 4 * t + jj, h * HT:h * HT + HT], n == 0, n == 7)
                                n += 1
                    x.then_inc(S("s5_ymm"), 1)

                def variance(m):
                    pe.wait_ge(S("gn_sq"), m + 1)
                    if some(m - 1):
                        pe.wait_ge(S("gn_ln"), m - 1)
                    for h in range(2):
                        x = mm(BK[:, 4 + 2 * (m % 2) + h, 0:HT], BONES64[:, :], AA[:, m, h * HT:h * HT + HT])
                    x.then_inc(S("gn_var"), 1)
                pe.wait_ge(S("wc"), 2)
                pe.wait_ge(S("s5_out"), 2 * N_STATE_TILES)
                states_out(0)
                pe.wait_ge(S("gn_d"), PAIRS)
                for m in range(PAIRS):
                    variance(m)
                states_out(1)
                pe.wait_ge(S("s5_gelu"), 2)
                for t in range(2):
                    for h in range(2):
                        for k in range(2):
                            x = mm(BK[:, 2 - 2 * t + h, 0:HT], GLW[:, k, P * t:P * t + P], UIN[:, k, h * HT:h * HT + HT],
                                   k == 0, k == 1)
                    x.then_inc(S("glu_mm"), 1)
                pe.wait_ge(S("gn_ln"), PAIRS)
                for m in range(PAIRS):
                    if some(m - 1):
                        pe.wait_ge(S("mx"), m - 1)
                    for h in range(2):
                        x = mm(BK[:, 4 + 2 * (m % 2) + h, 0:HT], G2[:, P * m:P * m + P], RKV[:, 19, h * HT:h * HT + HT])
                    x.then_inc(S("gate_mm"), 1)
                gemm("out0")
            if "ffn0" in stages:
                gemm("up0")
                gemm("down0")
            if "fox" in stages:
                q0 = at["in1"][1]

                def qk_sum(u, b):
                    pe.wait_ge(S("fx_sq"), u + 1)
                    if some(u - 1):
                        pe.wait_ge(S("fx_ln"), u - 1)
                    for h in range(2):
                        x = mm(BK[:, b + h, 0:HT], BONES64[:, :], FSQ[:, (b - 4) // 2, h * HT:h * HT + HT])
                    x.then_inc(S("fx_sum"), 1)

                def projections(i, sums=True):
                    for s in range(2):
                        unit("in1", i, s, q0 + 2 * i + s, s, True, True)
                        if sums:
                            qk_sum(2 * i - 2 + s, 4 + 2 * s)
                first_pair("in1")
                pe.wait_ge(S("wf_lo"), 1)
                for h in range(2):
                    n = 0
                    for k in range(KD):
                        for w, x_part in ((WFH, XNH), (WFH, XNL), (WFL, XNH)):
                            x = mm(BK[0:16, 4 + h, 0:HT], w[:, k, :], x_part[:, k, h * HT:h * HT + HT],
                                   n == 0, n == 3 * KD - 1)
                            n += 1
                x.then_inc(S("f_mm"), 1)
                pe.wait_ge(S("f_rd"), 1)
                projections(1)
                with pe.Fori(2, 9) as i:
                    projections(i)
                with pe.Fori(9, 12) as i:
                    projections(i, sums=False)
                pe.wait_ge(S("fx_const"), 3)
                pe.wait_ge(S("ps_free"), q0 + 24)
                pe.wait_ge(S("fx_ln"), 16)

                def scores(i, j):
                    if j == 0:
                        pe.wait_ge(S("fx_k"), i + 1)
                    if some(NQ * i + j - BANKS_BACK[j] + 1):
                        pe.wait_ge(S("fx_ss"), NQ * i + j - BANKS_BACK[j] + 1)
                    b = 2 * SLOT[j]
                    lo, n = TILES[j]
                    w = n - lo
                    m = min(n, 512)
                    c = 0 if j else 512 - w
                    for e in range(2):
                        mm(BK[0:w, b + e, c:c + m], QZ[:, e, lo:n], KS[:, 0:m], True, False)
                        x = mm(BK[0:w, b + e, c + lo:c + m], IDENT[:, 0:w], CM[:, 0:m - lo], False, True)
                    if n > m:
                        pe.wait_ge(S("fx_vs"), i + 1)
                        for e in range(2):
                            mm(BK[0:w, 6 + e, 0:n - m], QZ[:, e, lo:n], KS[:, m:n], True, False)
                            x = mm(BK[0:w, 6 + e, 0:n - m], IDENT[:, 0:w], CM[:, m - lo:w], False, True)
                    x.then_inc(S("fx_s"), 1)

                def turn(i, j):
                    pe.wait_ge(S("fx_d"), NQ * i + j + 1)
                    if some(NQ * i + j):
                        pe.wait_ge(S("fx_pt"), NQ * i + j)
                    if j == 0:
                        own_wait()
                    w = TILES[j][1] - TILES[j][0]
                    c = 0 if j else 512
                    for e in range(2):
                        for k in range(j + 1):
                            k0, k1 = TILES[k]
                            if k:
                                o = BK[:, 4 + e, P * (k - 1):P * k]
                            elif j < NQ - 1:
                                o = BK[0:N_META, 4 + e, 512 - P:512 - P + w]
                            else:
                                o = BK[0:N_META, 2 + e, 0:P]
                            x = pe.transpose(o, PR[0:w, SLOT[j], e, c + k0:c + k1], IDENT[0:w, 0:w])
                    x.then_inc(S("fx_t"), 1)

                def values(i):
                    pe.wait_ge(S("fx_vf"), i + 1)
                    if some(i):
                        pe.wait_ge(S("fx_oc"), i)
                    for k, (lo, n) in enumerate(TILES):
                        o = BK[:, 6, P * (k - 1):P * k] if k else BK[0:N_META, 7, 0:P]
                        x = pe.transpose(o, VF[:, lo:n], IDENT[:, :])
                    x.then_inc(S("fx_vt"), 1)

                def mix(i, b):
                    if b == 0:
                        pe.wait_ge(S("fx_ss"), NQ * i + NQ)
                    pe.wait_ge(S("fx_pt"), NQ * i + (NQ if b else 3))
                    blocks = [k for k in range(NQ) if TILES[k][0] < HT * (b + 1)]
                    for k in blocks:
                        lo = max(TILES[k][0], HT * b)
                        w = TILES[k][1] - TILES[k][0]
                        for h in HEADS:
                            x = mm(BK[h, 6 + b, lo - HT * b:HT], VS[0:w, k, h],
                                   PTT[0:w, h.start // 64, k, lo:HT * (b + 1)], k == 0, k == blocks[-1])
                    if b:
                        x.then_inc(S("fx_o"), 1)

                def pair(i):
                    last = isinstance(i, int) and i == FOX_PAIRS - 1
                    for j in range(NQ):
                        if j < NQ - 2:
                            scores(i, j + 2)
                        turn(i, j)
                        if j == 0:
                            values(i)
                        if j == NQ - 2:
                            mix(i, 0)
                        if j >= NQ - 2 and not last:
                            scores(i + 1, j - NQ + 2)
                    mix(i, 1)
                scores(0, 0)
                scores(0, 1)
                rounds(pe, FOX_PAIRS, pair, first=True)
                gemm("out1")
            if "ffn1" in stages:
                gemm("up1")
                gemm("down1")
            if some(n_groups):
                pe.wait_ge(S("ps_free"), n_groups)
            for j in range(4):
                for b in range(2):
                    i = 2 * j + b
                    if some(i - 1):
                        pe.wait_ge(S("o_cp"), i - 1)
                    for k in range(4):
                        t0 = N_META + P * j
                        x = pe.transpose(BK[:, 4 + i % 2, P * k:P * k + P], H[:, 4 * b + k, t0:t0 + P], IDENT[:, :])
                    x.then_inc(S("o_t"), 1)

        @block.scalar
        def _(act):
            act.dma_start(XIN[0:N_META, 0, :], a["meta_tokens"]).then_inc(S("x_in"), 16)
            for j in range(4):
                act.dma_start(XIN[:, 1 + j, :], a["x"][0, P * j:P * j + P, :]).then_inc(S("x_in"), 16)

            def fn(o, i, f, **kw):
                return nc.scalar.activation(o, i, f, **kw)

            def split(g, i, s):
                u0, _, _, k = at[g]
                u = u0 + 2 * i + s
                act.wait_ge(S(f"w_in{s}"), 16 * (u0 // 2 + i + 1))
                if some(u - 1):
                    act.wait_ge(S("w_used"), u - 1)
                fn(WHI[:, s, 0:k, :], RAW[:, s, 0:k, :], ACT.Copy).then_inc(S("w_hi"), 1)

            def square(n, k, slot, h_done):
                if some(h_done):
                    act.wait_ge(S("ps_free"), h_done)
                if some(KD * n + k - 1):
                    act.wait_ge(S("sq_used"), KD * n + k - 1)
                fn(SQ[:, slot:slot + 1, :], H[:, ds(k, 1), :], ACT.Square).then_inc(S("sq"), 1)

            def norm(g):
                n = norm_of[g]
                if g == order[0]:
                    for k in range(KD):
                        square(n, k, k % 2, 0)
                    split(g, 0, 0)
                split(g, 0, 1)
                act.wait_ge(S("sq_used"), KD * n + KD)
                fn(RST[:, :, :], bk(4, 2), ACT.Ln, scale=1.0 / D_MODEL, bias=EPS[:, 0:1]).then_inc(S("rms"), 1)
                act.wait_ge(S("rms"), 2 * n + 1)
                fn(RST[:, :, :], RST[:, :, :], ACT.Exp, scale=-0.5).then_inc(S("rms"), 1)
                for k in range(KD):
                    act.wait_ge(S("nt"), KD * n + k + 1)
                    fn(XNH[:, k, :], NT[:, k % 2, :], ACT.Copy).then_inc(S("nt_hi"), 1)

            def gemm(g, evac, late=None):
                n = at[g][2] // 2

                def body(i):
                    last = isinstance(i, int) and i == n - 1
                    if not (g in norm_of and not some(i)):
                        split(g, i, 1)
                    if late and some(i):
                        late(i - 1)
                    evac(i, 0)
                    if not last:
                        split(g, i + 1, 0)
                    elif after[g]:
                        split(after[g], 0, 0)
                    evac(i, 1)
                rounds(act, n, body, first=True)
                if late:
                    late(n - 1)

            def squares(g):
                h0 = h_ready[g] - KD
                n = norm_of.get(after[g])

                def evac(i, s):
                    if n is not None:
                        square(n, 2 * i + s, s, h0 + 2 * i + s + 1)
                return evac

            def down(g):
                h0 = h_ready[g] - KD
                n = norm_of.get(after[g])

                def body(ii):
                    for r in range(2):
                        i = 2 * ii + r
                        split(g, i, 1)
                        if not (isinstance(i, int) and i == KD - 1):
                            split(g, i + 1, 0)
                        elif after[g]:
                            split(after[g], 0, 0)
                        if n is not None:
                            square(n, i, r, h0 + i + 1)
                rounds(act, KD // 2, body, first=True)

            def up(l):
                g = f"up{l}"
                u0 = at[g][0]
                uc = 2 * KF * l if "ffn0" in stages else 0
                mc = uc // 2

                def evac(i, s):
                    act.wait_ge(S("w_used"), u0 + 2 * i + s + 1)
                    if some(uc + 2 * i + s - 1):
                        act.wait_ge(S("conv"), uc + 2 * i + s - 1)
                    if s == 0:
                        if some(mc + i):
                            act.wait_ge(S("mlp_mul"), mc + i)
                    src = bk(2 * s, 2)
                    fn(halves(CP[:, s, 2:T + 2]), src, ACT.Copy)
                    col = PC_CONV + CONV_COLS * l + KF * s + i
                    fn(halves(CA[:, s, :]), src, ACT.Identity, scale=PRM[:, ds(col + 4 * KF, 1)],
                       bias=PRM[:, ds(col + 6 * KF, 1)]).then_inc(S("ps_free"), 1)

                def late(i):
                    act.wait_ge(S("conv"), uc + 2 * i + 1)
                    fn(SG[:, :], CA[:, 0, :], ACT.Silu).then_inc(S("silu"), 1)
                    act.wait_ge(S("mlp_mul"), mc + i + 1)
                    fn(GH[:, ds(i, 1), :], GT[:, :].unsqueeze(1), ACT.Copy).then_inc(S("mlp_hi"), 1)
                gemm(g, evac, late)

            for j in range(5):
                n, t0 = (N_META, 0) if j == 0 else (P, N_META + P * (j - 1))
                act.wait_ge(S("x_t1"), j + 1)
                fn(H[:, 4:8, t0:t0 + n], BK[:, 3, :].rearrange("p (k t) -> p k t", k=4)[:, :, 0:n], ACT.Copy)\
                    .then_inc(S("x_out1"), 1)
            for b in range(2):
                act.wait_ge(S(f"x_out{b}"), 5)
            act.wait_ge(S("consts"), 2)
            if "mix0" in stages:
                norm("in0")

                def evac(i, s):
                    u = 2 * i + s
                    act.wait_ge(S("w_used"), u + 1)
                    if some(u - 1):
                        act.wait_ge(S("shift"), u - 1)
                    fn(halves(PB[:, s, 1:T + 1]), bk(2 * s, 2), ACT.Copy).then_inc(S("ps_free"), 1)

                def body(i):
                    if some(i):
                        split("in0", i, 1)
                    evac(i, 0)
                    split("in0", i + 1, 0)
                    evac(i, 1)
                act.wait_ge(S("pb0"), 1)
                body(0)
                v = lambda i: S5V[:, i, :]
                act.wait_ge(S("s5_ldt"), 1)
                fn(v(0), v(0), ACT.Exp).then_inc(S("s5_mag"), 1)
                body(1)
                act.wait_ge(S("s5_ph"), 1)
                fn(MAG[:, :], v(1), ACT.Exp).then_inc(S("s5_mag"), 1)
                fn(v(4), v(4), ACT.Sin).then_inc(S("s5_mag"), 1)
                fn(v(5), v(5), ACT.Sin).then_inc(S("s5_mag"), 1)
                with act.Fori(2, 10) as i:
                    body(i)
                split("in0", 10, 1)
                act.wait_ge(S("shift"), 20)
                fn(RKV[0:LORA, 18, 0:T], RKV[0:LORA, 18, 0:T], ACT.Tanh).then_inc(S("lora_act"), 1)
                for m in range(PAIRS):
                    act.wait_ge(S("kk_raw"), m + 1)
                    fn(SIG[:, m, 0:T], KK[:, m, 0:T], ACT.Square).then_inc(S("kk_sq"), 1)
                for s in range(2):
                    act.wait_ge(S("w_used"), 21 + s)
                    fn(halves(UIN[:, s, :]), bk(2 * s, 2), ACT.Copy).then_inc(S("ps_free"), 1)
                act.wait_ge(S("kk_max"), PAIRS)
                pp = PP[:, :, :, :].rearrange("p a b c -> p (a b c)")[:, 0:PAIRS * T].rearrange("p (m t) -> p m t", t=T)
                fn(pp, pp, ACT.Ln, scale=LN_SHIFT).then_inc(S("kk_rn"), 1)
                act.wait_ge(S("kk_rn"), 1)
                fn(pp, pp, ACT.Exp, scale=-0.5, bias=EPS[:, 2:3]).then_inc(S("kk_rn"), 1)
                for n in range(2 * PAIRS):
                    m, i = divmod(n, 2)
                    act.wait_ge(S("lora_mm"), n + 1)
                    fn(halves((AA if i else SIG)[:, m, 0:T]), bk(2 * (n % 2), 2), ACT.Sigmoid,
                       bias=PRM[:, (PC_A0 if i else PC_W0) + m:(PC_A0 if i else PC_W0) + m + 1]).then_inc(S("lora_cp"), 1)
                fn(RKV[:, 19, 0:T], RKV[:, 19, 0:T], ACT.Sigmoid)
                act.wait_ge(S("cs"), PAIRS)
                act.wait_ge(S("kkn"), 2)
                act.wait_ge(S("cleared"), 7)
                csv = CS[:, :, :].rearrange("p m (c t) -> p m c t", t=C)
                for m in range(PAIRS):
                    fn(PP[:, m, :, 1:C + 1], csv[:, m], ACT.Exp, scale=-DECAY).then_inc(S("dec"), 1)
                act.wait_ge(S("dec"), PAIRS)
                fn(CS[:, :, :], CS[:, :, :], ACT.Exp, scale=DECAY).then_inc(S("dec"), 1)

                act.wait_ge(S("masks"), 5)
                for n in range(16):
                    j, i = divmod(n, 2)
                    act.wait_ge(S("s5_bum"), n + 1)
                    fn(halves(U[:, i, j, :]), bk(4 + 2 * (n % 2), 2), ACT.Copy).then_inc(S("s5_ucp"), 1)
                act.wait_ge(S("s5_ucp"), 16)
                def stage(c):
                    for e in range(2):
                        h = slice(64 * e, 64 * e + 64)
                        fn(BHD[h, :, e, :], AA[h, :, ds(c * C, C)], ACT.Copy)
                        fn(KHD[h, :, e, :], RKV[h, PAIRS:2 * PAIRS, ds(c * C, C)], ACT.Copy)
                    fn(VH[:, :, :], RKV[:, 2 * PAIRS:3 * PAIRS, ds(c * C, C)], ACT.Copy).then_inc(S("bv_stage"), 1)

                def chunk(c):
                    short = isinstance(c, int) and c == CHUNKS - 1
                    for p in range(PAIRS):
                        act.wait_ge(S("ph_dve"), PAIRS * c + p + 1)
                        ph = BK[:, p % 2, :]
                        fn(BKT[:, p, :, :], ph[:, 0:384].rearrange("p (a b t) -> p a b t", a=2, b=3)[:, :, 2, :],
                           ACT.Copy)
                        fn(VT[:, p, :], ph[:, 384:448], ACT.Copy).then_inc(S("ph_out"), 1)
                        if p >= PAIRS - 2:
                            g = p - PAIRS + 2
                            act.wait_ge(S(f"xx_mm{g}"), 5 * c + 1)
                            fn(XX[:, G3 * g:G3 * g + G3].rearrange("p q e t -> p q (e t)"),
                               BK[:, 3 + 3 * g, 0:G3 * P].rearrange("p (q t) -> p q t", t=P), ACT.Copy)\
                                .then_inc(S(f"x_up{g}"), 1)
                    if not short:
                        act.wait_ge(S("ph"), PAIRS * c + PAIRS)
                        stage(c + 1)
                    levels = 3 if short else 5
                    for n in range(levels):
                        for g in range(2):
                            q = slice(G3 * g, G3 * g + G3)
                            fl = lambda t: t[:, q].rearrange("p q e t -> p q (e t)")
                            pq = lambda b: BK[:, b + 3 * g, 0:G3 * P].rearrange("p (q t) -> p q t", t=P)
                            if n < levels - 1:
                                act.wait_ge(S(f"xx_mm{g}"), 5 * c + n + 2)
                                fn(fl(XX), pq(3), ACT.Copy, scale=-1.0).then_inc(S(f"x_up{g}"), 1)
                            act.wait_ge(S(f"x_mm{g}"), 5 * c + n + 1)
                            fn(fl(XT), pq(4), ACT.Copy, scale=-1.0).then_inc(S(f"xt_up{g}"), 1)
                    for g in range(2):
                        q = slice(G3 * g, G3 * g + G3)
                        act.wait_ge(S(f"g_mm{g}"), c + 1)
                        fn(NG[:, q, :], BK[:, 2 + 3 * g, 0:G3 * C].rearrange("p (q t) -> p q t", t=C), ACT.Copy,
                           scale=-1.0).then_inc(S(f"g_cp{g}"), 1)
                    for g in range(2):
                        q = slice(G3 * g, G3 * g + G3)
                        act.wait_ge(S(f"sa_mm{g}"), c + 1)
                        fn(SA[:, q, :], BK[:, 3 + 3 * g, 0:G3 * C].rearrange("p (q t) -> p q t", t=C),
                           ACT.Copy).then_inc(S(f"sa_cp{g}"), 1)
                    for g in range(2):
                        q = slice(G3 * g, G3 * g + G3)
                        act.wait_ge(S(f"y_mm{g}"), c + 1)
                        fn(KK[:, q, ds(c * C, C)], BK[:, 4 + 3 * g, 0:G3 * C].rearrange("p (q t) -> p q t", t=C),
                           ACT.Copy).then_inc(S(f"y_out{g}"), 1)
                act.wait_ge(S("tilde"), 1)
                act.wait_ge(S("chunk_init"), 2 * PAIRS)
                act.wait_ge(S("b_ops"), 2 * PAIRS)
                stage(0)
                rounds(act, CHUNKS, chunk, first=True)

                for m in range(PAIRS):
                    act.wait_ge(S("gn_d"), m + 1)
                    fn(AA[:, m, 0:T], KK[:, m, 0:T], ACT.Square).then_inc(S("gn_sq"), 1)
                for m in range(PAIRS):
                    act.wait_ge(S("gn_var"), m + 1)
                    fn(halves(RS6[:, m, :]), bk(4 + 2 * (m % 2), 2), ACT.Ln, bias=EPS[:, 1:2]).then_inc(S("gn_ln"), 1)
                act.wait_ge(S("gn_ln"), PAIRS)
                for m in range(PAIRS):
                    fn(RS6[:, m, :], RS6[:, m, :], ACT.Exp, scale=-0.5).then_inc(S("gn_rs"), 1)
                for t in range(2):
                    act.wait_ge(S("s5_y"), t + 1)
                    fn(UIN[:, t, :], UIN[:, t, :], ACT.Gelu_apprx_tanh).then_inc(S("s5_gelu"), 1)

                def mixed(k):
                    act.wait_ge(S("mx"), k + 1)
                    fn(XNH[:, k, :], PT2[:, k % 2, :], ACT.Copy).then_inc(S("mx_hi"), 1)
                for t in range(2):
                    act.wait_ge(S("glu_mm"), t + 1)
                    fn(halves(GLS[:, t, :]), bk(2 - 2 * t, 2), ACT.Sigmoid, bias=PRM[:, PC_GLB + t:PC_GLB + t + 1])\
                        .then_inc(S("glu_sg"), 1)
                for k in range(KD):
                    mixed(k)
                split("out0", 0, 0)
                gemm("out0", squares("out0"))
            if "ffn0" in stages:
                norm("up0")
                up(0)
                down("down0")
            if "fox" in stages:
                norm("in1")
                u0 = at["in1"][0]

                def evac(i, s):
                    act.wait_ge(S("w_used"), u0 + 2 * i + s + 1)
                    fn(QKV[:, ds(2 * i + s, 1), :].rearrange("p o (a b) -> p (o a) b", a=2), bk(2 * s, 2), ACT.Copy)\
                        .then_inc(S("ps_free"), 1)

                def own_wait():
                    act.sem_inc(S("own_wait"), 1)

                def inverse_rms(i):
                    for s in range(2):
                        act.wait_ge(S("fx_sum"), 2 * i + s + 1)
                        fn(FRS[:, ds(2 * i + s, 1), :].rearrange("p o (a b) -> p (o a) b", a=2), bk(4 + 2 * s, 2),
                           ACT.Ln, bias=EPS[:, 0:1]).then_inc(S("fx_ln"), 1)
                    act.wait_ge(S("fx_ln"), 2 * i + 2)
                    own_wait()
                    fn(FRS[:, ds(2 * i, 2), :], FRS[:, ds(2 * i, 2), :], ACT.Exp, scale=-0.5).then_inc(S("fx_rs"), 1)

                def body(i, squares=True, sums=True, more=True):
                    for s in range(2):
                        u = 2 * i + s
                        if s == 0:
                            if some(i):
                                split("in1", i, 1)
                            if sums:
                                inverse_rms(i - 2)
                        elif more:
                            split("in1", i + 1, 0)
                        evac(i, s)
                        if squares:
                            act.wait_ge(S("ps_free"), at["in1"][1] + u + 1)
                            if some(u - 1):
                                act.wait_ge(S("fx_sum"), u - 1)
                            own_wait()
                            fn(FSQ[:, s:s + 1, :], QKV[:, ds(u, 1), :], ACT.Square).then_inc(S("fx_sq"), 1)
                act.wait_ge(S("wf_in"), 32)
                fn(WFH[:, :, :], WF[:, :, :], ACT.Copy).then_inc(S("wf_hi"), 1)
                body(0, sums=False)
                body(1, sums=False)
                act.wait_ge(S("f_rd"), 2)
                fn(CUM[0:16, 1, :], CUM[0:16, 1, :], ACT.Exp, scale=-1.0).then_inc(S("f_act"), 1)
                act.wait_ge(S("f_act"), 1)
                fn(CUM[0:16, 1, :], CUM[0:16, 1, :], ACT.Ln, bias=ONES[0:16, 0:1]).then_inc(S("f_act"), 1)
                with act.Fori(2, 8) as i:
                    body(i)
                for i in (8, 9):
                    body(i, squares=False)
                body(10, squares=False, sums=False)
                body(11, squares=False, sums=False, more=False)

                def exps(i, j):
                    lo, n = TILES[j]
                    w = n - lo
                    c = 0 if j else 512
                    act.wait_ge(S("fx_mx"), NQ * i + j + 1)
                    if some(NQ * i + j - COLS_BACK[j] + 1):
                        act.wait_ge(S("fx_t"), NQ * i + j - COLS_BACK[j] + 1)
                    for e in range(2):
                        x = fn(PR[0:w, SLOT[j], e, c:c + n], SS[0:w, SLOT[j], e, c:c + n], ACT.Exp,
                               bias=MX[0:w, j, e:e + 1], accum_out=SM[0:w, j, e:e + 1])
                    x.then_inc(S("fx_e"), 1)

                def out_pt(i, j):
                    act.wait_ge(S("fx_t"), NQ * i + j + 1)
                    lo, n = TILES[j]
                    w = n - lo
                    if j == 0 and some(i):
                        act.wait_ge(S("fx_o"), i)
                    if j:
                        fn(PTT[:, :, 1:j + 1, lo:n], BK[:, 4:6, 0:P * j].rearrange("p e (k t) -> p e k t", t=P), ACT.Copy)
                    meta = BK[0:N_META, 4:6, 512 - P:512 - P + w] if j < NQ - 1 else BK[0:N_META, 2:4, 0:P]
                    fn(PTT[0:N_META, :, 0, lo:n], meta, ACT.Copy).then_inc(S("fx_pt"), 1)

                def out(i):
                    act.wait_ge(S("fx_o"), i + 1)
                    if some(i):
                        act.wait_ge(S("x_lo"), x_ready["out1"] - KD + i)
                    fn(halves(OT[:, :]), bk(6, 2), ACT.Copy).then_inc(S("fx_oc"), 1)
                    act.wait_ge(S("fx_oc"), i + 1)
                    fn(XNH[:, ds(i, 1), :], OT[:, :].unsqueeze(1), ACT.Copy).then_inc(S("ot_hi"), 1)

                def pair(i):
                    last = isinstance(i, int) and i == FOX_PAIRS - 1
                    for j in range(NQ):
                        if j < NQ - 2:
                            exps(i, j + 1)
                        if j == 0 and some(i):
                            out(i - 1)
                        out_pt(i, j)
                        if j == NQ - 2:
                            exps(i, j + 1)
                        elif j == NQ - 1 and not last:
                            exps(i + 1, 0)
                        if j == 0:
                            act.wait_ge(S("fx_vt"), i + 1)
                            fn(VS[:, 1:NQ, :], BK[:, 6, :].rearrange("p (k t) -> p k t", t=P), ACT.Copy)
                            fn(VS[0:N_META, 0, :], BK[0:N_META, 7, 0:P], ACT.Copy).then_inc(S("fx_vs"), 1)
                exps(0, 0)
                rounds(act, FOX_PAIRS, pair, first=True)
                out(FOX_PAIRS - 1)
                split("out1", 0, 0)
                gemm("out1", squares("out1"))
            if "ffn1" in stages:
                norm("up1")
                up(1)
                down("down1")
            for i in range(1, 8, 2):
                act.wait_ge(S("o_t"), i + 1)
                act.wait_ge(S("o_cp"), i)
                fn(OUTB[:, i // 2, 512:1024], BK[:, 5, :], ACT.Copy).then_inc(S("o_cp"), 1)

        @block.vector
        def _(ve):
            od = Order(ve, "ve_order")

            def step(ins):
                od.done(ins)
                od.settle()

            def tt(o, x, y, op):
                return nc.vector.tensor_tensor(o, x, y, op)

            def ts(o, x, s1, s2, op0, op1=None):
                return nc.vector.tensor_scalar(o, x, s1, s2, op0, op1) if op1 is not None else \
                    nc.vector.tensor_scalar(o, x, s1, s2, op0)

            def stt(o, x, s, y, op0, op1):
                return nc.vector.scalar_tensor_tensor(out=o, in0=x, scalar=s, in1=y, op0=op0, op1=op1)

            def f32(ap):
                return ap.bitcast(F32)

            def split(g, i, s):
                u0, _, _, k = at[g]
                ve.wait_ge(S("w_hi"), u0 + 2 * i + s + 1)
                tt(WLO[:, s, 0:k, :], RAW[:, s, 0:k, :], f32(WHI[:, s, 0:k, :]), ALU.subtract).then_inc(S("w_lo"), 1)

            def norm(g, col):
                n = norm_of[g]
                x0 = x_ready[g] - KD
                if g == order[0]:
                    split(g, 0, 0)
                split(g, 0, 1)
                ve.wait_ge(S("rms"), 2 * n + 2)

                def scaled(k):
                    if some(KD * n + k - 1):
                        ve.wait_ge(S("nt_hi"), KD * n + k - 1)
                    if some(x0 + k - 1):
                        ve.wait_ge(S("x_lo"), x0 + k - 1)
                    stt(NT[:, k % 2, :], H[:, k, :], PRM[:, col + k:col + k + 1], RST[:, :, :].rearrange("p a b -> p (a b)"),
                        ALU.mult, ALU.mult).then_inc(S("nt"), 1)
                scaled(0)
                for k in range(KD):
                    if k + 1 < KD:
                        scaled(k + 1)
                    ve.wait_ge(S("nt_hi"), KD * n + k + 1)
                    tt(XNL[:, k, :], NT[:, k % 2, :], f32(XNH[:, k, :]), ALU.subtract).then_inc(S("x_lo"), 1)

            def gemm(g, use, late=None):
                n = at[g][2] // 2

                def body(i):
                    last = isinstance(i, int) and i == n - 1
                    if not (g in norm_of and not some(i)):
                        split(g, i, 1)
                    if late and some(i):
                        late(i - 1)
                    use(i, 0)
                    if not last:
                        split(g, i + 1, 0)
                    elif after[g]:
                        split(after[g], 0, 0)
                    use(i, 1)
                rounds(ve, n, body, first=True)
                if late:
                    late(n - 1)

            def residual(g):
                u0, _, units, _ = at[g]
                h0 = h_ready[g] - KD
                if g.startswith("down"):
                    def body(ii, last=False):
                        for r in range(2):
                            i = 2 * ii + r
                            split(g, i, 1)
                            if not (last and r == 1):
                                split(g, i + 1, 0)
                            elif after[g]:
                                split(after[g], 0, 0)
                            ve.wait_ge(S("w_used"), u0 + 2 * i + 2)
                            hm = H[:, ds(i, 1), :].rearrange("p o (a b) -> p (o a) b", a=2)
                            tt(hm, hm, bk(2 * r, 2), ALU.add).then_inc(S("ps_free"), 1)
                    with ve.Fori(0, 3) as ii:
                        body(ii)
                    body(3, True)
                else:
                    def use(i, s):
                        ve.wait_ge(S("w_used"), u0 + 2 * i + s + 1)
                        hm = H[:, ds(2 * i + s, 1), :].rearrange("p o (a b) -> p (o a) b", a=2)
                        tt(hm, hm, bk(2 * s, 2), ALU.add).then_inc(S("ps_free"), 1)
                    gemm(g, use)

            def up(l):
                g = f"up{l}"
                uc = 2 * KF * l if "ffn0" in stages else 0
                mc = uc // 2
                x0 = x_ready[f"down{l}"] - KF
                ve.wait_ge(S("x_lo"), x_ready[g])
                ve.memset(CP[:, :, 0:2], 0.0).then_inc(S("cp0"), 1)
                ve.wait_ge(S("cp0"), l + 1 if "ffn0" in stages else 1)

                def use(i, s):
                    n = uc + 2 * i + s
                    q = at[g][1] + 2 * i + s
                    ve.wait_ge(S("ps_free"), q + 1)
                    col = PC_CONV + CONV_COLS * l + KF * s + i
                    stt(CA[:, s, :], CP[:, s, 1:T + 1], PRM[:, ds(col + 2 * KF, 1)], CA[:, s, :], ALU.mult, ALU.add)\
                        .then_inc(S("conv_a"), 1)
                    ve.wait_ge(S("conv_a"), n + 1)
                    stt(CA[:, s, :], CP[:, s, 0:T], PRM[:, ds(col, 1)], CA[:, s, :], ALU.mult, ALU.add)\
                        .then_inc(S("conv"), 1)

                def late(i):
                    ve.wait_ge(S("silu"), mc + i + 1)
                    ve.wait_ge(S("conv"), uc + 2 * i + 2)
                    ve.wait_ge(S("x_lo"), x0 + i)
                    tt(GT[:, :], SG[:, :], CA[:, 1, :], ALU.mult).then_inc(S("mlp_mul"), 1)
                    ve.wait_ge(S("mlp_hi"), mc + i + 1)
                    gm = GH[:, ds(i, 1), :]
                    tt(GL[:, ds(i, 1), :], GT[:, :].unsqueeze(1), f32(gm), ALU.subtract).then_inc(S("x_lo"), 1)
                gemm(g, use, late)

            for j in range(5):
                n, t0 = (N_META, 0) if j == 0 else (P, N_META + P * (j - 1))
                ve.wait_ge(S("x_t0"), j + 1)
                ve.tensor_copy(H[:, 0:4, t0:t0 + n], BK[:, 2, :].rearrange("p (k t) -> p k t", k=4)[:, :, 0:n])\
                    .then_inc(S("x_out0"), 1)
            ve.wait_ge(S("prm_in"), 16 * (N_PRM_LOADS + 1))
            ve.tensor_copy(PRAW[0:8, 5, :].rearrange("p (g n) -> p g n", g=2),
                           S5V[0:8, 15, 0:2].unsqueeze(2).to_broadcast([8, 2, 64])).then_inc(S("ldt"), 1)
            ve.wait_ge(S("prm_t"), 1)
            col = 0
            for t, n in enumerate((114, 88, 88, 88, 88)):
                od.done(ve.tensor_copy(PRM[:, col:col + n], BK[:, t // 4, P * (t % 4):P * (t % 4) + n]))
                col += n
            ve.tensor_copy(S5V[:, 0, :], BK[:, 1, P:P + 8]).then_inc(S("s5_ldt"), 1)
            od.settle()
            ve.wait_ge(S("s5_ldt"), 1)
            for b in range(2):
                ve.wait_ge(S(f"x_out{b}"), 5)
            ve.wait_ge(S("consts"), 2)
            if "mix0" in stages:
                ve.memset(PB[:, :, 0:1], 0.0).then_inc(S("pb0"), 1)
                norm("in0", PC_MIX)
                ve.wait_ge(S("pb0"), 1)

                def use(i, s):
                    u = 2 * i + s
                    ve.wait_ge(S("ps_free"), u + 1)
                    tt(DT[:, s, :], PB[:, s, 0:T], PB[:, s, 1:T + 1], ALU.subtract).then_inc(S("diff"), 1)
                    ve.wait_ge(S("diff"), u + 1)
                    stt(RKV[:, ds(u, 1), 0:T], DT[:, s, :].unsqueeze(1), PRM[:, ds(PC_MU + u, 1)],
                        PB[:, s, 1:T + 1].unsqueeze(1), ALU.mult, ALU.add).then_inc(S("shift"), 1)

                def body(i):
                    if some(i):
                        split("in0", i, 1)
                    use(i, 0)
                    split("in0", i + 1, 0)
                    use(i, 1)
                v = lambda i: S5V[:, i, :]
                are, aim = PRM[:, PC_ARE:PC_ARE + 8], PRM[:, PC_AIM:PC_AIM + 8]
                cs, sn = v(5), v(4)

                def s5_phases():
                    ve.wait_ge(S("s5_mag"), 1)
                    step(tt(v(1), are, v(0), ALU.mult))
                    step(tt(v(2), aim, v(0), ALU.mult))
                    big = 1.5 * 2.0 ** 23
                    turn = 2 * math.pi
                    c1 = 6.28125
                    c2 = float.fromhex("0x1.fb4p-10")
                    c3 = turn - c1 - c2
                    for dst, quarter in ((4, 0.0), (5, 0.25)):
                        step(ts(v(3), v(2), 1.0 / turn, quarter, ALU.mult, ALU.add))
                        step(ts(v(3), v(3), big, None, ALU.add))
                        step(ts(v(3), v(3), big, None, ALU.subtract))
                        step(stt(v(dst), v(3), -c1, v(2), ALU.mult, ALU.add))
                        step(stt(v(dst), v(3), -c2, v(dst), ALU.mult, ALU.add))
                        step(stt(v(dst), v(3), -c3, v(dst), ALU.mult, ALU.add))
                        step(ts(v(dst), v(dst), quarter * turn, None, ALU.add))
                        x = ts(v(dst), v(dst), 3.1415925, -3.1415925, ALU.min, ALU.max)
                        if quarter:
                            x.then_inc(S("s5_ph"), 1)
                        else:
                            step(x)

                def s5_z():
                    ve.wait_ge(S("s5_mag"), 4)
                    step(tt(v(6), MAG[:, :], cs, ALU.mult))
                    step(tt(v(7), MAG[:, :], sn, ALU.mult))
                    step(ts(v(6), v(6), 1.0, None, ALU.subtract))
                    step(tt(v(8), are, are, ALU.mult))
                    step(tt(v(9), aim, aim, ALU.mult))
                    step(tt(v(8), v(8), v(9), ALU.add))
                    step(nc.vector.reciprocal(v(8), v(8)))
                    step(tt(v(9), v(6), are, ALU.mult))
                    step(tt(v(10), v(7), aim, ALU.mult))
                    step(tt(v(9), v(9), v(10), ALU.add))
                    step(tt(v(9), v(9), v(8), ALU.mult))
                    step(tt(v(10), v(7), are, ALU.mult))
                    step(tt(v(11), v(6), aim, ALU.mult))
                    step(tt(v(10), v(10), v(11), ALU.subtract))
                    step(tt(v(10), v(10), v(8), ALU.mult))
                    step(ve.tensor_copy(POW[:, :, 0, 0], cs))
                    step(ve.tensor_copy(POW[:, :, 0, 1], sn))

                def s5_powers(lo, hi):
                    for n in range(lo, hi):
                        step(tt(v(12), POW[:, :, n, 0], POW[:, :, n, 0], ALU.mult))
                        step(tt(v(13), POW[:, :, n, 1], POW[:, :, n, 1], ALU.mult))
                        step(tt(POW[:, :, n + 1, 0], v(12), v(13), ALU.subtract))
                        x = stt(POW[:, :, n + 1, 1], POW[:, :, n, 0], 2.0, POW[:, :, n, 1], ALU.mult, ALU.mult)
                        if n < 8:
                            step(x)
                        else:
                            x.then_inc(S("s5_pow"), 1)

                def s5_inputs():
                    ve.wait_ge(S("b_in"), 32)
                    zr = v(9).unsqueeze(2).to_broadcast([P, 8, 16])
                    zi = v(10).unsqueeze(2).to_broadcast([P, 8, 16])
                    t1 = BBM[:, 0, 0, :].rearrange("p (j c) -> p j c", c=16)
                    step(tt(BB[:, 0], BR[:, 0], zr, ALU.mult))
                    step(tt(t1, BR[:, 1], zi, ALU.mult))
                    step(tt(BB[:, 0], BB[:, 0], t1, ALU.subtract))
                    step(tt(BB[:, 1], BR[:, 1], zr, ALU.mult))
                    step(tt(t1, BR[:, 0], zi, ALU.mult))
                    step(tt(BB[:, 1], BB[:, 1], t1, ALU.add))
                    ve.wait_ge(S("mk"), 8)
                    for i in range(2):
                        for j in range(8):
                            x = tt(BBM[:, i, j, :].rearrange("p (s c) -> p s c", c=16),
                                   BB[:, i, j, :].unsqueeze(1).to_broadcast([P, 8, 16]),
                                   MK[:, j % 4, :].rearrange("p (s c) -> p s c", c=16), ALU.mult)
                    x.then_inc(S("bbm"), 1)

                body(0)
                s5_phases()
                body(1)
                body(2)
                s5_z()
                body(3)
                s5_powers(0, 5)
                body(4)
                s5_powers(5, 9)
                body(5)
                s5_inputs()
                with ve.Fori(6, 10) as i:
                    body(i)
                split("in0", 10, 1)
                ve.wait_ge(S("shift"), 20)
                for m in range(PAIRS):
                    ts(KK[:, m, 0:T], RKV[:, PAIRS + m, 0:T], PRM[:, PC_KK + m:PC_KK + m + 1], None, ALU.mult)\
                        .then_inc(S("kk_raw"), 1)
                ve.wait_ge(S("w_lo"), 22)
                for n in range(4):
                    i, jh = divmod(n, 2)
                    ve.wait_ge(S("wb_t"), n + 1)
                    ve.tensor_copy(WB[:, i, 4 * jh:4 * jh + 4, :], BK[:, 6 + n % 2, :].rearrange("p (j c) -> p j c", j=4))\
                        .then_inc(S("wb_cp"), 1)
                pp = PP[:, :, :, :].rearrange("p a b c -> p (a b c)")[:, 0:PAIRS * T].rearrange("p (m t) -> p m t", t=T)
                for m in range(PAIRS):
                    ve.wait_ge(S("kk_sum"), m + 1)
                    if m == 0:
                        ve.wait_ge(S("cleared"), 7)
                    ts(pp[:, m, :].rearrange("p (a b) -> p a b", a=2), bk(4 + 2 * (m % 2), 2), 1e-24, None, ALU.max)\
                        .then_inc(S("kk_max"), 1)
                ve.wait_ge(S("kk_rn"), 2)
                ve.wait_ge(S("kk_raw"), PAIRS)
                tt(KK[:, :, 0:T], KK[:, :, 0:T], pp, ALU.mult).then_inc(S("kkn"), 1)
                ve.wait_ge(S("kkn"), 1)
                ve.memset(PP[:, :, :, 0:1], 1.0).then_inc(S("kkn"), 1)
                ve.wait_ge(S("cleared"), 3)
                for m in range(PAIRS):
                    ve.wait_ge(S("lora_cp"), 2 * m + 1)
                    nc.vector.tensor_tensor_scan(CS[:, m, :], RESET[:, :], SIG[:, m, :], 0.0, ALU.mult, ALU.add)\
                        .then_inc(S("cs"), 1)
                ve.wait_ge(S("lora_cp"), 2 * PAIRS)
                om = FT1[:, 0:PAIRS]
                step(ts(om, PRM[:, PC_KA:PC_KA + PAIRS], -1.0, 1.0, ALU.mult, ALU.add))
                for m in range(PAIRS):
                    ts(SIG[:, m, 0:T], AA[:, m, 0:T], PRM[:, PC_KA + m:PC_KA + m + 1], FT1[:, m:m + 1],
                       ALU.mult, ALU.add).then_inc(S("k_mod"), 1)
                ve.wait_ge(S("k_mod"), PAIRS)
                step(tt(RKV[:, PAIRS:2 * PAIRS, 0:T], RKV[:, PAIRS:2 * PAIRS, 0:T], SIG[:, :, 0:T], ALU.mult))
                for m in range(PAIRS):
                    stt(SIG[:, m, 0:T], RKV[:, m, 0:T], PRM[:, PC_RK + m:PC_RK + m + 1], RKV[:, PAIRS + m, 0:T],
                        ALU.mult, ALU.mult).then_inc(S("rk"), 1)
                for m in range(PAIRS):
                    ve.wait_ge(S("bonus_mm"), m + 1)
                    tt(halves(SIG[:, m, 0:T]), bk(2 * (m % 2), 2), halves(RKV[:, 2 * PAIRS + m, 0:T]), ALU.mult)\
                        .then_inc(S("bonus"), 1)
                ve.wait_ge(S("dec"), PAIRS + 1)
                ve.wait_ge(S("kkn"), 2)
                for m in range(PAIRS):
                    r, k = RKV[:, m, :], RKV[:, PAIRS + m, :]
                    ve.wait_ge(S("b_ops"), m + 1)
                    c4 = lambda ap: ap.rearrange("p (c t) -> p c t", t=C)
                    od.done(tt(c4(KK[:, m, :]), c4(KK[:, m, :]), PP[:, m, :, 0:C], ALU.mult))
                    od.done(tt(c4(r), c4(r), PP[:, m, :, 1:C + 1], ALU.mult))
                    od.done(tt(k, k, CS[:, m, :], ALU.mult))
                od.settle()
                ve.tensor_copy(PCH[:, :, :], PP[:, :, :, C]).then_inc(S("tilde"), 1)

                ve.wait_ge(S("tilde"), 1)
                o0 = od.at
                PER = PAIRS + 2 + 2

                def stage(c, g):
                    q = slice(G3 * g, G3 * g + G3)
                    t = ds(c * C, C)
                    ve.tensor_copy(KR[:, q, 0, :], KK[:, q, t])
                    ve.tensor_copy(KR[:, q, 1, :], RKV[:, q, t]).then_inc(S(f"stage{g}"), 1)

                def chunk(c, s5):
                    short = isinstance(c, int) and c == CHUNKS - 1
                    od.at = o0 + PER * c
                    for p in range(PAIRS):
                        ve.wait_ge(S("ph"), PAIRS * c + p + 1)
                        ph = BK[:, p % 2, :]
                        two = lambda ap: ap.unsqueeze(1).to_broadcast([P, 2, C])
                        m2 = lambda t: t[:, :].rearrange("p (e t) -> p e t", e=2)
                        od.done(tt(AT[:, p], two(ph[:, 0:64]), m2(MU2), ALU.mult))
                        tt(MQA[:, p], ph[:, 0:384].rearrange("p (a b t) -> p a b t", a=2, b=3)[:, :, 0:2, :],
                           MQ[:, :, :].unsqueeze(1).to_broadcast([P, 2, 2, C]), ALU.mult).then_inc(S("ph_dve"), 1)
                        if p % G3 == G3 - 1:
                            g = p // G3
                            q = slice(G3 * g, G3 * g + G3)
                            fl = lambda t: t[:, q].rearrange("p q e t -> p q (e t)")
                            over = lambda t: t[:, :].unsqueeze(1).to_broadcast([P, G3, P])
                            od.settle()
                            step(tt(fl(AT), fl(AT), over(IDENT), ALU.subtract))
                            tt(fl(XT), fl(AT), over(M1T), ALU.mult).then_inc(S(f"xt_up{g}"), 1)
                    for n in range(3 if short else 5):
                        for g in range(2):
                            q = slice(G3 * g, G3 * g + G3)
                            fl = lambda t: t[:, q].rearrange("p q e t -> p q (e t)")
                            pq = lambda b: BK[:, b + 3 * g, 0:G3 * P].rearrange("p (q t) -> p q t", t=P)
                            ve.wait_ge(S(f"t_mm{g}"), 5 * c + n + 1)
                            tt(fl(TM), pq(2), LVL[:, n, :].unsqueeze(1).to_broadcast([P, G3, P]), ALU.mult)\
                                .then_inc(S(f"t_mask{g}"), 1)
                    if s5:
                        ve.wait_ge(S("s5_in"), 2 * c + 2)
                        for i in range(2):
                            u = U[:, i, ds(c, 1), :].rearrange("p a t -> p (a t)")
                            nc.vector.tensor_tensor_scan(u, MAG[:, ds(c, 1)].to_broadcast([P, T]), u, 0.0,
                                                         ALU.mult, ALU.add).then_inc(S("s5_scan"), 1)
                    for g in range(2):
                        if short:
                            continue
                        q = slice(G3 * g, G3 * g + G3)
                        ve.wait_ge(S(f"y_mm{g}"), c + 1)
                        od.done(tt(SS0[:, q, :], SS0[:, q, :],
                                   BK[:, 2 + 3 * g, 0:G3 * C].rearrange("p (q t) -> p q t", t=C), ALU.add))
                        od.settle()
                        tt(SS0[:, q, :], SS0[:, q, :], PCH[:, q, ds(c, 1)].to_broadcast([P, G3, C]), ALU.mult)\
                            .then_inc(S(f"state{g}"), 1)
                        stage(c + 1, g)
                ve.wait_ge(S("chunk_init"), 2 * PAIRS)
                for g in range(2):
                    stage(0, g)
                chunk(0, True)
                assert od.at == o0 + PER, (od.at, o0, PER)
                with ve.Fori(1, N_STATE_TILES) as c:
                    chunk(c, True)
                chunk(CHUNKS - 1, False)
                od.at = o0 + PER * CHUNKS - 2
                for g in range(2):
                    ve.wait_ge(S(f"y_out{g}"), CHUNKS)
                    ve.wait_ge(S(f"state{g}"), CHUNKS - 1)

                ve.wait_ge(S("c_t"), 1)
                ve.wait_ge(S("mk"), 16)
                for i in range(2):
                    for t in range(2):
                        x = stt(WC[:, i, 4 * t:4 * t + 4, :],
                                BK[:, 0, P * (2 * i + t):P * (2 * i + t) + P].unsqueeze(1).to_broadcast([P, 4, P]),
                                -1.0 if i else 1.0, MK2[:, :, :], ALU.mult, ALU.mult)
                    x.then_inc(S("wc"), 1)
                for m in range(PAIRS):
                    ve.wait_ge(S("gn_mean"), m + 1)
                    tt(halves(KK[:, m, 0:T]), halves(KK[:, m, 0:T]), bk(4 + 2 * (m % 2), 2), ALU.subtract)\
                        .then_inc(S("gn_d"), 1)
                for t in range(2):
                    ve.wait_ge(S("s5_ymm"), t + 1)
                    stt(halves(UIN[:, t, :]), halves(UIN[:, t, :]), PRM[:, PC_SD + t:PC_SD + t + 1], bk(2 - 2 * t, 2),
                        ALU.mult, ALU.add).then_inc(S("s5_y"), 1)
                for m in range(PAIRS):
                    ve.wait_ge(S("gn_rs"), m + 1)
                    stt(KK[:, m, 0:T], KK[:, m, 0:T], PRM[:, PC_LNW + m:PC_LNW + m + 1], RS6[:, m, :],
                        ALU.mult, ALU.mult).then_inc(S("gn_w"), 1)
                    ve.wait_ge(S("gn_w"), m + 1)
                    stt(KK[:, m, 0:T], KK[:, m, 0:T], PRM[:, PC_LNB + m:PC_LNB + m + 1], SIG[:, m, 0:T],
                        ALU.add, ALU.add).then_inc(S("gn_out"), 1)

                def mixed(k):
                    if some(k - 1):
                        ve.wait_ge(S("x_lo"), x_ready["out0"] - KD + k - 1)
                        ve.wait_ge(S("mx_hi"), k - 1)
                    if k < PAIRS:
                        ve.wait_ge(S("gate_mm"), k + 1)
                        ve.wait_ge(S("gn_out"), k + 1)
                        tt(halves(PT2[:, k % 2, :]), halves(KK[:, k, 0:T]), bk(4 + 2 * (k % 2), 2), ALU.mult)\
                            .then_inc(S("mx"), 1)
                    else:
                        t = k - PAIRS
                        ve.wait_ge(S("glu_sg"), t + 1)
                        tt(PT2[:, k % 2, :], GLS[:, t, :], UIN[:, t, :], ALU.mult).then_inc(S("mx"), 1)

                def mixed_low(k):
                    ve.wait_ge(S("mx_hi"), k + 1)
                    tt(XNL[:, k, :], PT2[:, k % 2, :], f32(XNH[:, k, :]), ALU.subtract).then_inc(S("x_lo"), 1)
                mixed(0)
                for k in range(KD):
                    if k + 1 < KD:
                        mixed(k + 1)
                    mixed_low(k)
                split("out0", 0, 0)
                residual("out0")
            if "ffn0" in stages:
                norm("up0", PC_FFN)
                up(0)
                residual("down0")
            if "fox" in stages:
                norm("in1", PC_MIX + KD)
                ve.wait_ge(S("wf_hi"), 1)
                tt(WFL[:, :, :], WF[:, :, :], f32(WFH[:, :, :]), ALU.subtract).then_inc(S("wf_lo"), 1)
                split("in1", 1, 0)
                ve.wait_ge(S("f_mm"), 1)
                ts(halves(CUM[0:16, 0, :]), BK[0:16, 4:6, 0:HT], BF[0:16, 0:1], None, ALU.add).then_inc(S("f_rd"), 1)
                ve.wait_ge(S("f_rd"), 1)
                step(ts(CUM[0:16, 1, :], CUM[0:16, 0, :], -1.0, None, ALU.mult))
                tt(CUM[0:16, 1, :], CUM[0:16, 1, :], CUM[0:16, 0, :], ALU.max).then_inc(S("f_rd"), 1)
                step(ts(CUM[0:16, 2, :], CUM[0:16, 0, :], 0.0, None, ALU.min))
                split("in1", 1, 1)
                split("in1", 2, 0)
                split("in1", 2, 1)
                split("in1", 3, 0)
                ve.wait_ge(S("f_act"), 2)
                step(tt(CUM[0:16, 1, :], CUM[0:16, 1, :], CUM[0:16, 2, :], ALU.subtract))
                nc.vector.tensor_tensor_scan(CUM[0:16, 0, :], ONES[0:16, 0:1].to_broadcast([16, T]), CUM[0:16, 1, :],
                                             0.0, ALU.mult, ALU.add).then_inc(S("cum"), 1)
                with ve.Fori(3, 11) as i:
                    split("in1", i, 1)
                    split("in1", i + 1, 0)
                split("in1", 11, 1)
                ve.wait_ge(S("gain_in"), 64)
                ve.wait_ge(S("fx_rs"), FOX_PAIRS)
                ve.wait_ge(S("fx_const"), 3)
                ve.wait_ge(S("w_used"), at["in1"][0] + 24)
                ve.wait_ge(S("ps_free"), at["in1"][1] + 24)
                o0 = od.at

                def operands(i):
                    if some(NQ * i):
                        ve.wait_ge(S("fx_s"), NQ * i)
                    for e in range(2):
                        h = slice(64 * e, 64 * e + 64)
                        stt(QZ[h, e:e + 1, :], QKV[h, ds(i, 1), :], GAINS[h, 0:1], FRS[h, ds(i, 1), :], ALU.mult, ALU.mult)
                    stt(KS[:, :].unsqueeze(1), QKV[:, ds(8 + i, 1), :], GAINS[:, 1:2], FRS[:, ds(8 + i, 1), :],
                        ALU.mult, ALU.mult).then_inc(S("fx_k"), 1)

                def maxima(i, j):
                    lo, n = TILES[j]
                    w = n - lo
                    m = min(n, 512)
                    b = 2 * SLOT[j]
                    ss = SS[0:w, SLOT[j], :, 0:n] if j else SS[0:w, SLOT[j], :, 512:512 + n]
                    c = 0 if j else 512 - w
                    bias = CB[0:w, :, ds(i, 1), :].rearrange("p e o t -> p (e o) t")
                    ve.wait_ge(S("fx_s"), NQ * i + j + 1)
                    if some(NQ * i + j - COLS_BACK[j] + 1):
                        ve.wait_ge(S("fx_e"), NQ * i + j - COLS_BACK[j] + 1)
                    if n > m:
                        stt(ss[:, :, m:n], BK[0:w, 6:8, 0:n - m], 0.125, bias[:, :, m:n], ALU.mult, ALU.add)
                    stt(ss[:, :, 0:m], BK[0:w, b:b + 2, c:c + m], 0.125, bias[:, :, 0:m], ALU.mult, ALU.add)\
                        .then_inc(S("fx_ss"), 1)
                    ve.wait_ge(S("fx_ss"), NQ * i + j + 1)
                    nc.vector.tensor_reduce(MX[0:w, j, :], ss, AXX, ALU.max, negate=True).then_inc(S("fx_mx"), 1)

                def weights(i, j):
                    n = TILES[j][1]
                    w = n - TILES[j][0]
                    c = 0 if j else 512
                    ve.wait_ge(S("fx_e"), NQ * i + j + 1)
                    step(nc.vector.reciprocal(RC[0:w, j, :], SM[0:w, j, :]))
                    for e in range(2):
                        pr = PR[0:w, SLOT[j], e, c:c + n]
                        x = ts(pr, pr, RC[0:w, j, e:e + 1], None, ALU.mult)
                    x.then_inc(S("fx_d"), 1)

                def low(i):
                    ve.wait_ge(S("ot_hi"), i + 1)
                    tt(XNL[:, ds(i, 1), :], OT[:, :].unsqueeze(1), f32(XNH[:, ds(i, 1), :]), ALU.subtract)\
                        .then_inc(S("x_lo"), 1)

                def pair(i):
                    last = isinstance(i, int) and i == FOX_PAIRS - 1
                    od.at = o0 + NQ * i
                    for j in range(NQ):
                        if j != NQ - 2:
                            weights(i, j)
                        if j == NQ - 3:
                            weights(i, j + 1)
                        if j == NQ - 2 and not last:
                            operands(i + 1)
                        if j < NQ - 2:
                            maxima(i, j + 2)
                        elif j == NQ - 1 and not last:
                            if not some(i):
                                ve.wait_ge(S("cb_in"), 16 * (FOX_PAIRS - 1))
                            maxima(i + 1, 0)
                            maxima(i + 1, 1)
                        if j == 0 and some(i):
                            low(i - 1)
                operands(0)
                ve.wait_ge(S("cb0_in"), 16)
                maxima(0, 0)
                maxima(0, 1)
                rounds(ve, FOX_PAIRS, pair, first=True)
                low(FOX_PAIRS - 1)
                ve.wait_ge(S("x_lo"), x_ready["out1"])
                od.at = o0 + NQ * FOX_PAIRS
                split("out1", 0, 0)
                residual("out1")
            if "ffn1" in stages:
                norm("up1", PC_FFN + KD)
                up(1)
                residual("down1")
            for i in range(0, 8, 2):
                ve.wait_ge(S("o_t"), i + 1)
                if some(i):
                    ve.wait_ge(S("o_cp"), i)
                ve.tensor_copy(OUTB[:, i // 2, 0:512], BK[:, 4, :]).then_inc(S("o_cp"), 1)


_INS = ['x', 'meta_tokens', 'mix_norm', 'ffn_norm', 'even_w_in', 'even_w_out', 'rwkv_mu', 'rwkv_w0', 'rwkv_w2',
        'rwkv_a0', 'rwkv_a2', 'rwkv_g2', 'rwkv_k_k', 'rwkv_k_a', 'rwkv_r_k', 'rwkv_ln_w', 'rwkv_ln_b', 's5_a_re',
        's5_a_im', 's5_log_dt', 's5_b_re', 's5_b_im', 's5_c_re', 's5_c_im', 's5_d', 's5_glu_w', 's5_glu_b',
        'odd_w_in', 'odd_w_out', 'fox_b_f', 'fox_q_gain', 'fox_k_gain', 'ffn_w_up', 'ffn_conv_w', 'ffn_conv_b',
        'ffn_w_down']
_OUTS = [((1, SEQ, D_MODEL), 'float32')]


def kernel(**inputs):
    import numpy as _np
    import concourse.bacc as _bacc
    from concourse import mybir as _mybir
    from concourse.bass_utils import run_bass_kernel_spmd as _run

    nc = _bacc.Bacc("TRN2", target_bir_lowering=False, num_devices=1)
    arrays, args = {}, {}
    for name in _INS:
        a = _np.ascontiguousarray(inputs[name])
        arrays[f"in_{name}_dram"] = a
        args[name] = nc.dram_tensor(f"in_{name}_dram", a.shape, _mybir.dt.from_np(a.dtype), kind="ExternalInput").ap()
    shape, dtype = _OUTS[0]
    o = nc.dram_tensor("out_0_dram", shape, _mybir.dt.from_np(_np.dtype(dtype)), kind="ExternalOutput").ap()
    decoder_trunk(nc, args, o)
    r = _run(nc, [arrays], core_ids=[0])
    return r.results[0]["out_0_dram"]
```
